# Optimizing a Trainium2 kernel written in Bass

```python
import math, functools
import jax, jax.numpy as jnp
from jax import lax
import numpy as np

D_MODEL = 1024
BATCH = 1
SEQ = 256
DEPTH = 1

N_HEADS_A = 8
HEAD_DIM = 64
N_KV_GROUPS = 2
Q_PER_GROUP = N_HEADS_A // N_KV_GROUPS
D_ATTN = N_HEADS_A * HEAD_DIM
D_KV = N_KV_GROUPS * HEAD_DIM
CMP_BLOCK = 32
CMP_STRIDE = 16
CMP_HIDDEN = 256
SLC_BLOCK = 64
N_SELECT = 16
N_LOCAL = 2
WINDOW = 512
Q_CHUNK = 128
ATTN_SCALE = HEAD_DIM ** -0.5
NEG = -1e30
FORCE_SCORE = 1e4
D_RNN = D_MODEL
N_RNN_BLOCKS = 16
RNN_BLOCK = D_RNN // N_RNN_BLOCKS
CONV_WIDTH = 4
LRU_C = 8.0
D_FF = 4 * D_MODEL
EPS = 1e-6

IN_SIZES = (D_ATTN, D_KV, D_KV, D_KV, D_KV, D_KV, D_KV, N_HEADS_A * 3, D_RNN, D_RNN, D_MODEL, D_MODEL)
IN_SPLITS = tuple(int(v) for v in np.cumsum(IN_SIZES)[:-1])
D_IN = int(sum(IN_SIZES))


def rms_norm(x, w):
    xf = x.astype(jnp.float32)
    var = jnp.mean(xf * xf, axis=-1, keepdims=True)
    return (xf * lax.rsqrt(var + EPS) * w.astype(jnp.float32)).astype(x.dtype)

def masked_softmax(s, mask):
    s = jnp.where(mask, s.astype(jnp.float32), NEG)
    m = jnp.max(s, axis=-1, keepdims=True)
    e = jnp.where(mask, jnp.exp(s - m), 0.0)
    return e / jnp.maximum(jnp.sum(e, axis=-1, keepdims=True), 1e-20)

def compress_blocks(k, pos, w1, w2):
    B, S = k.shape[0], k.shape[1]
    kb = k.reshape(B, S // CMP_STRIDE, CMP_STRIDE, N_KV_GROUPS, HEAD_DIM)
    blocks = jnp.concatenate([kb[:, :-1], kb[:, 1:]], axis=2) + pos[:, None, :]
    nc = blocks.shape[1]
    flat = blocks.transpose(0, 1, 3, 2, 4).reshape(B, nc, N_KV_GROUPS, CMP_BLOCK * HEAD_DIM)
    c = jax.nn.gelu(flat @ w1) @ w2
    return c.transpose(0, 2, 1, 3)

def nsa_attention(q, k_cmp, v_cmp, k_slc, v_slc, k_win, v_win, gates, pos_k, pos_v, ck_w1, ck_w2, cv_w1, cv_w2):
    B, S = q.shape[0], q.shape[1]
    G, R, dh = N_KV_GROUPS, Q_PER_GROUP, HEAD_DIM
    nb = S // SLC_BLOCK
    nc = S // CMP_STRIDE - 1
    nqb = S // Q_CHUNK
    k_sel = min(N_SELECT, nb)
    r_s = SLC_BLOCK // CMP_STRIDE
    r_c = CMP_BLOCK // CMP_STRIDE
    off = r_s + r_c - 2

    qh = q.reshape(B, S, G, R, dh).transpose(0, 2, 3, 1, 4)
    gh = gates.reshape(B, S, G, R, 3).transpose(0, 2, 3, 1, 4)
    kc = compress_blocks(k_cmp, pos_k, ck_w1, ck_w2)
    vc = compress_blocks(v_cmp, pos_v, cv_w1, cv_w2)
    ks_blk = k_slc.transpose(0, 2, 1, 3).reshape(B, G, nb, SLC_BLOCK, dh)
    vs_blk = v_slc.transpose(0, 2, 1, 3).reshape(B, G, nb, SLC_BLOCK, dh)
    pad_w = ((0, 0), (0, 0), (WINDOW, 0), (0, 0))
    kw_pad = jnp.pad(k_win.transpose(0, 2, 1, 3), pad_w)
    vw_pad = jnp.pad(v_win.transpose(0, 2, 1, 3), pad_w)
    cmp_end = jnp.arange(nc) * CMP_STRIDE + CMP_BLOCK - 1
    blk = jnp.arange(nb)
    gather = jax.vmap(jax.vmap(lambda blocks, ix: blocks[ix]))

    def chunk(qb):
        t0 = qb * Q_CHUNK
        qc = lax.dynamic_slice_in_dim(qh, t0, Q_CHUNK, axis=3)
        gc = lax.dynamic_slice_in_dim(gh, t0, Q_CHUNK, axis=3)
        tpos = t0 + jnp.arange(Q_CHUNK)
        s = jnp.einsum('bgrcd,bgnd->bgrcn', qc, kc) * ATTN_SCALE
        p_cmp = masked_softmax(s, cmp_end[None, :] <= tpos[:, None])
        o_cmp = jnp.einsum('bgrcn,bgnd->bgrcd', p_cmp, vc.astype(jnp.float32))
        ps = jnp.pad(p_cmp.sum(axis=2), ((0, 0), (0, 0), (0, 0), (off, 0)))
        imp = 0.0
        for m in range(r_s):
            for n in range(r_c):
                st = off - m - n
                imp = imp + ps[..., st:st + r_s * (nb - 1) + 1:r_s]
        cur = tpos // SLC_BLOCK
        valid_b = blk[None, :] <= cur[:, None]
        forced = (blk[None, :] == 0) | (blk[None, :] > cur[:, None] - N_LOCAL)
        score = jnp.where(valid_b, jnp.where(forced, FORCE_SCORE, imp), NEG)
        top_s, idx = lax.top_k(score, k_sel)
        sel_ok = top_s > NEG / 2
        ksel = gather(ks_blk, idx).reshape(B, G, Q_CHUNK, k_sel * SLC_BLOCK, dh)
        vsel = gather(vs_blk, idx).reshape(B, G, Q_CHUNK, k_sel * SLC_BLOCK, dh)
        kpos = idx[..., None] * SLC_BLOCK + jnp.arange(SLC_BLOCK)
        m_slc = (sel_ok[..., None] & (kpos <= tpos[:, None, None])).reshape(B, G, 1, Q_CHUNK, k_sel * SLC_BLOCK)
        s = jnp.einsum('bgrcd,bgcnd->bgrcn', qc, ksel) * ATTN_SCALE
        o_slc = jnp.einsum('bgrcn,bgcnd->bgrcd', masked_softmax(s, m_slc), vsel.astype(jnp.float32))
        kw = lax.dynamic_slice_in_dim(kw_pad, t0, Q_CHUNK + WINDOW, axis=2)
        vw = lax.dynamic_slice_in_dim(vw_pad, t0, Q_CHUNK + WINDOW, axis=2)
        kpos_w = t0 - WINDOW + jnp.arange(Q_CHUNK + WINDOW)
        diff = tpos[:, None] - kpos_w[None, :]
        m_win = (diff >= 0) & (diff < WINDOW) & (kpos_w[None, :] >= 0)
        s = jnp.einsum('bgrcd,bgnd->bgrcn', qc, kw) * ATTN_SCALE
        o_win = jnp.einsum('bgrcn,bgnd->bgrcd', masked_softmax(s, m_win), vw.astype(jnp.float32))
        out = gc[..., 0:1] * o_cmp + gc[..., 1:2] * o_slc + gc[..., 2:3] * o_win
        return out.astype(q.dtype)

    res = lax.map(chunk, jnp.arange(nqb))
    return res.transpose(1, 0, 4, 2, 3, 5).reshape(B, S, D_ATTN)

def rg_lru_branch(xr, gate, conv_w, conv_b, w_a, b_a, w_i, b_i, lam):
    B, S = xr.shape[0], xr.shape[1]
    xp = jnp.pad(xr, ((0, 0), (CONV_WIDTH - 1, 0), (0, 0)))
    xc = conv_b
    for i in range(CONV_WIDTH):
        xc = xc + xp[:, i:i + S] * conv_w[i]
    xb = xc.reshape(B, S, N_RNN_BLOCKS, RNN_BLOCK)
    r = jax.nn.sigmoid(jnp.einsum('bshi,hij->bshj', xb, w_a).reshape(B, S, D_RNN) + b_a)
    ig = jax.nn.sigmoid(jnp.einsum('bshi,hij->bshj', xb, w_i).reshape(B, S, D_RNN) + b_i)
    log_a = -LRU_C * r.astype(jnp.float32) * jax.nn.softplus(-lam.astype(jnp.float32))
    a = jnp.exp(log_a)
    bt = jnp.sqrt(-jnp.expm1(2.0 * log_a)) * (ig * xc).astype(jnp.float32)

    def combine(lhs, rhs):
        a1, b1 = lhs
        a2, b2 = rhs
        return a1 * a2, a2 * b1 + b2

    _, h = lax.associative_scan(combine, (a, bt), axis=1)
    return h.astype(xr.dtype) * jax.nn.gelu(gate)

def first_inputs(seed: int = 0) -> dict:
    key = jax.random.key(seed)
    ks = jax.random.split(key, 24)
    f32 = jnp.float32

    def nrm(k, shape, fan_in):
        return jax.random.normal(k, shape, f32) * (fan_in ** -0.5)

    a_c = jax.random.uniform(ks[17], (DEPTH, D_RNN), f32, 0.9, 0.999)
    s_l = a_c ** (1.0 / LRU_C)
    lam = jnp.log(s_l) - jnp.log1p(-s_l)
    return {
        "x": jax.random.normal(ks[0], (BATCH, SEQ, D_MODEL), f32),
        "norm1_w": 1.0 + 0.02 * jax.random.normal(ks[1], (DEPTH, D_MODEL), f32),
        "w_in": nrm(ks[2], (DEPTH, D_MODEL, D_IN), D_MODEL),
        "cmp_pos_k": 0.1 * jax.random.normal(ks[3], (DEPTH, CMP_BLOCK, HEAD_DIM), f32),
        "cmp_pos_v": 0.1 * jax.random.normal(ks[4], (DEPTH, CMP_BLOCK, HEAD_DIM), f32),
        "cmp_k_w1": nrm(ks[5], (DEPTH, CMP_BLOCK * HEAD_DIM, CMP_HIDDEN), CMP_BLOCK * HEAD_DIM),
        "cmp_k_w2": nrm(ks[6], (DEPTH, CMP_HIDDEN, HEAD_DIM), CMP_HIDDEN),
        "cmp_v_w1": nrm(ks[7], (DEPTH, CMP_BLOCK * HEAD_DIM, CMP_HIDDEN), CMP_BLOCK * HEAD_DIM),
        "cmp_v_w2": nrm(ks[8], (DEPTH, CMP_HIDDEN, HEAD_DIM), CMP_HIDDEN),
        "conv_w": nrm(ks[9], (DEPTH, CONV_WIDTH, D_RNN), CONV_WIDTH),
        "conv_b": 0.01 * jax.random.normal(ks[10], (DEPTH, D_RNN), f32),
        "lru_w_a": nrm(ks[11], (DEPTH, N_RNN_BLOCKS, RNN_BLOCK, RNN_BLOCK), RNN_BLOCK),
        "lru_b_a": 0.01 * jax.random.normal(ks[12], (DEPTH, D_RNN), f32),
        "lru_w_i": nrm(ks[13], (DEPTH, N_RNN_BLOCKS, RNN_BLOCK, RNN_BLOCK), RNN_BLOCK),
        "lru_b_i": 0.01 * jax.random.normal(ks[14], (DEPTH, D_RNN), f32),
        "lru_lambda": lam,
        "w_up_attn": nrm(ks[15], (DEPTH, D_ATTN, D_MODEL), D_ATTN),
        "w_up_rnn": nrm(ks[16], (DEPTH, D_RNN, D_MODEL), D_RNN),
        "w_out": nrm(ks[18], (DEPTH, D_MODEL, D_MODEL), D_MODEL),
        "norm2_w": 1.0 + 0.02 * jax.random.normal(ks[19], (DEPTH, D_MODEL), f32),
        "mlp_w1": nrm(ks[20], (DEPTH, D_MODEL, D_FF), D_MODEL),
        "mlp_w2": nrm(ks[21], (DEPTH, D_FF, D_MODEL), D_FF),
        "final_norm_w": 1.0 + 0.02 * jax.random.normal(ks[22], (D_MODEL,), f32),
    }

def first_block(x, norm1_w, w_in, cmp_pos_k, cmp_pos_v, cmp_k_w1, cmp_k_w2, cmp_v_w1, cmp_v_w2,
              conv_w, conv_b, lru_w_a, lru_b_a, lru_w_i, lru_b_i, lru_lambda,
              w_up_attn, w_up_rnn, w_out, norm2_w, mlp_w1, mlp_w2, final_norm_w):
    B, S = x.shape[0], x.shape[1]
    for l in range(DEPTH):
        xn = rms_norm(x, norm1_w[l])
        z = xn @ w_in[l]
        (q, k_c, v_c, k_s, v_s, k_w, v_w, g_nsa, xr, gr, g_a, g_b) = jnp.split(z, IN_SPLITS, axis=-1)
        kv_shape = (B, S, N_KV_GROUPS, HEAD_DIM)
        attn = nsa_attention(
            q.reshape(B, S, N_HEADS_A, HEAD_DIM),
            k_c.reshape(kv_shape), v_c.reshape(kv_shape),
            k_s.reshape(kv_shape), v_s.reshape(kv_shape),
            k_w.reshape(kv_shape), v_w.reshape(kv_shape),
            jax.nn.sigmoid(g_nsa).reshape(B, S, N_HEADS_A, 3),
            cmp_pos_k[l], cmp_pos_v[l], cmp_k_w1[l], cmp_k_w2[l], cmp_v_w1[l], cmp_v_w2[l])
        rnn = rg_lru_branch(xr, gr, conv_w[l], conv_b[l], lru_w_a[l], lru_b_a[l],
                            lru_w_i[l], lru_b_i[l], lru_lambda[l])
        merged = jax.nn.sigmoid(g_a) * (attn @ w_up_attn[l]) + jax.nn.sigmoid(g_b) * (rnn @ w_up_rnn[l])
        x = x + merged @ w_out[l]
        hn = rms_norm(x, norm2_w[l])
        x = x + jnp.square(jax.nn.relu(hn @ mlp_w1[l])) @ mlp_w2[l]
    return rms_norm(x, final_norm_w)


NA_HEADS = 8
NB_HEADS = 8
NB_KV_HEADS = 2
GRID_W = 64
NA_KH_MAX = 8
NA_KW = 16
WIN = 128
BLOCK = 128
ROPE_THETA = 10000.0
D_FF_2 = 2816

WIDTH_A = NA_HEADS * HEAD_DIM
WIDTH_BQ = NB_HEADS * HEAD_DIM
WIDTH_BKV = NB_KV_HEADS * HEAD_DIM
D_IN_2 = 3 * WIDTH_A + WIDTH_BQ + 2 * WIDTH_BKV + 2 * D_MODEL
SPLITS = (WIDTH_A, 2 * WIDTH_A, 3 * WIDTH_A,
          3 * WIDTH_A + WIDTH_BQ,
          3 * WIDTH_A + WIDTH_BQ + WIDTH_BKV,
          3 * WIDTH_A + WIDTH_BQ + 2 * WIDTH_BKV,
          3 * WIDTH_A + WIDTH_BQ + 2 * WIDTH_BKV + D_MODEL)


def rms_norm_2(x, g):
    xf = x.astype(jnp.float32)
    y = xf * lax.rsqrt(jnp.mean(xf * xf, axis=-1, keepdims=True) + EPS)
    return (y * g.astype(jnp.float32)).astype(x.dtype)

def swiglu(x, w_gate, w_up, w_down):
    return (jax.nn.silu(x @ w_gate) * (x @ w_up)) @ w_down

def rope(x, pos):
    half = x.shape[-1] // 2
    inv = ROPE_THETA ** (-jnp.arange(half, dtype=jnp.float32) / half)
    ang = pos.astype(jnp.float32)[:, None] * inv[None, :]
    cos = jnp.cos(ang)[None, :, None, :]
    sin = jnp.sin(ang)[None, :, None, :]
    x1 = x[..., :half].astype(jnp.float32)
    x2 = x[..., half:].astype(jnp.float32)
    out = jnp.concatenate([x1 * cos - x2 * sin, x2 * cos + x1 * sin], axis=-1)
    return out.astype(x.dtype)

def neighbourhood_attention_2d(q, k, v, rpb):
    B, T, H, dh = q.shape
    rows = T // GRID_W
    kh = min(NA_KH_MAX, rows)
    q = q.reshape(B, rows, GRID_W, H, dh)
    k = k.reshape(B, rows, GRID_W, H, dh)
    v = v.reshape(B, rows, GRID_W, H, dh)
    cols = jnp.arange(GRID_W)
    col_start = jnp.clip(cols - NA_KW // 2, 0, GRID_W - NA_KW)
    col_idx = col_start[:, None] + jnp.arange(NA_KW)[None, :]
    col_off = col_idx - cols[:, None] + (NA_KW - 1)
    rpb = rpb.astype(jnp.float32)
    scale = dh ** -0.5

    def row_block(args):
        r, q_r = args
        rs = jnp.clip(r - kh // 2, 0, rows - kh)
        k_slab = lax.dynamic_slice_in_dim(k, rs, kh, axis=1)
        v_slab = lax.dynamic_slice_in_dim(v, rs, kh, axis=1)
        k_g = k_slab[:, :, col_idx]
        v_g = v_slab[:, :, col_idx]
        row_off = rs + jnp.arange(kh) - r + (NA_KH_MAX - 1)
        bias = rpb[:, row_off[None, :, None], col_off[:, None, :]]
        s = jnp.einsum('bchd,bicjhd->bhcij', q_r, k_g).astype(jnp.float32) * scale
        s = s + bias[None]
        p = jax.nn.softmax(s.reshape(B, H, GRID_W, kh * NA_KW), axis=-1)
        p = p.reshape(B, H, GRID_W, kh, NA_KW).astype(v.dtype)
        return jnp.einsum('bhcij,bicjhd->bchd', p, v_g)

    out = lax.map(row_block, (jnp.arange(rows), jnp.moveaxis(q, 1, 0)))
    return jnp.moveaxis(out, 0, 1).reshape(B, T, H * dh)

def windowed_gqa_sink(q, k, v, sink):
    B, T, Hq, dh = q.shape
    Hkv = k.shape[2]
    G = Hq // Hkv
    nb = T // BLOCK
    qb = q.reshape(B, nb, BLOCK, Hkv, G, dh)

    def band(a):
        ap = jnp.pad(a, ((0, 0), (BLOCK, BLOCK), (0, 0), (0, 0)))
        ab = ap.reshape(B, nb + 2, BLOCK, Hkv, dh)
        return jnp.concatenate([ab[:, :-2], ab[:, 1:-1], ab[:, 2:]], axis=2)

    kb = band(k)
    vb = band(v)
    qpos = jnp.arange(nb)[:, None] * BLOCK + jnp.arange(BLOCK)[None, :]
    kpos = jnp.arange(nb)[:, None] * BLOCK - BLOCK + jnp.arange(3 * BLOCK)[None, :]
    kp = kpos[:, None, :]
    mask = (jnp.abs(qpos[:, :, None] - kp) <= WIN) & (kp >= 0) & (kp < T)
    s = jnp.einsum('bnqhgd,bnkhd->bnhgqk', qb, kb).astype(jnp.float32) * (dh ** -0.5)
    s = jnp.where(mask[None, :, None, None], s, -jnp.inf)
    sink_l = sink.astype(jnp.float32).reshape(Hkv, G)[None, None, :, :, None, None]
    m = jnp.maximum(jnp.max(s, axis=-1, keepdims=True), sink_l)
    e = jnp.exp(s - m)
    p = e / (jnp.sum(e, axis=-1, keepdims=True) + jnp.exp(sink_l - m))
    o = jnp.einsum('bnhgqk,bnkhd->bnqhgd', p.astype(v.dtype), vb)
    return o.reshape(B, T, Hq * dh)

def second_inputs(seed: int = 0) -> dict:
    key = jax.random.key(seed)
    ks = jax.random.split(key, 20)
    f32 = jnp.float32

    def w(k, shape, fan_in):
        return jax.random.normal(k, shape, f32) * (fan_in ** -0.5)

    def gain(k, shape):
        return 1.0 + 0.02 * jax.random.normal(k, shape, f32)

    return {
        "x": jax.random.normal(ks[0], (BATCH, SEQ, D_MODEL), f32),
        "ffn1_norm": gain(ks[1], (DEPTH, D_MODEL)),
        "ffn1_w_gate": w(ks[2], (DEPTH, D_MODEL, D_FF_2), D_MODEL),
        "ffn1_w_up": w(ks[3], (DEPTH, D_MODEL, D_FF_2), D_MODEL),
        "ffn1_w_down": w(ks[4], (DEPTH, D_FF_2, D_MODEL), D_FF_2),
        "mix_norm": gain(ks[5], (DEPTH, D_MODEL)),
        "w_in": w(ks[6], (DEPTH, D_MODEL, D_IN_2), D_MODEL),
        "na_rpb": 0.1 * jax.random.normal(ks[7], (DEPTH, NA_HEADS, 2 * NA_KH_MAX - 1, 2 * NA_KW - 1), f32),
        "sink_logit": 0.5 * jax.random.normal(ks[8], (DEPTH, NB_HEADS), f32),
        "w_branch_a": w(ks[9], (DEPTH, WIDTH_A, D_MODEL), WIDTH_A),
        "w_branch_b": w(ks[10], (DEPTH, WIDTH_BQ, D_MODEL), WIDTH_BQ),
        "w_out": w(ks[11], (DEPTH, D_MODEL, D_MODEL), D_MODEL),
        "ffn2_norm": gain(ks[12], (DEPTH, D_MODEL)),
        "ffn2_w_gate": w(ks[13], (DEPTH, D_MODEL, D_FF_2), D_MODEL),
        "ffn2_w_up": w(ks[14], (DEPTH, D_MODEL, D_FF_2), D_MODEL),
        "ffn2_w_down": w(ks[15], (DEPTH, D_FF_2, D_MODEL), D_FF_2),
        "final_norm": gain(ks[16], (D_MODEL,)),
    }

def second_block(x, ffn1_norm, ffn1_w_gate, ffn1_w_up, ffn1_w_down, mix_norm, w_in, na_rpb,
              sink_logit, w_branch_a, w_branch_b, w_out, ffn2_norm, ffn2_w_gate, ffn2_w_up,
              ffn2_w_down, final_norm):
    B, T, _ = x.shape
    pos = jnp.arange(T)
    h = x
    for l in range(DEPTH):
        h = h + 0.5 * swiglu(rms_norm_2(h, ffn1_norm[l]), ffn1_w_gate[l], ffn1_w_up[l], ffn1_w_down[l])
        u = rms_norm_2(h, mix_norm[l])
        z = u @ w_in[l]
        qa, ka, va, qb, kb, vb, ga, gb = jnp.split(z, SPLITS, axis=-1)
        qa = qa.reshape(B, T, NA_HEADS, HEAD_DIM)
        ka = ka.reshape(B, T, NA_HEADS, HEAD_DIM)
        va = va.reshape(B, T, NA_HEADS, HEAD_DIM)
        ya = neighbourhood_attention_2d(qa, ka, va, na_rpb[l])
        qb = rope(qb.reshape(B, T, NB_HEADS, HEAD_DIM), pos)
        kb = rope(kb.reshape(B, T, NB_KV_HEADS, HEAD_DIM), pos)
        vb = vb.reshape(B, T, NB_KV_HEADS, HEAD_DIM)
        yb = windowed_gqa_sink(qb, kb, vb, sink_logit[l])
        merged = jax.nn.sigmoid(ga) * (ya @ w_branch_a[l]) + jax.nn.sigmoid(gb) * (yb @ w_branch_b[l])
        h = h + merged @ w_out[l]
        h = h + 0.5 * swiglu(rms_norm_2(h, ffn2_norm[l]), ffn2_w_gate[l], ffn2_w_up[l], ffn2_w_down[l])
    return rms_norm_2(h, final_norm)


def setup_inputs(seed=0):
    out = dict(first_inputs(seed))
    for name, value in second_inputs(seed + 1).items():
        if name != "x":
            out[name + "_2"] = value
    return out


def reference(
    x, norm1_w, w_in, cmp_pos_k, cmp_pos_v, cmp_k_w1, cmp_k_w2, cmp_v_w1, cmp_v_w2, conv_w,
    conv_b, lru_w_a, lru_b_a, lru_w_i, lru_b_i, lru_lambda, w_up_attn, w_up_rnn, w_out, norm2_w,
    mlp_w1, mlp_w2, final_norm_w, ffn1_norm_2, ffn1_w_gate_2, ffn1_w_up_2, ffn1_w_down_2,
    mix_norm_2, w_in_2, na_rpb_2, sink_logit_2, w_branch_a_2, w_branch_b_2, w_out_2,
    ffn2_norm_2, ffn2_w_gate_2, ffn2_w_up_2, ffn2_w_down_2, final_norm_2,
):
    x = first_block(
        x, norm1_w, w_in, cmp_pos_k, cmp_pos_v, cmp_k_w1, cmp_k_w2, cmp_v_w1, cmp_v_w2, conv_w,
        conv_b, lru_w_a, lru_b_a, lru_w_i, lru_b_i, lru_lambda, w_up_attn, w_up_rnn, w_out,
        norm2_w, mlp_w1, mlp_w2, final_norm_w,
    )
    return second_block(
        x, ffn1_norm_2, ffn1_w_gate_2, ffn1_w_up_2, ffn1_w_down_2, mix_norm_2, w_in_2, na_rpb_2,
        sink_logit_2, w_branch_a_2, w_branch_b_2, w_out_2, ffn2_norm_2, ffn2_w_gate_2,
        ffn2_w_up_2, ffn2_w_down_2, final_norm_2,
    )


_drawn_inputs = setup_inputs


def setup_inputs(seed=0):
    import zlib

    import numpy as np

    out = dict(_drawn_inputs(seed))
    spreads = {}
    factors = {'norm1_w': 6.506,
     'cmp_pos_k': 8.0,
     'cmp_pos_v': 3.28,
     'conv_b': 3.733,
     'lru_b_a': 8.0,
     'lru_b_i': 8.0,
     'norm2_w': 2.992,
     'ffn1_norm_2': 6.591,
     'mix_norm_2': 8.0,
     'na_rpb_2': 6.469,
     'sink_logit_2': 8.0,
     'ffn2_norm_2': 7.382,
     'final_norm_2': 2.737}
    for name, (base, spread) in spreads.items():
        noise = np.random.default_rng([zlib.crc32(name.encode()), seed]).standard_normal(out[name].shape)
        drawn = base * np.exp(spread * noise) if base else spread * noise
        out[name] = __import__('jax').numpy.asarray(drawn.astype(out[name].dtype))
    for name, factor in factors.items():
        out[name] = (out[name] * factor).astype(out[name].dtype)
    return out
```

```python
from contextlib import ExitStack

import numpy as np
import concourse.bass as bass
from concourse import mybir

F32 = mybir.dt.float32
F32R = mybir.dt.float32r
ALU = mybir.AluOpType
ACT = mybir.ActivationFunctionType
AX_X = mybir.AxisListType.X

P = 128
T = 256
TT = T // P
D = 1024
KT = D // P
DH = 64
NH = 8
GR = 2
NC = 15
CH = 256
NPOS = 16
CW = 4
PW = 2048
R = 3
QSCALE = -(DH ** -0.5)
EPS = 1e-6
BIG = 1e30
GS = 32

Q, KCVC, KSVS, KWVW, CK, CV, XR, GRP, GA, GB = 0, 2, 3, 4, 5, 7, 9, 13, 17, 21
UPA, UPR, WO, ML = 25, 27, 31, 35
ML_STEPS = 16
F1 = ML + 2 * ML_STEPS
FF_STEPS = 11
QKV2 = F1 + 3 * FF_STEPS
QB, KBVB, GA2, GB2 = QKV2 + 6, QKV2 + 8, QKV2 + 9, QKV2 + 13
BRA, BRB, WO2, F2 = QKV2 + 17, QKV2 + 19, QKV2 + 21, QKV2 + 25
END = F2 + 3 * FF_STEPS

V_N1, V_N2, V_F1, V_MX, V_F2, V_CW, V_CB, V_BA, V_BI, V_LAM, V_PK, V_PV = (
    0, 8, 16, 24, 32, 40, 72, 80, 88, 96, 104, 120)
V_ALL = 136

C_ID, C_TRIU, C_ZERO, C_CAUS, C_PERM, C_CMP, C_VALID, C_NA, C_COS, C_SIN, C_MHALF = (
    0, 128, 256, 384, 512, 640, 672, 674, 738, 994, 1250)
C_ALL = 1252


def constants():
    c = np.zeros((P, C_ALL), np.float32)
    i = np.arange(P)
    c[:, C_ID:C_ID + P] = np.eye(P)
    c[:, C_TRIU:C_TRIU + P] = np.where(i[None, :] >= i[:, None], 0, BIG)
    c[:, C_CAUS:C_CAUS + P] = np.where(i[None, :] <= i[:, None], 0, BIG)
    swap = np.zeros((P, P), np.float32)
    swap[(i // 64) * 64 + (i % 64 + 32) % 64, i] = 1
    c[:, C_PERM:C_PERM + P] = swap
    n = np.arange(NC)
    for tt in range(TT):
        c[:, C_CMP + tt * NC:C_CMP + tt * NC + NC] = np.where(
            n[None, :] * 16 + 31 <= (tt * P + i)[:, None], 0, BIG)
        c[:, C_VALID + tt] = tt * P + i >= 31
    col = i % 64
    start = np.clip(col - 8, 0, 48)
    cc = np.arange(64)
    inside = (cc[None, :] >= start[:, None]) & (cc[None, :] < start[:, None] + 16)
    c[:, C_NA:C_NA + 64] = np.where(inside, 0, BIG)
    half = DH // 2
    inv = np.float32(10000.0) ** (-np.arange(half, dtype=np.float32) / np.float32(half))
    ang = np.arange(T, dtype=np.float32)[None, :] * inv[i % half][:, None].astype(np.float32)
    c[:, C_COS:C_COS + T] = np.cos(ang)
    c[:, C_SIN:C_SIN + T] = np.sin(ang) * np.where(i % 64 < half, -1, 1)[:, None]
    c[:, C_MHALF:C_MHALF + 2] = -0.5
    return c


def build(nc, a, out):
    ctx = ExitStack()
    with ctx:
        def sb(name, shape, dt=F32):
            return ctx.enter_context(nc.sbuf_tensor(name, shape, dt))

        def sem(name):
            return ctx.enter_context(nc.semaphore(name))

        raw = sb("raw", [P, R, PW])
        wh = sb("wh", [P, R, PW], F32R)
        wl = sb("wl", [P, R, PW], F32R)
        acth = sb("acth", [P, KT, T], F32R)
        actl = sb("actl", [P, KT, T], F32R)
        midh = sb("midh", [P, 6, T], F32R)
        midl = sb("midl", [P, 6, T], F32R)
        mrgh = sb("mrgh", [P, KT, T], F32R)
        mrgl = sb("mrgl", [P, KT, T], F32R)
        cst = sb("cst", [P, C_ALL])
        xt = sb("xt", [P, TT, D])
        xs = sb("xs", [P, TT, D])
        vec = sb("vec", [P, V_ALL])
        vrow = sb("vrow", [V_PK, P])
        prow = sb("prow", [V_ALL - V_PK, P])
        gwr = sb("gwr", [P, KT, 24])
        gwh = sb("gwh", [P, KT, 24], F32R)
        gwl = sb("gwl", [P, KT, 24], F32R)
        cw2 = sb("cw2", [P, 2, 2, DH])
        hid = sb("hid", [P, 2, 2, 2 * NC])
        ssq = sb("ssq", [P, TT])
        var = sb("var", [P, TT])
        rstd = sb("rstd", [P, TT])
        small = sb("small", [P, 64])
        lru = sb("lru", [P, 12, KT])
        nmax = sb("nmax", [P, 3, 4])
        sums = sb("sums", [P, 3, 4])
        coef = sb("coef", [P, 3, 4])
        esink = sb("esink", [P, 3, 2])
        nsink = sb("nsink", [P, NH])
        arena = sb("arena", [P, 15600])

        def carve(at, *shape):
            n = int(np.prod(shape))
            v = arena[:, at:at + n]
            names = "abcd"[:len(shape)]
            if len(shape) == 1:
                return v
            return v.rearrange("p (%s) -> p %s" % (" ".join(names), " ".join(names)),
                               **{k: s for k, s in zip(names, shape)})

        xrp = carve(0, KT, T + CW - 1)
        xc = carve(2080, KT, T)
        igx = carve(4128, KT, T)
        gru = carve(6176, KT, T)
        qT = carve(8224, 4, T)
        ksd = carve(9248, GR, T)
        kwd = carve(9760, GR, T)
        vsw = carve(10272, TT, 2, P)
        prob = carve(10784, 768)
        probT = carve(11552, 768)
        sga = carve(10272, KT, T)
        bd = carve(12320, KT, 2, P)
        sgb = carve(12320, KT, T)
        atok = carve(14368, TT, NH * DH)
        flat = carve(4128, 2, NPOS * 2 * NC)
        abuf = xs[:, :, :].rearrange("p t (k f) -> p (t k) f", f=T)
        gates = sb("gates", [P, TT, NH, 3])
        xsf = xs[:, :, :].rearrange("p t d -> p (t d)")
        vblk = xsf[:, 512:1024].rearrange("p (g r d) -> p g r d", g=GR, r=4)
        pc = xsf[:, 1024:1536].rearrange("p (t h n) -> p t h n", t=TT, h=NH)
        pcT = xsf[:, 1536:2048].rearrange("p (a q) -> p a q", q=P)
        kcd = sb("kcd", [P, GR, NC])
        thr = carve(9760, T)
        nth = carve(9760 + T, T)
        nab = carve(0, TT, NH, T)
        sga2 = carve(4096, KT, T)
        sgb2 = carve(6144, KT, T)
        nabr = carve(4096, TT, NH, T)
        qaT = carve(8192, 4, T)
        kaT = carve(9216, 4, T)
        va = carve(10240, TT, NH * DH)
        qbT = carve(11264, 4, T)
        kbT = carve(12288, T)
        kbd = carve(12544, GR, T)
        vb = carve(13056, TT, P)
        prob2 = carve(13312, TT, T)
        probT2 = carve(13824, 512)
        atok2 = carve(14336, TT, NH * DH)
        btok = xs[:, 0, :].rearrange("p (t n) -> p t n", t=TT)
        rope1 = xs[:, 1, 0:512]
        rope2 = xs[:, 1, 512:1024]
        fnb = carve(0, D)
        ffa = xs[:, 0, 0:512]
        ffs = xs[:, 0, 512:1024]

        ps = [ctx.enter_context(nc.psum_tensor(f"ps{i}", [P, 512], F32)) for i in range(2)]
        acc4 = ctx.enter_context(nc.psum_tensor("acc4", [P, 4, 512], F32))
        ps += [acc4[:, i, :] for i in range(4)]
        ps += [ctx.enter_context(nc.psum_tensor(f"ps{i}", [P, 512], F32)) for i in (6, 7)]

        ident = cst[:, C_ID:C_ID + P]

        def vcol(v, k=0):
            return vec[:, v + k:v + k + 1]

        x_loaded = sem("x_loaded")
        cst_loaded = sem("cst_loaded")
        vec_loaded = sem("vec_loaded")
        small_loaded = sem("small_loaded")
        bd_zeroed = sem("bd_zeroed")
        bd_loaded = sem("bd_loaded")
        fnb_loaded = sem("fnb_loaded")
        nab_loaded = sem("nab_loaded")
        nab_ready = sem("nab_ready")
        sink_ready = sem("sink_ready")
        padded = sem("padded")
        panel_loaded = [sem(f"panel_loaded{s}") for s in range(R)]
        hi_ready = sem("hi_ready")
        lo_ready = sem("lo_ready")
        panel_done = sem("panel_done")
        dve_chain = sem("dve_chain")
        act_chain = sem("act_chain")
        pool_chain = sem("pool_chain")
        vec_turned = sem("vec_turned")
        vec_ready = sem("vec_ready")
        exp_lam = sem("exp_lam")
        abs_lam = sem("abs_lam")
        lru_consts = sem("lru_consts")
        x_summed = sem("x_summed")
        ssq_ready = sem("ssq_ready")
        ssq_ready_d = sem("ssq_ready_d")
        rstd_ready = sem("rstd_ready")
        xs_ready = sem("xs_ready")
        xs_turned = sem("xs_turned")
        acth_ready = sem("acth_ready")
        actl_ready = sem("actl_ready")
        q_evac = sem("q_evac")
        flat_ready = sem("flat_ready")
        flath_ready = sem("flath_ready")
        flatl_ready = sem("flatl_ready")
        ks_evac = sem("ks_evac")
        kw_evac = sem("kw_evac")
        gw_hi = sem("gw_hi")
        gw_lo = sem("gw_lo")
        gates_done = sem("gates_done")
        gates_tanh = sem("gates_tanh")
        gates_ready = sem("gates_ready")
        hid_ready = sem("hid_ready")
        ckv_done = sem("ckv_done")
        ckv_ready = sem("ckv_ready")
        sc_done = sem("sc_done")
        sc_read = sem("sc_read")
        sc_shifted = sem("sc_shifted")
        sc_exped = sem("sc_exped")
        pc_ready = sem("pc_ready")
        pc_turned = sem("pc_turned")
        pcT_ready = sem("pcT_ready")
        oc_done = sem("oc_done")
        oc_read = sem("oc_read")
        scored = sem("scored")
        masked = sem("masked")
        exped = sem("exped")
        turned = sem("turned")
        probT_ready = sem("probT_ready")
        mixed = sem("mixed")
        normed = sem("normed")
        atok_turned = sem("atok_turned")
        midh_ready = sem("midh_ready")
        midl_ready = sem("midl_ready")
        xr_evac = sem("xr_evac")
        gr_evac = sem("gr_evac")
        gr_gelu = sem("gr_gelu")
        ga_evac = sem("ga_evac")
        gb_evac = sem("gb_evac")
        conv_done = sem("conv_done")
        lru_done = sem("lru_done")
        lru_act = sem("lru_act")
        lru_q = sem("lru_q")
        root_ready = sem("root_ready")
        rnn_ready = sem("rnn_ready")
        rnnh_ready = sem("rnnh_ready")
        rnnl_ready = sem("rnnl_ready")
        upa_evac = sem("upa_evac")
        upr_evac = sem("upr_evac")
        mrg_sum = sem("mrg_sum")
        mrgh_ready = sem("mrgh_ready")
        mrgl_ready = sem("mrgl_ready")
        seeded = sem("seeded")
        ff_act = sem("ff_act")
        ff_prod = sem("ff_prod")
        ff_hi = sem("ff_hi")
        ff_lo = sem("ff_lo")
        qa_evac = sem("qa_evac")
        ka_evac = sem("ka_evac")
        va_evac = sem("va_evac")
        qb_evac = sem("qb_evac")
        kv_evac = sem("kv_evac")
        rope_done = sem("rope_done")
        rope_read = sem("rope_read")
        qb_ready = sem("qb_ready")
        kb_ready = sem("kb_ready")
        out_ready = sem("out_ready")
        stored = sem("stored")

        def pv(n, kt, dst):
            return dst[:, n % R, :].rearrange("p (k c) -> p k c", k=kt)

        w_in, w_in2 = a["w_in"][0], a["w_in_2"][0]

        def up_src(w, col, width=256):
            return w[:, bass.ds(col, width)].rearrange("(k p) c -> p k c", p=P)

        def down_src(w, row):
            return w[bass.ds(row, 256), :].rearrange("(k p) c -> p k c", p=P)

        col1 = {Q: 0, Q + 1: 256, KCVC: 512, KSVS: 768, KWVW: 1024}
        for u in range(4):
            col1[XR + u] = 1304 + 256 * u
            col1[GRP + u] = 2328 + 256 * u
            col1[GA + u] = 3352 + 256 * u
            col1[GB + u] = 4376 + 256 * u
        col2 = {}
        for u in range(2):
            for s in range(3):
                col2[QKV2 + 3 * u + s] = 512 * s + 256 * u
            col2[QB + u] = 1536 + 256 * u
        col2[KBVB] = 2048
        for u in range(4):
            col2[GA2 + u] = 2304 + 256 * u
            col2[GB2 + u] = 3328 + 256 * u

        block = ctx.enter_context(nc.Block())

        @block.sync
        def _(sp):
            sp.dma_start(xt[:, :, :], a["x"][0].rearrange("(t p) d -> p t d", p=P)).then_inc(x_loaded, 16)

            def load(n, kt, src):
                if n >= R:
                    sp.wait_ge(lo_ready, n - R + 1)
                sp.dma_start(pv(n, kt, raw), src).then_inc(panel_loaded[n % R], 16)

            def load_in_loop(i, n, kt, src):
                sp.wait_ge(lo_ready, i * 6 + (n - R + 1))
                sp.dma_start(pv(n, kt, raw), src).then_inc(panel_loaded[n % R], 16)

            def load_ffn(n0, wg, wu, wd):
                load(n0, KT, up_src(wg, 0))
                load(n0 + 1, KT, up_src(wu, 0))
                with sp.Fori(0, (FF_STEPS - 1) // 2) as i:
                    for m in range(2):
                        n = n0 + 2 + 3 * m
                        load_in_loop(i, n, KT, up_src(wg, i * 512 + 256 * (m + 1)))
                        load_in_loop(i, n + 1, KT, up_src(wu, i * 512 + 256 * (m + 1)))
                        load_in_loop(i, n + 2, 2, down_src(wd, i * 512 + 256 * m))
                load(n0 + 3 * FF_STEPS - 1, 2, down_src(wd, 256 * (FF_STEPS - 1)))

            for n in range(0, CK):
                load(n, KT, up_src(w_in, col1[n]))
            for n, name in ((CK, "cmp_k_w1"), (CV, "cmp_v_w1")):
                for u in range(2):
                    load(n + u, KT, a[name][0, 1024 * u:1024 * (u + 1), :].rearrange("(k p) c -> p k c", p=P))
            for n in range(XR, UPA):
                load(n, KT, up_src(w_in, col1[n]))
            for u in range(2):
                load(UPA + u, 4, up_src(a["w_up_attn"][0], 512 * u, 512))
            for u in range(4):
                load(UPR + u, KT, up_src(a["w_up_rnn"][0], 256 * u))
            for u in range(4):
                load(WO + u, 2, down_src(a["w_out"][0], 256 * u))
            w1, w2 = a["mlp_w1"][0], a["mlp_w2"][0]
            load(ML, KT, up_src(w1, 0))
            with sp.Fori(0, (ML_STEPS - 1) // 3) as i:
                for m in range(3):
                    n = ML + 1 + 2 * m
                    load_in_loop(i, n, KT, up_src(w1, i * 768 + 256 * (m + 1)))
                    load_in_loop(i, n + 1, 2, down_src(w2, i * 768 + 256 * m))
            load(F1 - 1, 2, down_src(w2, 256 * (ML_STEPS - 1)))
            load_ffn(F1, a["ffn1_w_gate_2"][0], a["ffn1_w_up_2"][0], a["ffn1_w_down_2"][0])
            for n in range(QKV2, BRA):
                load(n, KT, up_src(w_in2, col2[n]))
            for n, name in ((BRA, "w_branch_a_2"), (BRB, "w_branch_b_2")):
                for u in range(2):
                    load(n + u, 4, up_src(a[name][0], 512 * u, 512))
            for u in range(4):
                load(WO2 + u, 2, down_src(a["w_out_2"][0], 256 * u))
            load_ffn(F2, a["ffn2_w_gate_2"][0], a["ffn2_w_up_2"][0], a["ffn2_w_down_2"][0])
            for tt in range(TT):
                sp.wait_ge(out_ready, tt + 1)
                sp.dma_start(out[0, tt * P:(tt + 1) * P, :], xs[:, tt, :]).then_inc(stored, 16)
            sp.wait_ge(stored, 16 * TT)

        @block.gpsimd
        def _(pool):
            pool.dma_start(cst[:, :], a["consts"]).then_inc(cst_loaded, 16)
            rows = [("norm1_w", V_N1), ("norm2_w", V_N2), ("ffn1_norm_2", V_F1), ("mix_norm_2", V_MX),
                    ("ffn2_norm_2", V_F2), ("conv_b", V_CB), ("lru_b_a", V_BA), ("lru_b_i", V_BI),
                    ("lru_lambda", V_LAM)]
            for name, v in rows:
                pool.dma_start(vrow[v:v + KT, :], a[name][0].rearrange("(k p) -> k p", p=P)).then_inc(vec_loaded, 16)
            pool.dma_start(vrow[V_CW:V_CW + CW * KT, :],
                           a["conv_w"][0].rearrange("i (k p) -> (i k) p", p=P)).then_inc(vec_loaded, 16)
            for s, name in enumerate(("cmp_pos_k", "cmp_pos_v")):
                pool.dma_start(prow[NPOS * s:NPOS * (s + 1), :],
                               a[name][0].rearrange("(j l) d -> j (l d)", l=2)).then_inc(vec_loaded, 16)
            pool.dma_start(gwr[:, :, :], w_in[:, 1280:1304].rearrange("(k p) c -> p k c", p=P)).then_inc(small_loaded, 16)
            for s, name in enumerate(("cmp_k_w2", "cmp_v_w2")):
                pool.dma_start(cw2[:, s, :, :], a[name][0].rearrange("(c p) d -> p c d", p=P)).then_inc(small_loaded, 16)
            pool.dma_start(nsink[:, :], a["sink_logit_2"][0:1, :].broadcast_to([P, NH])).then_inc(small_loaded, 16)
            nc.gpsimd.memset(bd[:, :, :, :], 0.0).then_inc(bd_zeroed, 1)
            nc.gpsimd.memset(xrp[:, :, 0:CW - 1], 0.0)
            nc.gpsimd.memset(atok[:, :, :], 0.0).then_inc(padded, 1)
            pool.wait_ge(bd_zeroed, 1)
            for s, name in enumerate(("lru_w_a", "lru_w_i")):
                pairs = a[name][0].rearrange("(t e) i j -> e i t j", e=2)
                for e in range(2):
                    pool.dma_start(bd[DH * e:DH * (e + 1), :, s, DH * e:DH * (e + 1)], pairs[e]).then_inc(bd_loaded, 16)
            pool.wait_ge(small_loaded, 64)
            nc.gpsimd.tensor_scalar(small[:, 0:NH], nsink[:, :], -1.0, None, ALU.mult).then_inc(sink_ready, 1)

            def norm_root(r):
                pool.wait_ge(ssq_ready, r + 1)
                pool.wait_ge(ssq_ready_d, r + 1)
                if r == 0:
                    pool.wait_ge(cst_loaded, 16)
                nc.gpsimd.tensor_scalar(var[:, :], ssq[:, :], 1.0 / D, EPS, ALU.mult, ALU.add).then_inc(pool_chain, 1)
                pool.wait_ge(pool_chain, r + 1)
                nc.gpsimd.tensor_tensor(rstd[:, :], var[:, :], cst[:, C_MHALF:C_MHALF + TT], ALU.pow).then_inc(rstd_ready, 1)

            norm_root(0)
            pool.wait_ge(panel_done, ML)
            norm_root(1)
            pool.dma_start(fnb[:, :], a["final_norm_w"].rearrange("(o d) -> o d", o=1).broadcast_to([P, D])).then_inc(fnb_loaded, 16)
            norm_root(2)
            norm_root(3)
            pool.wait_ge(acth_ready, KT * 3)
            rpb = a["rpb_rev"]
            for tt in range(TT):
                for rr in range(2):
                    for i in range(4):
                        src = bass.AP(rpb.tensor, (7 + i - 2 * tt - rr) * 31 + 15 - 63, [[1, 64], [15 * 31, NH], [1, 64]])
                        pool.dma_start(nabr[64 * rr:64 * rr + 64, tt, :, 64 * i:64 * i + 64], src).then_inc(nab_loaded, 16)
            pool.wait_ge(nab_loaded, 16 * 16)
            for tt in range(TT):
                bias = nabr[:, tt, :, :].rearrange("p h (i c) -> p (h i) c", c=64)[:, :, ::-1]
                mask = cst[:, C_NA:C_NA + 64].unsqueeze(1).broadcast_to([P, 4 * NH, 64])
                nc.gpsimd.tensor_tensor(nab[:, tt, :, :].rearrange("p h (i c) -> p (h i) c", c=64),
                                        mask, bias, ALU.subtract).then_inc(nab_ready, 1)
            norm_root(4)
            pool.wait_ge(panel_done, F2)
            norm_root(5)
            pool.dma_start(fnb[:, :], a["final_norm_2"].rearrange("(o d) -> o d", o=1).broadcast_to([P, D])).then_inc(fnb_loaded, 16)
            norm_root(6)


        flath = mrgh[:, :, :].rearrange("p k t -> p (k t)")[:, 0:2 * NPOS * 2 * NC]
        flatl = mrgl[:, :, :].rearrange("p k t -> p (k t)")[:, 0:2 * NPOS * 2 * NC]
        ML_F, F1_F, F2_F = 0, ML_STEPS, ML_STEPS + FF_STEPS

        def head2(k):
            h = k % NH
            b = DH * (h % 2)
            if k < NH:
                return (qaT[b:b + DH, h // 2, :], kaT[b:b + DH, h // 2, :],
                        [va[:, kt, DH * h:DH * (h + 1)] for kt in range(TT)])
            g = h // 4
            return (qbT[b:b + DH, h // 2, :], kbd[b:b + DH, g, :],
                    [vb[:, kt, DH * g:DH * (g + 1)] for kt in range(TT)])

        turn2 = {(QKV2 + 2 + k, 1): k for k in range(7)}
        turn2[QKV2 + 9, 1] = 7
        turn2[QKV2 + 10, 1] = 8
        for k in range(9, 17):
            turn2[QKV2 + 11 + (k - 9) // 2, (k - 9) % 2] = k
        turn2[QKV2 + 15, 1] = 17

        @block.tensor
        def _(pe):
            def split(n):
                pe.wait_ge(lo_ready, n + 1)

            def three(out_, lh, ll, rh, rl, start, stop, **kw):
                nc.tensor.matmul(out_, lh, rh, start=start, stop=False, **kw)
                nc.tensor.matmul(out_, lh, rl, start=False, stop=False, **kw)
                return nc.tensor.matmul(out_, ll, rh, start=False, stop=stop, **kw)

            def feature_tile(n, kt, c, out_, ah, al):
                h, l = pv(n, kt, wh), pv(n, kt, wl)
                for k in range(kt):
                    last = three(out_, h[:, k, c * P:(c + 1) * P], l[:, k, c * P:(c + 1) * P],
                                 ah[:, k, :], al[:, k, :], k == 0, k == kt - 1)
                return last

            def token_tile(n, c0, c1, tt, out_):
                h, l = pv(n, KT, wh), pv(n, KT, wl)
                s = slice(tt * P, (tt + 1) * P)
                for k in range(KT):
                    last = three(out_, acth[:, k, s], actl[:, k, s], h[:, k, c0:c1], l[:, k, c0:c1],
                                 k == 0, k == KT - 1)
                return last

            def down(n, kt, lhs_h, lhs_l, first, final):
                h, l = pv(n, 2, wh), pv(n, 2, wl)
                for k in range(2):
                    for tt in range(TT):
                        s = slice(tt * P, (tt + 1) * P)
                        for hf in range(2):
                            cs = slice(512 * hf, 512 * hf + 512)
                            last = three(acc4[:, 2 * tt + hf, :], lhs_h[:, kt + k, s], lhs_l[:, kt + k, s],
                                         h[:, k, cs], l[:, k, cs], first and k == 0, final and k == 1)
                return last

            def turn_tokens(j):
                for tt in range(TT):
                    pe.wait_ge(xs_ready, TT * j + tt + 1)
                    for k in range(KT):
                        b = ps[(6, 7, 0, 1)[k // 2]]
                        m = nc.tensor.transpose(b[:, (k % 2) * T + tt * P:(k % 2) * T + (tt + 1) * P],
                                                xs[:, tt, k * P:(k + 1) * P], ident)
                        if tt == TT - 1 and k % 2:
                            m.then_inc(xs_turned, 1)

            def seed():
                for b in range(4):
                    nc.tensor.matmul(acc4[:, b, :], cst[:, C_ZERO:C_ZERO + P], cst[:, 0:512], start=True, stop=False)

            pe.wait_ge(cst_loaded, 16)
            pe.wait_ge(vec_loaded, 16 * 12)
            nc.tensor.transpose(ps[2][:, 0:V_PK], vrow[:, :], cst[0:V_PK, C_ID:C_ID + V_PK])
            nc.tensor.transpose(ps[2][:, V_PK:V_ALL], prow[:, :],
                                cst[0:V_ALL - V_PK, C_ID:C_ID + V_ALL - V_PK]).then_inc(vec_turned, 1)
            turn_tokens(0)
            pe.wait_ge(actl_ready, KT)

            def head_score(k):
                if k:
                    pe.wait_ge(masked, k)
                b, t, g = DH * (k % 2), k // 2, k // 4
                q = qT[b:b + DH, t, :]
                for e, kd in enumerate((ksd, kwd)):
                    nc.tensor.matmul(ps[2][:, e * P:(e + 1) * P], q[:, 0:P], kd[b:b + DH, g, 0:P], start=True, stop=True)
                for e, kd in enumerate((ksd, kwd)):
                    m = nc.tensor.matmul(ps[3][:, e * T:(e + 1) * T], q[:, P:T], kd[b:b + DH, g, :], start=True, stop=True)
                m.then_inc(scored, 1)

            def head_turn(k):
                pe.wait_ge(exped, k + 1)
                if k:
                    pe.wait_ge(probT_ready, k)
                for i in range(6):
                    m = nc.tensor.transpose(ps[4 + i // 4][:, (i % 4) * P:(i % 4 + 1) * P], prob[:, i * P:(i + 1) * P], ident)
                m.then_inc(turned, 1)

            def head_mix(k):
                pe.wait_ge(probT_ready, k + 1)
                if k:
                    pe.wait_ge(normed, k)
                vs = slice(DH * (k // 4), DH * (k // 4) + DH)
                for e in range(2):
                    nc.tensor.matmul(ps[6][:, e * DH:(e + 1) * DH], probT[:, e * P:(e + 1) * P], vsw[:, 0, e, vs],
                                     start=True, stop=True)
                    for kt in range(TT):
                        c = (2 + 2 * e + kt) * P
                        m = nc.tensor.matmul(ps[6][:, (2 + e) * DH:(3 + e) * DH], probT[:, c:c + P], vsw[:, kt, e, vs],
                                             start=kt == 0, stop=kt == 1)
                m.then_inc(mixed, 1)

            def heads(k):
                if 0 <= k - 2 < NH:
                    head_mix(k - 2)
                if 0 <= k - 1 < NH:
                    head_turn(k - 1)
                if k < NH:
                    head_score(k)

            def free_bank(n):
                if n in (KCVC, KSVS):
                    pe.wait_ge(q_evac, n - 1)
                elif n == KWVW:
                    pe.wait_ge(flat_ready, 2)
                elif n == XR:
                    pe.wait_ge(ks_evac, 1)
                elif n == XR + 1:
                    pe.wait_ge(kw_evac, 1)
                elif XR + 2 <= n < UPA:
                    group = (n - 2 - XR) // 4
                    pe.wait_ge((xr_evac, gr_evac, ga_evac, gb_evac)[group], (n - 2 - XR) % 4 + 1)

            for n in range(UPA):
                split(n)
                free_bank(n)
                if n in (KSVS, KWVW):
                    feature_tile(n, KT, 0, ps[n % 2][:, 0:T], acth, actl)
                    for tt in range(TT):
                        m = token_tile(n, P, 2 * P, tt, ps[n % 2][:, T + tt * P:T + (tt + 1) * P])
                elif CK <= n < XR:
                    s, u = (n - CK) // 2, (n - CK) % 2
                    if n == CK:
                        pe.wait_ge(flatl_ready, 1)
                    h, l = pv(n, KT, wh), pv(n, KT, wl)
                    for c in range(2):
                        for k in range(KT):
                            at = (s * NPOS + u * KT + k) * 2 * NC
                            m = three(ps[7][:, (2 * s + c) * 2 * NC:(2 * s + c + 1) * 2 * NC],
                                      h[:, k, c * P:(c + 1) * P], l[:, k, c * P:(c + 1) * P],
                                      flath[:, at:at + 2 * NC], flatl[:, at:at + 2 * NC],
                                      n == CK and c == 0 and k == 0, u == 1 and k == KT - 1, skip_group_check=True)
                else:
                    for c in range(2):
                        m = feature_tile(n, KT, c, ps[n % 2][:, c * T:(c + 1) * T], acth, actl)
                m.then_inc(panel_done, 1)

                if n == KWVW:
                    pe.wait_ge(gw_lo, 1)
                    for tt in range(TT):
                        s = slice(tt * P, (tt + 1) * P)
                        for k in range(KT):
                            m = three(ps[5][:, tt * 24:(tt + 1) * 24], acth[:, k, s], actl[:, k, s],
                                      gwh[:, k, :], gwl[:, k, :], k == 0, k == KT - 1)
                    m.then_inc(gates_done, 1)
                if n == CK:
                    pe.wait_ge(q_evac, 2)
                    pe.wait_ge(ks_evac, 1)
                    pe.wait_ge(kw_evac, 1)
                    pe.wait_ge(gates_tanh, 1)
                if CK <= n < CK + NH + 2:
                    heads(n - CK)
                if n == XR:
                    pe.wait_ge(hid_ready, 1)
                    for c in range(2):
                        nc.tensor.matmul(ps[7][0:DH, 128:128 + 2 * NC], cw2[:, 0, c, :], hid[:, 0, c, :],
                                         start=c == 0, stop=c == 1)
                    for g in range(GR):
                        for c in range(2):
                            m = nc.tensor.matmul(ps[7][0:NC, 192 + DH * g:192 + DH * (g + 1)],
                                                 hid[:, 1, c, NC * g:NC * (g + 1)], cw2[:, 1, c, :],
                                                 start=c == 0, stop=c == 1)
                    m.then_inc(ckv_done, 1)
                if n in (XR + 1, XR + 2):
                    e = n - XR - 1
                    pe.wait_ge(ckv_ready, 1)
                    if e:
                        pe.wait_ge(sc_read, 1)
                    b = DH * e
                    for tt in range(TT):
                        for t in range(4):
                            m = nc.tensor.matmul(ps[7][:, (tt * 4 + t) * NC:(tt * 4 + t + 1) * NC],
                                                 qT[b:b + DH, t, tt * P:(tt + 1) * P], kcd[b:b + DH, t // 2, :],
                                                 start=True, stop=True)
                    m.then_inc(sc_done, 1)
                if n == XR + 4:
                    pe.wait_ge(pc_ready, 1)
                    for i in range(2 * TT):
                        tt, g = i // 2, i % 2
                        m = nc.tensor.transpose(ps[7][:, i * P:(i + 1) * P],
                                                pc[:, tt, 4 * g:4 * g + 4, :].rearrange("p h n -> p (h n)"), ident)
                    m.then_inc(pc_turned, 1)
                if n in (XR + 5, XR + 6):
                    tt = n - XR - 5
                    pe.wait_ge(pcT_ready, 1)
                    if tt:
                        pe.wait_ge(oc_read, 1)
                    for g in range(GR):
                        m = nc.tensor.matmul(ps[7][:, g * T:(g + 1) * T], pcT[:, tt * 2 + g, :],
                                             vblk[:, g, :, :].rearrange("p r d -> p (r d)"), start=True, stop=True)
                    m.then_inc(oc_done, 1)
                if XR + 4 <= n < XR + 4 + KT:
                    t = n - XR - 4
                    pe.wait_ge(conv_done, t + 1)
                    if t == 0:
                        pe.wait_ge(bd_loaded, 64)
                        pe.wait_ge(masked, NH)
                    if t >= 2:
                        pe.wait_ge(lru_act, t - 1)
                    for s in range(2):
                        m = nc.tensor.matmul(ps[2 + t % 2][:, s * T:(s + 1) * T], bd[:, t, s, :], xc[:, t, :],
                                             start=True, stop=True)
                    m.then_inc(lru_done, 1)
                if n == GA + 1:
                    pe.wait_ge(normed, NH)
                    pe.wait_ge(oc_read, 2)
                    for k in range(4):
                        for tt in range(TT):
                            m = nc.tensor.transpose(ps[4 + k // 2][:, (k % 2) * T + tt * P:(k % 2) * T + (tt + 1) * P],
                                                    atok[:, tt, k * P:(k + 1) * P], ident)
                    m.then_inc(atok_turned, 1)

            pe.wait_ge(midl_ready, 1)
            for u in range(2):
                split(UPA + u)
                for c in range(4):
                    if c % 2 == 0:
                        if u == 0:
                            pe.wait_ge(gb_evac, 4)
                        else:
                            pe.wait_ge(upa_evac, c // 2 + 1)
                    m = feature_tile(UPA + u, 4, c, ps[c // 2][:, (c % 2) * T:(c % 2 + 1) * T], midh, midl)
                m.then_inc(panel_done, 1)
            pe.wait_ge(rnnl_ready, 2)
            for u in range(4):
                n = UPR + u
                split(n)
                pe.wait_ge(upa_evac, 4)
                if u >= 2:
                    pe.wait_ge(upr_evac, u - 1)
                for c in range(2):
                    m = feature_tile(n, KT, c, ps[n % 2][:, c * T:(c + 1) * T], acth, actl)
                m.then_inc(panel_done, 1)

            def project(n0, e):
                for u in range(4):
                    split(n0 + u)
                    pe.wait_ge(mrgl_ready, 4 * e + u + 1)
                    down(n0 + u, 2 * u, mrgh, mrgl, u == 0, u == 3).then_inc(panel_done, 1)

            project(WO, 0)
            turn_tokens(1)
            seed()
            pe.wait_ge(actl_ready, 2 * KT)

            def ffn_up(n, b):
                h = [feature_tile(n, KT, c, ps[b][:, c * T:(c + 1) * T], acth, actl) for c in range(2)]
                h[1].then_inc(panel_done, 1)

            split(ML)
            ffn_up(ML, 0)
            with pe.Fori(0, (ML_STEPS - 1) // 3) as i:
                for m in range(3):
                    n = ML + 1 + 2 * m
                    pe.wait_ge(lo_ready, i * 6 + (n + 1))
                    pe.wait_ge(ff_act, i * 3 + (ML_F + m + 1))
                    ffn_up(n, 0)
                    pe.wait_ge(lo_ready, i * 6 + (n + 2))
                    pe.wait_ge(ff_lo, i * 3 + (ML_F + m + 1))
                    down(n + 1, 2 * m, midh, midl, False, False).then_inc(panel_done, 1)
            split(F1 - 1)
            pe.wait_ge(ff_lo, ML_F + ML_STEPS)
            down(F1 - 1, 2 * ((ML_STEPS - 1) % 3), midh, midl, False, True).then_inc(panel_done, 1)

            def swiglu(n0, f0, j):
                turn_tokens(j)
                seed()
                pe.wait_ge(actl_ready, (j + 1) * KT)
                for b in range(2):
                    split(n0 + b)
                    ffn_up(n0 + b, b)
                with pe.Fori(0, (FF_STEPS - 1) // 2) as i:
                    for m in range(2):
                        n = n0 + 2 + 3 * m
                        for b, read in enumerate((ff_act, ff_prod)):
                            pe.wait_ge(lo_ready, i * 6 + (n + b + 1))
                            pe.wait_ge(read, i * 2 + (f0 + m + 1))
                            ffn_up(n + b, b)
                        pe.wait_ge(lo_ready, i * 6 + (n + 3))
                        pe.wait_ge(ff_lo, i * 2 + (f0 + m + 1))
                        down(n + 2, 2 * m, midh, midl, False, False).then_inc(panel_done, 1)
                n = n0 + 3 * FF_STEPS - 1
                split(n)
                pe.wait_ge(ff_lo, f0 + FF_STEPS)
                down(n, 2 * ((FF_STEPS - 1) % 2), midh, midl, False, True).then_inc(panel_done, 1)

            swiglu(F1, F1_F, 2)
            turn_tokens(3)
            pe.wait_ge(actl_ready, 4 * KT)

            def score2(k):
                if k == 0:
                    pe.wait_ge(qa_evac, 1)
                    pe.wait_ge(ka_evac, 1)
                else:
                    pe.wait_ge(masked, NH + k)
                if k == 4:
                    pe.wait_ge(qa_evac, 2)
                    pe.wait_ge(ka_evac, 2)
                if k == NH:
                    pe.wait_ge(qb_ready, 2)
                    pe.wait_ge(kb_ready, 1)
                q, kk, _ = head2(k)
                for tt in range(TT):
                    m = nc.tensor.matmul(ps[2][:, tt * T:(tt + 1) * T], q[:, tt * P:(tt + 1) * P], kk, start=True, stop=True)
                m.then_inc(scored, 1)

            def turn2_(k):
                pe.wait_ge(exped, NH + k + 1)
                pe.wait_ge(probT_ready, NH + k)
                for i in range(4):
                    tt, kt = i // 2, i % 2
                    m = nc.tensor.transpose(ps[3][:, i * P:(i + 1) * P], prob2[:, tt, kt * P:(kt + 1) * P], ident)
                m.then_inc(turned, 1)

            def mix2(k):
                pe.wait_ge(probT_ready, NH + k + 1)
                pe.wait_ge(normed, NH + k)
                if k == 0:
                    pe.wait_ge(va_evac, 1)
                if k == 4:
                    pe.wait_ge(va_evac, 2)
                if k == NH:
                    pe.wait_ge(kv_evac, 1)
                vt = head2(k)[2]
                for tt in range(TT):
                    for kt in range(TT):
                        c = (2 * tt + kt) * P
                        m = nc.tensor.matmul(ps[4][:, tt * DH:(tt + 1) * DH], probT2[:, c:c + P], vt[kt],
                                             start=kt == 0, stop=kt == 1)
                m.then_inc(mixed, 1)

            def heads2(n, part):
                k = turn2.get((n, part))
                if k is None:
                    return
                if 0 <= k - 2:
                    mix2(k - 2)
                if 0 <= k - 1 < 2 * NH:
                    turn2_(k - 1)
                if k < 2 * NH:
                    score2(k)

            def free_bank2(n):
                last = {QKV2 + 2: (qa_evac, 1), QKV2 + 3: (ka_evac, 1), QKV2 + 4: (va_evac, 1),
                        QKV2 + 5: (qa_evac, 2), QB: (ka_evac, 2), QB + 1: (va_evac, 2),
                        KBVB: (qb_evac, 1), GA2: (qb_evac, 2), GA2 + 1: (kv_evac, 1)}
                if n in last:
                    pe.wait_ge(*last[n])
                elif n >= GA2 + 2:
                    u = n - GA2 - 2
                    pe.wait_ge((ga_evac, gb_evac)[u // 4], 4 + u % 4 + 1)

            def turn_out(tok):
                for k in range(4):
                    for tt in range(TT):
                        m = nc.tensor.transpose(ps[5 + k // 2][:, (k % 2) * T + tt * P:(k % 2) * T + (tt + 1) * P],
                                                tok[:, tt, k * P:(k + 1) * P], ident)
                m.then_inc(atok_turned, 1)

            for n in range(QKV2, BRA):
                split(n)
                free_bank2(n)
                o = ps[n % 2]
                for c in range(2):
                    if n in (QKV2 + 2, QKV2 + 5):
                        m = token_tile(n, 0, 256, c, o[:, c * T:(c + 1) * T])
                    elif n == KBVB and c == 1:
                        for tt in range(TT):
                            m = token_tile(n, P, 2 * P, tt, o[:, T + tt * P:T + (tt + 1) * P])
                    else:
                        m = feature_tile(n, KT, c, o[:, c * T:(c + 1) * T], acth, actl)
                    if c == 1:
                        m.then_inc(panel_done, 1)
                    heads2(n, c)
                if n in (QB + 1, KBVB):
                    u = n - QB - 1
                    pe.wait_ge(qb_evac, u + 1)
                    if u:
                        pe.wait_ge(rope_read, 1)
                    nc.tensor.matmul(ps[7][:, :], cst[:, C_PERM:C_PERM + P],
                                     qbT[:, 2 * u:2 * u + 2, :].rearrange("p a t -> p (a t)"),
                                     start=True, stop=True).then_inc(rope_done, 1)
                if n == GA2:
                    pe.wait_ge(kv_evac, 1)
                    pe.wait_ge(rope_read, 2)
                    nc.tensor.matmul(ps[7][:, 0:T], cst[:, C_PERM:C_PERM + P], kbT[:, :],
                                     start=True, stop=True).then_inc(rope_done, 1)
                if n == GA2 + 3:
                    pe.wait_ge(normed, 2 * NH)
                    turn_out(atok2)
                if n == GB2 + 3:
                    pe.wait_ge(normed, 3 * NH)
                    pe.wait_ge(midl_ready, 2)
                    turn_out(btok)

            for br, (n0, ah, al) in enumerate(((BRA, midh, midl), (BRB, acth, actl))):
                pe.wait_ge(midl_ready, 2 + br)
                for u in range(2):
                    split(n0 + u)
                    for c in range(4):
                        if c % 2 == 0:
                            if br == 0 and u == 0:
                                pe.wait_ge(gb_evac, 8)
                            elif br == 0:
                                pe.wait_ge(upa_evac, 4 + c // 2 + 1)
                            elif u == 0:
                                pe.wait_ge(upa_evac, 4 + 2 + c // 2 + 1)
                            else:
                                pe.wait_ge(upr_evac, 4 + c // 2 + 1)
                        m = feature_tile(n0 + u, 4, c, ps[c // 2][:, (c % 2) * T:(c % 2 + 1) * T], ah, al)
                    m.then_inc(panel_done, 1)
            project(WO2, 1)
            swiglu(F2, F2_F, 4)

        @block.scalar
        def _(act):
            ac = [0]

            def link(ins):
                ac[0] += 1
                ins.then_inc(act_chain, 1)
                act.wait_ge(act_chain, ac[0])

            def hi(n):
                act.wait_ge(panel_loaded[n % R], 16 * (n // R + 1))
                if n >= R:
                    act.wait_ge(panel_done, n - R + 1)
                nc.scalar.activation(wh[:, n % R, :], raw[:, n % R, :], ACT.Copy).then_inc(hi_ready, 1)

            def hi_in_loop(i, n):
                if n < END:
                    act.wait_ge(panel_loaded[n % R], i * 32 + 16 * (n // R + 1))
                    act.wait_ge(panel_done, i * 6 + (n - R + 1))
                    nc.scalar.activation(wh[:, n % R, :], raw[:, n % R, :], ACT.Copy).then_inc(hi_ready, 1)

            def square_sum(r):
                if r:
                    act.wait_ge(x_summed, TT * (r - 1) + 1)
                else:
                    act.wait_ge(x_loaded, 16)
                nc.scalar.activation(xs[:, 0, :], xt[:, 0, :], ACT.Square, accum_out=ssq[:, 0:1]).then_inc(ssq_ready, 1)

            def norm_hi(j, v):
                if j == 0:
                    act.wait_ge(vec_ready, 1)
                for k in range(KT):
                    act.wait_ge(xs_turned, 4 * j + k // 2 + 1)
                    nc.scalar.activation(acth[:, k, :], ps[(6, 7, 0, 1)[k // 2]][:, (k % 2) * T:(k % 2 + 1) * T],
                                         ACT.Copy, scale=vcol(v, k)).then_inc(acth_ready, 1)

            square_sum(0)
            hi(0)
            hi(1)
            act.wait_ge(abs_lam, 1)
            nc.scalar.activation(lru[:, 1, :], lru[:, 0, :], ACT.Exp, scale=-1.0).then_inc(exp_lam, 1)
            norm_hi(0, V_N1)
            act.wait_ge(small_loaded, 64)
            nc.scalar.activation(gwh[:, :, :], gwr[:, :, :], ACT.Copy).then_inc(gw_hi, 1)

            def done(n):
                act.wait_ge(panel_done, n + 1)

            def keys_values(b, kd, e, ev):
                for g in range(GR):
                    for half in range(2):
                        nc.scalar.activation(kd[DH * half:DH * (half + 1), g, :], b[DH * g:DH * (g + 1), 0:T], ACT.Copy)
                nc.scalar.activation(vsw[:, :, e, :], b[:, T:2 * T].rearrange("p (t c) -> p t c", c=P),
                                     ACT.Copy).then_inc(ev, 1)

            def head_exp(k):
                act.wait_ge(masked, k + 1)
                o = k % 3
                for i, (c0, c1) in enumerate(((0, P), (P, 2 * P), (2 * P, 4 * P), (4 * P, 6 * P))):
                    m = nc.scalar.activation(prob[:, c0:c1], prob[:, c0:c1], ACT.Exp, scale=-1.0,
                                             bias=nmax[:, o, i:i + 1], accum_out=sums[:, o, i:i + 1])
                m.then_inc(exped, 1)

            def head_copy(k):
                act.wait_ge(turned, k + 1)
                if k:
                    act.wait_ge(mixed, k)
                nc.scalar.activation(probT[:, :], acc4[:, 2:4, :].rearrange("p b c -> p (b c)")[:, 0:768],
                                     ACT.Copy).then_inc(probT_ready, 1)

            for n in range(ML):
                hi(n + 2)
                if n in (Q + 1, Q + 2):
                    u = n - Q - 1
                    done(n - 1)
                    nc.scalar.activation(qT[:, 2 * u:2 * u + 2, :].rearrange("p a t -> p (a t)"), ps[u][:, :], ACT.Copy,
                                         scale=QSCALE).then_inc(q_evac, 1)
                if n == KCVC + 1:
                    act.wait_ge(flat_ready, 2)
                    nc.scalar.activation(flath, flat[:, :, :].rearrange("p s c -> p (s c)"), ACT.Copy).then_inc(flath_ready, 1)
                if n == KSVS + 1:
                    done(KSVS)
                    keys_values(ps[KSVS % 2], ksd, 0, ks_evac)
                if n == KWVW + 1:
                    done(KWVW)
                    keys_values(ps[KWVW % 2], kwd, 1, kw_evac)
                    act.wait_ge(gates_done, 1)
                    nc.scalar.activation(gates[:, :, :, :].rearrange("p t h b -> p (t h b)"), ps[5][:, 0:48],
                                         ACT.Tanh, scale=0.5).then_inc(gates_tanh, 1)
                k = n - CK - 1
                if 0 <= k - 1 < NH:
                    head_copy(k - 1)
                if 0 <= k < NH:
                    head_exp(k)
                if n == XR:
                    done(XR - 1)
                    nc.scalar.activation(hid[:, :, :, :].rearrange("p s c n -> p (s c n)"), ps[7][:, 0:8 * NC],
                                         ACT.Gelu_apprx_tanh).then_inc(hid_ready, 1)
                if XR < n <= XR + 4:
                    u = n - XR - 1
                    done(n - 1)
                    nc.scalar.activation(xrp[:, 2 * u:2 * u + 2, CW - 1:CW - 1 + T],
                                         ps[(n - 1) % 2][:, :].rearrange("p (a t) -> p a t", a=2), ACT.Copy).then_inc(xr_evac, 1)
                if n == XR + 4:
                    act.wait_ge(sc_shifted, 1)
                    nc.scalar.activation(pc[:, :, :, 0:NC], pc[:, :, :, 0:NC], ACT.Exp, scale=-1.0).then_inc(sc_exped, 1)
                if n == XR + 5:
                    act.wait_ge(pc_turned, 1)
                    nc.scalar.activation(pcT[:, :, :].rearrange("p a q -> p (a q)"), ps[7][:, :], ACT.Copy).then_inc(pcT_ready, 1)
                if GRP < n <= GRP + 4:
                    u = n - GRP - 1
                    done(n - 1)
                    nc.scalar.activation(gru[:, 2 * u:2 * u + 2, :].rearrange("p a t -> p (a t)"), ps[(n - 1) % 2][:, :],
                                         ACT.Copy).then_inc(gr_evac, 1)
                for g0, sg, ev in ((GA, sga, ga_evac), (GB, sgb, gb_evac)):
                    if g0 < n <= g0 + 4:
                        u = n - g0 - 1
                        done(n - 1)
                        if g0 == GB and u == 0:
                            act.wait_ge(lru_done, KT)
                        nc.scalar.activation(sg[:, 2 * u:2 * u + 2, :].rearrange("p a t -> p (a t)"), ps[(n - 1) % 2][:, :],
                                             ACT.Tanh, scale=0.5).then_inc(ev, 1)
                if n == GRP + 5:
                    act.wait_ge(gr_evac, 4)
                    nc.scalar.activation(gru[:, :, :], gru[:, :, :], ACT.Gelu_apprx_tanh).then_inc(gr_gelu, 1)
                t = n - XR - 5
                if 0 <= t < KT:
                    if t == 0:
                        act.wait_ge(lru_consts, 1)
                    act.wait_ge(lru_done, t + 1)
                    b = ps[2 + t % 2]
                    nc.scalar.activation(igx[:, t, :], b[:, T:2 * T], ACT.Tanh, scale=0.5, bias=lru[:, 9, t:t + 1])
                    if t:
                        act.wait_ge(lru_act, t)
                    link(nc.scalar.activation(thr[:, :], b[:, 0:T], ACT.Tanh, scale=0.5, bias=lru[:, 8, t:t + 1]))
                    nc.scalar.activation(abuf[:, t, :], thr[:, :], ACT.Exp, scale=lru[:, 6, t:t + 1], bias=lru[:, 6, t:t + 1])
                    if t:
                        act.wait_ge(lru_q, t)
                    nc.scalar.activation(nth[:, :], thr[:, :], ACT.Tanh, scale=lru[:, 7, t:t + 1],
                                         bias=lru[:, 7, t:t + 1]).then_inc(lru_act, 1)
                if n in (GA + 1, GB + 1):
                    hf = (n - GA - 1) // 4
                    act.wait_ge(lru_q, 4 * hf + 4)
                    q2 = xrp[:, 4 * hf:4 * hf + 4, 0:T]
                    nc.scalar.activation(q2, q2, ACT.Sqrt).then_inc(root_ready, 1)
                if n == GA + 2:
                    act.wait_ge(atok_turned, 1)
                    nc.scalar.activation(midh[:, 0:4, :].rearrange("p k t -> p (k t)"),
                                         acc4[:, 2:4, :].rearrange("p b c -> p (b c)"), ACT.Copy).then_inc(midh_ready, 1)
                if n == UPA:
                    done(UPA - 1)
                    for hf in range(2):
                        act.wait_ge(rnn_ready, hf + 1)
                        nc.scalar.activation(acth[:, 4 * hf:4 * hf + 4, :], gru[:, 4 * hf:4 * hf + 4, :],
                                             ACT.Copy).then_inc(rnnh_ready, 1)
                if UPR < n <= UPR + 4:
                    u = n - UPR - 1
                    act.wait_ge(mrg_sum, u + 1)
                    nc.scalar.activation(mrgh[:, 2 * u:2 * u + 2, :], sga[:, 2 * u:2 * u + 2, :], ACT.Copy,
                                         scale=0.5).then_inc(mrgh_ready, 1)

            square_sum(1)
            norm_hi(1, V_N2)

            def hidden_hi(s):
                return nc.scalar.activation(midh[:, 2 * s:2 * s + 2, :].rearrange("p a t -> p (a t)"), ffs, ACT.Copy)

            hi(ML + 2)
            done(ML)
            nc.scalar.activation(ffa, ps[0][:, :], ACT.Relu).then_inc(ff_act, 1)
            hi(ML + 3)
            act.wait_ge(ff_prod, ML_F + 1)
            hidden_hi(0).then_inc(ff_hi, 1)
            with act.Fori(0, (ML_STEPS - 1) // 3) as i:
                for m in range(3):
                    n = ML + 1 + 2 * m
                    act.wait_ge(panel_done, i * 6 + (n + 1))
                    nc.scalar.activation(ffa, ps[0][:, :], ACT.Relu).then_inc(ff_act, 1)
                    hi_in_loop(i, n + 3)
                    act.wait_ge(ff_prod, i * 3 + (ML_F + m + 2))
                    hidden_hi((m + 1) % 3).then_inc(ff_hi, 1)
                    hi_in_loop(i, n + 4)

            def swiglu(n0, f0):
                hi(n0 + 2)
                done(n0)
                nc.scalar.activation(ffa, ps[0][:, :], ACT.Silu).then_inc(ff_act, 1)
                hi(n0 + 3)
                hi(n0 + 4)
                act.wait_ge(ff_prod, f0 + 1)
                hidden_hi(0).then_inc(ff_hi, 1)

                def two_steps(i, last):
                    for m in range(2):
                        n = n0 + 2 + 3 * m
                        act.wait_ge(panel_done, i * 6 + (n + 1))
                        nc.scalar.activation(ffa, ps[0][:, :], ACT.Silu).then_inc(ff_act, 1)
                        hi_in_loop(i, n + 3)
                        act.wait_ge(ff_prod, i * 2 + (f0 + m + 2))
                        hidden_hi((m + 1) % 2).then_inc(ff_hi, 1)
                        if not (last and m and n0 == F2):
                            hi_in_loop(i, n + 4)
                            hi_in_loop(i, n + 5)

                with act.Fori(0, (FF_STEPS - 1) // 2 - 1) as i:
                    two_steps(i, False)
                two_steps((FF_STEPS - 1) // 2 - 1, True)

            square_sum(2)
            square_sum(3)
            norm_hi(2, V_F1)
            swiglu(F1, F1_F)
            square_sum(4)
            norm_hi(3, V_MX)

            def copy2(k):
                act.wait_ge(turned, NH + k + 1)
                act.wait_ge(mixed, NH + k)
                nc.scalar.activation(probT2[:, :], ps[3][:, :], ACT.Copy).then_inc(probT_ready, 1)

            def exp2(k):
                act.wait_ge(masked, NH + k + 1)
                o = k % 3
                if k >= NH:
                    h = k - NH
                    for tt in range(TT):
                        nc.scalar.activation(esink[:, o, tt:tt + 1], small[:, h:h + 1], ACT.Exp, scale=-1.0,
                                             bias=nmax[:, o, tt:tt + 1])
                for tt in range(TT):
                    m = nc.scalar.activation(prob2[:, tt, :], prob2[:, tt, :], ACT.Exp, scale=-1.0,
                                             bias=nmax[:, o, tt:tt + 1], accum_out=sums[:, o, tt:tt + 1])
                m.then_inc(exped, 1)

            def heads2(n, part):
                k = turn2.get((n, part))
                if k is None:
                    return
                if 0 <= k - 1 < 2 * NH:
                    copy2(k - 1)
                if k < 2 * NH:
                    exp2(k)

            for n in range(QKV2, F2):
                hi(n + 2)
                b = ps[(n - 1) % 2][:, :]
                if n - 1 in (QKV2, QKV2 + 3, QB, QB + 1):
                    done(n - 1)
                    dst, ev, u = ((qaT, qa_evac, (n - 1 - QKV2) // 3) if n - 1 < QB else (qbT, qb_evac, n - 1 - QB))
                    nc.scalar.activation(dst[:, 2 * u:2 * u + 2, :].rearrange("p a t -> p (a t)"), b, ACT.Copy,
                                         scale=QSCALE).then_inc(ev, 1)
                if n - 1 in (QKV2 + 2, QKV2 + 5):
                    u = (n - 1 - QKV2) // 3
                    done(n - 1)
                    nc.scalar.activation(va[:, :, 256 * u:256 * (u + 1)], b.rearrange("p (t c) -> p t c", t=TT),
                                         ACT.Copy).then_inc(va_evac, 1)
                if n - 1 == KBVB:
                    done(n - 1)
                    nc.scalar.activation(kbT[:, :], b[:, 0:T], ACT.Copy)
                    nc.scalar.activation(vb[:, :, :], b[:, T:2 * T].rearrange("p (t c) -> p t c", c=P),
                                         ACT.Copy).then_inc(kv_evac, 1)
                heads2(n - 1, 1)
                heads2(n, 0)
                for g0, sg, ev in ((GA2, sga2, ga_evac), (GB2, sgb2, gb_evac)):
                    if g0 < n <= g0 + 4:
                        u = n - g0 - 1
                        done(n - 1)
                        if g0 == GA2 and u == 0:
                            act.wait_ge(nab_ready, 2)
                        nc.scalar.activation(sg[:, 2 * u:2 * u + 2, :].rearrange("p a t -> p (a t)"), b,
                                             ACT.Tanh, scale=0.5).then_inc(ev, 1)
                if n in (GA2 + 4, GB2 + 4):
                    br = n == GB2 + 4
                    act.wait_ge(atok_turned, 2 + br)
                    if br:
                        done(BRA - 1)
                    dst = acth if br else midh
                    nc.scalar.activation(dst[:, 0:2, :].rearrange("p k t -> p (k t)"), ps[5][:, :], ACT.Copy)
                    nc.scalar.activation(dst[:, 2:4, :].rearrange("p k t -> p (k t)"), ps[6][:, :],
                                         ACT.Copy).then_inc(midh_ready, 1)
                if n in (BRB + 1, BRB + 2):
                    for u in range(2 * (n - BRB - 1), 2 * (n - BRB)):
                        act.wait_ge(mrg_sum, 4 + u + 1)
                        nc.scalar.activation(mrgh[:, 2 * u:2 * u + 2, :], sga2[:, 2 * u:2 * u + 2, :], ACT.Copy,
                                             scale=0.5).then_inc(mrgh_ready, 1)

            square_sum(5)
            norm_hi(4, V_F2)
            swiglu(F2, F2_F)
            square_sum(6)

        @block.vector
        def _(dve):
            dc = [0]

            def link(ins):
                dc[0] += 1
                ins.then_inc(dve_chain, 1)
                dve.wait_ge(dve_chain, dc[0])

            def lo(n):
                dve.wait_ge(hi_ready, n + 1)
                nc.vector.tensor_tensor(wl[:, n % R, :], raw[:, n % R, :], wh[:, n % R, :].bitcast(F32),
                                        ALU.subtract).then_inc(lo_ready, 1)

            def lo_in_loop(i, n):
                dve.wait_ge(hi_ready, i * 6 + (n + 1))
                nc.vector.tensor_tensor(wl[:, n % R, :], raw[:, n % R, :], wh[:, n % R, :].bitcast(F32),
                                        ALU.subtract).then_inc(lo_ready, 1)

            def square_sum(r):
                if r:
                    dve.wait_ge(x_summed, TT * r)
                else:
                    dve.wait_ge(x_loaded, 16)
                nc.vector.tensor_tensor_reduce(out=xs[:, 1, :], in0=xt[:, 1, :], in1=xt[:, 1, :], scale=1.0, scalar=0.0,
                                               op0=ALU.mult, op1=ALU.add, accum_out=ssq[:, 1:2]).then_inc(ssq_ready_d, 1)
                dve.wait_ge(rstd_ready, r + 1)

            def normalise():
                for tt in range(TT):
                    nc.vector.tensor_scalar(xs[:, tt, :], xt[:, tt, :], rstd[:, tt:tt + 1], None, ALU.mult).then_inc(xs_ready, 1)

            def norm_lo(j, v):
                for k in range(KT):
                    dve.wait_ge(acth_ready, KT * j + k // 2 * 2 + 2)
                    nc.vector.scalar_tensor_tensor(actl[:, k, :], ps[(6, 7, 0, 1)[k // 2]][:, (k % 2) * T:(k % 2 + 1) * T],
                                                   vcol(v, k), acth[:, k, :].bitcast(F32), ALU.mult,
                                                   ALU.subtract).then_inc(actl_ready, 1)

            def done(n):
                dve.wait_ge(panel_done, n + 1)

            dve.wait_ge(vec_turned, 1)
            nc.vector.tensor_copy(vec[:, :], ps[2][:, 0:V_ALL]).then_inc(vec_ready, 1)
            dve.wait_ge(vec_ready, 1)
            lam = vec[:, V_LAM:V_LAM + KT]
            nc.vector.scalar_tensor_tensor(lru[:, 0, :], lam, -1.0, lam, ALU.mult, ALU.max).then_inc(abs_lam, 1)
            square_sum(0)
            normalise()
            lo(0)
            norm_lo(0, V_N1)
            lo(1)
            dve.wait_ge(gw_hi, 1)
            nc.vector.tensor_tensor(gwl[:, :, :], gwr[:, :, :], gwh[:, :, :].bitcast(F32), ALU.subtract).then_inc(gw_lo, 1)

            def lru_constants():
                dve.wait_ge(exp_lam, 1)
                e, den, s, s2, p = (lru[:, i, :] for i in (1, 2, 3, 4, 5))
                link(nc.vector.tensor_scalar(den, e, 2.0, None, ALU.add))
                link(nc.vector.reciprocal(den, den))
                link(nc.vector.tensor_tensor(s, e, den, ALU.mult))
                link(nc.vector.tensor_tensor(s2, s, s, ALU.mult))
                link(nc.vector.tensor_scalar(p, s2, 1.0 / 15, None, ALU.mult))
                for q in (13, 11, 9, 7, 5, 3):
                    link(nc.vector.scalar_tensor_tensor(p, p, 1.0 / q, s2, ALU.add, ALU.mult))
                link(nc.vector.scalar_tensor_tensor(p, p, 1.0, s, ALU.add, ALU.mult))
                link(nc.vector.tensor_scalar(lru[:, 10, :], lam, -1.0, 0.0, ALU.mult, ALU.max))
                link(nc.vector.scalar_tensor_tensor(lru[:, 11, :], p, 2.0, lru[:, 10, :], ALU.mult, ALU.add))
                nc.vector.tensor_scalar(lru[:, 6, :], lru[:, 11, :], -0.5 * 8.0, None, ALU.mult)
                nc.vector.tensor_scalar(lru[:, 7, :], lru[:, 11, :], 0.5 * 8.0, None, ALU.mult)
                nc.vector.tensor_scalar(lru[:, 8, :], vec[:, V_BA:V_BA + KT], 0.5, None, ALU.mult)
                nc.vector.tensor_scalar(lru[:, 9, :], vec[:, V_BI:V_BI + KT], 0.5, None, ALU.mult).then_inc(lru_consts, 1)

            def masked_min(out_, scores, mask, o, i, start=3e38):
                return nc.vector.tensor_tensor_reduce(out=out_, in0=scores, in1=mask, scale=1.0, scalar=start,
                                                      op0=ALU.add, op1=ALU.min, accum_out=nmax[:, o, i:i + 1])

            def head_mask(k):
                dve.wait_ge(scored, k + 1)
                if k:
                    dve.wait_ge(turned, k)
                o = k % 3
                for e in range(2):
                    masked_min(prob[:, e * P:(e + 1) * P], ps[2][:, e * P:(e + 1) * P], cst[:, C_CAUS:C_CAUS + P], o, e)
                for e in range(2):
                    m = masked_min(prob[:, (1 + e) * T:(2 + e) * T], ps[3][:, e * T:(e + 1) * T],
                                   cst[:, C_ZERO:C_ZERO + T], o, 2 + e)
                m.then_inc(masked, 1)

            def head_norm(k):
                dve.wait_ge(mixed, k + 1)
                o = k % 3
                link(nc.vector.reciprocal(coef[:, o, :], sums[:, o, :]))
                c4 = coef[:, o, :].rearrange("p (t e) -> p t e", e=2)
                link(nc.vector.tensor_tensor(c4, c4, gates[:, :, k, 1:3], ALU.mult))
                for e in range(2):
                    for tt in range(TT):
                        i = 2 * tt + e
                        at = atok[:, tt, DH * k:DH * (k + 1)]
                        m = nc.vector.scalar_tensor_tensor(at, ps[6][:, i * DH:(i + 1) * DH], coef[:, o, i:i + 1], at,
                                                           ALU.mult, ALU.add)
                        if e == 0:
                            link(m)
                m.then_inc(normed, 1)
                dve.wait_ge(normed, k + 1)

            def conv(t):
                dve.wait_ge(xr_evac, t // 2 + 1)
                link(nc.vector.tensor_scalar(xc[:, t, :], xrp[:, t, 0:T], vcol(V_CW, t), vcol(V_CB, t), ALU.mult, ALU.add))
                for i in range(1, CW):
                    m = nc.vector.scalar_tensor_tensor(xc[:, t, :], xrp[:, t, i:i + T], vcol(V_CW + KT * i, t), xc[:, t, :],
                                                       ALU.mult, ALU.add)
                    if i < CW - 1:
                        link(m)
                m.then_inc(conv_done, 1)

            def recur(hf):
                t0 = 4 * hf
                ts = slice(t0, t0 + 4)
                dve.wait_ge(root_ready, hf + 1)
                dve.wait_ge(gr_gelu, 1)
                link(nc.vector.scalar_tensor_tensor(igx[:, ts, :], igx[:, ts, :], 1.0, xc[:, ts, :], ALU.add, ALU.mult))
                link(nc.vector.tensor_tensor(igx[:, ts, :], xrp[:, ts, 0:T], igx[:, ts, :], ALU.mult))
                for t in range(t0, t0 + 4):
                    m = nc.vector.tensor_tensor_scan(xc[:, t, :], abuf[:, t, :], igx[:, t, :], 0.0, ALU.mult, ALU.add)
                link(m)
                nc.vector.scalar_tensor_tensor(gru[:, ts, :], xc[:, ts, :], 0.5, gru[:, ts, :], ALU.mult,
                                               ALU.mult).then_inc(rnn_ready, 1)

            def gate_a(sg, u, bank):
                s = sg[:, 2 * u:2 * u + 2, :].rearrange("p a t -> p (a t)")
                nc.vector.scalar_tensor_tensor(s, s, 1.0, bank, ALU.add, ALU.mult).then_inc(upa_evac, 1)

            def gate_b(sa, sg, u, bank, e):
                dst = sa[:, 2 * u:2 * u + 2, :].rearrange("p a t -> p (a t)")
                s = sg[:, 2 * u:2 * u + 2, :].rearrange("p a t -> p (a t)")
                nc.vector.scalar_tensor_tensor(s, s, 1.0, bank, ALU.add, ALU.mult).then_inc(upr_evac, 1)
                dve.wait_ge(upr_evac, 4 * e + u + 1)
                nc.vector.tensor_tensor(dst, dst, s, ALU.add).then_inc(mrg_sum, 1)

            def merge_lo(sa, u, e):
                dst = sa[:, 2 * u:2 * u + 2, :]
                dve.wait_ge(mrgh_ready, 4 * e + u + 1)
                nc.vector.scalar_tensor_tensor(mrgl[:, 2 * u:2 * u + 2, :], dst, 0.5, mrgh[:, 2 * u:2 * u + 2, :].bitcast(F32),
                                               ALU.mult, ALU.subtract).then_inc(mrgl_ready, 1)

            for n in range(ML):
                if n == KCVC + 1:
                    done(KCVC)
                    for s in range(2):
                        for l in range(2):
                            for g in range(GR):
                                first = ps[KCVC % 2][DH * g:DH * (g + 1), s * T + l:s * T + l + 1]
                                win = bass.AP(first.tensor, first.offset, [first.ap[0], [2, NPOS], [16, NC]])
                                dst = flat[DH * l:DH * (l + 1), s, :].rearrange("p (j g n) -> p j g n", g=GR, n=NC)[:, :, g, :]
                                pos = vec[DH * l:DH * (l + 1), V_PK + NPOS * s:V_PK + NPOS * (s + 1)]
                                m = nc.vector.tensor_tensor(dst, win, pos.unsqueeze(2).broadcast_to([DH, NPOS, NC]), ALU.add)
                        m.then_inc(flat_ready, 1)
                k = n - CK - 1
                if 0 <= k < NH:
                    head_mask(k)
                lo(n + 2)
                if n == 1:
                    lru_constants()
                if n == KCVC + 1:
                    dve.wait_ge(flath_ready, 1)
                    nc.vector.tensor_tensor(flatl, flat[:, :, :].rearrange("p s c -> p (s c)"), flath.bitcast(F32),
                                            ALU.subtract).then_inc(flatl_ready, 1)
                if n == KWVW:
                    link(nc.vector.memset(pc[:, :, :, :], 0.0))
                    link(nc.vector.memset(vblk[:, :, :, :], 0.0))
                if n == KWVW + 1:
                    dve.wait_ge(gates_tanh, 1)
                    gf = gates[:, :, :, :].rearrange("p t h b -> p (t h b)")
                    link(nc.vector.tensor_scalar(gf, gf, 0.5, 0.5, ALU.mult, ALU.add))
                    dve.wait_ge(padded, 1)
                if 0 <= k - 2 < NH:
                    head_norm(k - 2)
                if n == XR + 1:
                    dve.wait_ge(ckv_done, 1)
                    for half in range(2):
                        nc.vector.tensor_copy(kcd[DH * half:DH * (half + 1), :, :].rearrange("p g n -> p (g n)"),
                                              ps[7][0:DH, 128:128 + 2 * NC])
                    for r in range(4):
                        m = nc.vector.tensor_copy(vblk[GS * r:GS * r + NC, :, r, :],
                                                  ps[7][0:NC, 192:192 + 2 * DH].rearrange("p (g d) -> p g d", g=GR))
                    m.then_inc(ckv_ready, 1)
                if n in (XR + 2, XR + 3):
                    e = n - XR - 2
                    dve.wait_ge(sc_done, e + 1)
                    cm = cst[:, C_CMP:C_CMP + TT * NC].rearrange("p (t n) -> p t n", n=NC)
                    nc.vector.tensor_tensor(pc[:, :, e::2, 0:NC], ps[7][:, 0:8 * NC].rearrange("p (t h n) -> p t h n", t=TT, h=4),
                                            cm.unsqueeze(2).broadcast_to([P, TT, 4, NC]), ALU.add).then_inc(sc_read, 1)
                pcv = pc[:, :, :, :].rearrange("p t h n -> p (t h) n")[:, :, 0:NC]

                def over_n(v):
                    return v.unsqueeze(2).broadcast_to([P, TT * NH, NC])

                if n == XR + 3:
                    dve.wait_ge(sc_read, 2)
                    link(nc.vector.tensor_reduce(small[:, 8:24], pcv, AX_X, ALU.min))
                    nc.vector.tensor_tensor(pcv, pcv, over_n(small[:, 8:24]), ALU.subtract).then_inc(sc_shifted, 1)
                if n == XR + 4:
                    dve.wait_ge(sc_exped, 1)
                    c16 = small[:, 40:56]
                    cth = c16.rearrange("p (t h) -> p t h", t=TT)
                    link(nc.vector.tensor_reduce(small[:, 24:40], pcv, AX_X, ALU.add))
                    link(nc.vector.reciprocal(c16, small[:, 24:40]))
                    link(nc.vector.tensor_tensor(cth, cth, gates[:, :, :, 0], ALU.mult))
                    link(nc.vector.tensor_tensor(cth, cth, cst[:, C_VALID:C_VALID + TT].unsqueeze(2).broadcast_to([P, TT, NH]),
                                                 ALU.mult))
                    nc.vector.tensor_tensor(pcv, pcv, over_n(c16), ALU.mult).then_inc(pc_ready, 1)
                if n in (XR + 6, XR + 7):
                    tt = n - XR - 6
                    dve.wait_ge(oc_done, tt + 1)
                    nc.vector.tensor_tensor(atok[:, tt, :], atok[:, tt, :], ps[7][:, :], ALU.add).then_inc(oc_read, 1)
                    dve.wait_ge(oc_read, tt + 1)
                t = n - XR - 3
                if 0 <= t < KT:
                    conv(t)
                t = n - XR - 5
                if 0 <= t < KT:
                    dve.wait_ge(lru_act, t + 1)
                    q2 = xrp[:, t, 0:T]
                    link(nc.vector.tensor_tensor(q2, abuf[:, t, :], abuf[:, t, :], ALU.mult))
                    nc.vector.scalar_tensor_tensor(q2, q2, 1.0, nth[:, :], ALU.add, ALU.mult).then_inc(lru_q, 1)
                if n == GA + 2:
                    dve.wait_ge(midh_ready, 1)
                    nc.vector.tensor_tensor(midl[:, 0:4, :].rearrange("p k t -> p (k t)"),
                                            acc4[:, 2:4, :].rearrange("p b c -> p (b c)"),
                                            midh[:, 0:4, :].rearrange("p k t -> p (k t)").bitcast(F32),
                                            ALU.subtract).then_inc(midl_ready, 1)
                if n in (GA + 2, GB + 2):
                    recur((n - GA - 2) // 4)
                if n == UPA:
                    for hf in range(2):
                        ts = slice(4 * hf, 4 * hf + 4)
                        dve.wait_ge(rnnh_ready, hf + 1)
                        nc.vector.tensor_tensor(actl[:, ts, :], gru[:, ts, :], acth[:, ts, :].bitcast(F32),
                                                ALU.subtract).then_inc(rnnl_ready, 1)
                if n in (UPA + 1, UPA + 2):
                    done(n - 1)
                    for c in range(2):
                        gate_a(sga, 2 * (n - UPA - 1) + c, ps[c][:, :])
                if UPR < n <= UPR + 4:
                    u = n - UPR - 1
                    done(n - 1)
                    if u == 0:
                        dve.wait_ge(upa_evac, 4)
                    gate_b(sga, sgb, u, ps[(n - 1) % 2][:, :], 0)
                    merge_lo(sga, u, 0)

            def residual(last):
                done(last)
                for tt in range(TT):
                    nc.vector.tensor_tensor(xt[:, tt, :], xt[:, tt, :],
                                            acc4[:, 2 * tt:2 * tt + 2, :].rearrange("p b c -> p (b c)"),
                                            ALU.add).then_inc(x_summed, 1)

            def hidden_lo(s):
                return nc.vector.tensor_tensor(midl[:, 2 * s:2 * s + 2, :].rearrange("p a t -> p (a t)"), ffs,
                                               midh[:, 2 * s:2 * s + 2, :].rearrange("p a t -> p (a t)").bitcast(F32), ALU.subtract)

            residual(ML - 1)
            square_sum(1)
            normalise()
            norm_lo(1, V_N2)
            lo(ML + 2)
            dve.wait_ge(ff_act, ML_F + 1)
            nc.vector.tensor_tensor(ffs, ffa, ffa, ALU.mult).then_inc(ff_prod, 1)
            lo(ML + 3)
            dve.wait_ge(ff_hi, ML_F + 1)
            hidden_lo(0).then_inc(ff_lo, 1)
            with dve.Fori(0, (ML_STEPS - 1) // 3) as i:
                for m in range(3):
                    n = ML + 1 + 2 * m
                    dve.wait_ge(ff_act, i * 3 + (ML_F + m + 2))
                    dve.wait_ge(ff_lo, i * 3 + (ML_F + m + 1))
                    nc.vector.tensor_tensor(ffs, ffa, ffa, ALU.mult).then_inc(ff_prod, 1)
                    lo_in_loop(i, n + 3)
                    dve.wait_ge(ff_hi, i * 3 + (ML_F + m + 2))
                    hidden_lo((m + 1) % 3).then_inc(ff_lo, 1)
                    lo_in_loop(i, n + 4)

            def swiglu(n0, f0):
                def product(at_panel, at_act, at_lo):
                    dve.wait_ge(panel_done, at_panel)
                    dve.wait_ge(ff_act, at_act)
                    dve.wait_ge(ff_lo, at_lo)
                    nc.vector.scalar_tensor_tensor(ffs, ps[1][:, :], 0.5, ffa, ALU.mult, ALU.mult).then_inc(ff_prod, 1)

                lo(n0 + 2)
                lo(n0 + 3)
                product(n0 + 2, f0 + 1, f0)
                lo(n0 + 4)
                dve.wait_ge(ff_hi, f0 + 1)
                hidden_lo(0).then_inc(ff_lo, 1)

                def two_steps(i, last):
                    for m in range(2):
                        n = n0 + 2 + 3 * m
                        lo_in_loop(i, n + 3)
                        product(i * 6 + (n + 2), i * 2 + (f0 + m + 2), i * 2 + (f0 + m + 1))
                        dve.wait_ge(ff_hi, i * 2 + (f0 + m + 2))
                        hidden_lo((m + 1) % 2).then_inc(ff_lo, 1)
                        if not (last and m and n0 == F2):
                            lo_in_loop(i, n + 4)
                            lo_in_loop(i, n + 5)

                with dve.Fori(0, (FF_STEPS - 1) // 2 - 1) as i:
                    two_steps(i, False)
                two_steps((FF_STEPS - 1) // 2 - 1, True)

            def weighted(dst, done_sem):
                for tt in range(TT):
                    nc.vector.scalar_tensor_tensor(dst[:, tt, :], xt[:, tt, :], rstd[:, tt:tt + 1], fnb[:, :], ALU.mult,
                                                   ALU.mult).then_inc(done_sem, 1)

            residual(F1 - 1)
            square_sum(2)
            dve.wait_ge(fnb_loaded, 16)
            weighted(xt, x_summed)
            square_sum(3)
            normalise()
            norm_lo(2, V_F1)
            swiglu(F1, F1_F)
            residual(QKV2 - 1)
            square_sum(4)
            normalise()
            norm_lo(3, V_MX)

            def mask2(k):
                dve.wait_ge(scored, NH + k + 1)
                dve.wait_ge(turned, NH + k)
                o = k % 3
                if k == 0:
                    dve.wait_ge(nab_ready, 2)
                if k == NH:
                    dve.wait_ge(sink_ready, 1)
                for tt in range(TT):
                    if k < NH:
                        m = masked_min(prob2[:, tt, :], ps[2][:, tt * T:(tt + 1) * T], nab[:, tt, k, :], o, tt)
                    else:
                        c = (C_ZERO, C_TRIU)[tt]
                        m = masked_min(prob2[:, tt, :], ps[2][:, tt * T:(tt + 1) * T], cst[:, c:c + T], o, tt,
                                       small[:, k - NH:k - NH + 1])
                m.then_inc(masked, 1)

            def norm2(k):
                dve.wait_ge(mixed, NH + k + 1)
                o = k % 3
                h = k % NH
                c = coef[:, o, 0:TT]
                if k < NH:
                    link(nc.vector.reciprocal(c, sums[:, o, 0:TT]))
                else:
                    link(nc.vector.tensor_tensor(c, sums[:, o, 0:TT], esink[:, o, :], ALU.add))
                    link(nc.vector.reciprocal(c, c))
                tok = atok2 if k < NH else btok
                for tt in range(TT):
                    m = nc.vector.tensor_scalar(tok[:, tt, DH * h:DH * (h + 1)], ps[4][:, tt * DH:(tt + 1) * DH],
                                                coef[:, o, tt:tt + 1], None, ALU.mult)
                m.then_inc(normed, 1)

            def heads2(n, part):
                k = turn2.get((n, part))
                if k is None:
                    return
                if k < 2 * NH:
                    mask2(k)
                if 0 <= k - 2:
                    norm2(k - 2)

            def rope(x, swapped, r1, r2, width, done_count):
                dve.wait_ge(rope_done, done_count)
                reps = width // T

                def table(c):
                    return cst[:, c:c + T].unsqueeze(1).broadcast_to([P, reps, T])

                r1, r2, x, swapped = (v.rearrange("p (a t) -> p a t", t=T) for v in (r1, r2, x, swapped))
                nc.vector.tensor_tensor(r1, x, table(C_COS), ALU.mult)
                nc.vector.tensor_tensor(r2, swapped, table(C_SIN), ALU.mult).then_inc(rope_read, 1)
                dve.wait_ge(rope_read, done_count)
                return nc.vector.tensor_tensor(x, r1, r2, ALU.add)

            for n in range(QKV2, F2):
                if n - 1 in (QKV2 + 1, QKV2 + 4):
                    u = (n - 1 - QKV2) // 3
                    done(n - 1)
                    nc.vector.tensor_copy(kaT[:, 2 * u:2 * u + 2, :].rearrange("p a t -> p (a t)"),
                                          ps[(n - 1) % 2][:, :]).then_inc(ka_evac, 1)
                heads2(n - 1, 1)
                lo(n + 2)
                if n in (QB + 2, QB + 3):
                    u = n - QB - 2
                    rope(qbT[:, 2 * u:2 * u + 2, :].rearrange("p a t -> p (a t)"), ps[7][:, :], rope1, rope2, 2 * T,
                         u + 1).then_inc(qb_ready, 1)
                if n == GA2 + 1:
                    link(rope(kbT[:, :], ps[7][:, 0:T], rope1[:, 0:T], rope2[:, 0:T], T, 3))
                    for g in range(GR):
                        for half in range(2):
                            m = nc.vector.tensor_copy(kbd[DH * half:DH * (half + 1), g, :], kbT[DH * g:DH * (g + 1), :])
                    m.then_inc(kb_ready, 1)
                heads2(n, 0)
                if n in (GA2 + 4, GB2 + 4):
                    br = n == GB2 + 4
                    dve.wait_ge(midh_ready, 2 + br)
                    dl, dh = (actl, acth) if br else (midl, midh)
                    for i in range(2):
                        m = nc.vector.tensor_tensor(dl[:, 2 * i:2 * i + 2, :].rearrange("p k t -> p (k t)"), ps[5 + i][:, :],
                                                    dh[:, 2 * i:2 * i + 2, :].rearrange("p k t -> p (k t)").bitcast(F32),
                                                    ALU.subtract)
                    m.then_inc(midl_ready, 1)
                if n in (BRA + 1, BRA + 2):
                    done(n - 1)
                    for c in range(2):
                        gate_a(sga2, 2 * (n - BRA - 1) + c, ps[c][:, :])
                if n in (BRB + 1, BRB + 2):
                    done(n - 1)
                    dve.wait_ge(upa_evac, 8)
                    for c in range(2):
                        u = 2 * (n - BRB - 1) + c
                        gate_b(sga2, sgb2, u, ps[c][:, :], 1)
                    for c in range(2):
                        merge_lo(sga2, 2 * (n - BRB - 1) + c, 1)

            residual(F2 - 1)
            square_sum(5)
            normalise()
            norm_lo(4, V_F2)
            swiglu(F2, F2_F)
            residual(END - 1)
            square_sum(6)
            dve.wait_ge(fnb_loaded, 32)
            weighted(xs, out_ready)


_INS = ["x", "norm1_w", "w_in", "cmp_pos_k", "cmp_pos_v", "cmp_k_w1", "cmp_k_w2", "cmp_v_w1", "cmp_v_w2", "conv_w",
        "conv_b", "lru_w_a", "lru_b_a", "lru_w_i", "lru_b_i", "lru_lambda", "w_up_attn", "w_up_rnn", "w_out", "norm2_w",
        "mlp_w1", "mlp_w2", "final_norm_w", "ffn1_norm_2", "ffn1_w_gate_2", "ffn1_w_up_2", "ffn1_w_down_2",
        "mix_norm_2", "w_in_2", "sink_logit_2", "w_branch_a_2", "w_branch_b_2", "w_out_2",
        "ffn2_norm_2", "ffn2_w_gate_2", "ffn2_w_up_2", "ffn2_w_down_2", "final_norm_2"]


def kernel(**inputs):
    import concourse.bacc as bacc
    from concourse.bass_utils import run_bass_kernel_spmd

    nc = bacc.Bacc("TRN2", target_bir_lowering=False, num_devices=1)
    arrays = {name: np.ascontiguousarray(inputs[name]) for name in _INS}
    arrays["rpb_rev"] = np.ascontiguousarray(np.asarray(inputs["na_rpb_2"])[..., ::-1])
    arrays["consts"] = constants()
    aps = {name: nc.dram_tensor(f"in_{name}", v.shape, mybir.dt.from_np(v.dtype), kind="ExternalInput").ap()
           for name, v in arrays.items()}
    out = nc.dram_tensor("out", (1, T, D), F32, kind="ExternalOutput").ap()
    build(nc, aps, out)
    r = run_bass_kernel_spmd(nc, [{f"in_{name}": v for name, v in arrays.items()}], core_ids=[0])
    return r.results[0]["out"]
```

```python
from contextlib import ExitStack

import numpy as np
import concourse.bass as bass
from concourse import mybir

F32 = mybir.dt.float32
F32R = mybir.dt.float32r
ALU = mybir.AluOpType
ACT = mybir.ActivationFunctionType
AX_X = mybir.AxisListType.X

P = 128
T = 256
TT = T // P
D = 1024
KT = D // P
DH = 64
NH = 8
GR = 2
NC = 15
CH = 256
NPOS = 16
CW = 4
PW = 2048
R = 3
QSCALE = -(DH ** -0.5)
EPS = 1e-6
BIG = 1e30
GS = 32

Q, KCVC, KSVS, KWVW, CK, CV, XR, GRP, GA, GB = 0, 2, 3, 4, 5, 7, 9, 13, 17, 21
UPA, UPR, WO, ML = 25, 27, 31, 35
ML_STEPS = 16
F1 = ML + 2 * ML_STEPS
FF_STEPS = 11
QKV2 = F1 + 3 * FF_STEPS
QB, KBVB, GA2, GB2 = QKV2 + 6, QKV2 + 8, QKV2 + 9, QKV2 + 13
BRA, BRB, WO2, F2 = QKV2 + 17, QKV2 + 19, QKV2 + 21, QKV2 + 25
END = F2 + 3 * FF_STEPS

V_N1, V_N2, V_F1, V_MX, V_F2, V_CW, V_CB, V_BA, V_BI, V_LAM, V_PK, V_PV = (
    0, 8, 16, 24, 32, 40, 72, 80, 88, 96, 104, 120)
V_ALL = 136

C_ID, C_MHALF, C_TRIU, C_ZERO, C_CAUS, C_PERM, C_CMP, C_VALID, C_NA, C_COS, C_SIN = (
    0, 128, 130, 258, 386, 514, 642, 674, 676, 740, 996)
C_FIRST = C_TRIU
C_ALL = 1252


def constants():
    c = np.zeros((P, C_ALL), np.float32)
    i = np.arange(P)
    c[:, C_ID:C_ID + P] = np.eye(P)
    c[:, C_TRIU:C_TRIU + P] = np.where(i[None, :] >= i[:, None], 0, BIG)
    c[:, C_CAUS:C_CAUS + P] = np.where(i[None, :] <= i[:, None], 0, BIG)
    swap = np.zeros((P, P), np.float32)
    swap[(i // 64) * 64 + (i % 64 + 32) % 64, i] = 1
    c[:, C_PERM:C_PERM + P] = swap
    n = np.arange(NC)
    for tt in range(TT):
        c[:, C_CMP + tt * NC:C_CMP + tt * NC + NC] = np.where(
            n[None, :] * 16 + 31 <= (tt * P + i)[:, None], 0, BIG)
        c[:, C_VALID + tt] = tt * P + i >= 31
    col = i % 64
    start = np.clip(col - 8, 0, 48)
    cc = np.arange(64)
    inside = (cc[None, :] >= start[:, None]) & (cc[None, :] < start[:, None] + 16)
    c[:, C_NA:C_NA + 64] = np.where(inside, 0, BIG)
    half = DH // 2
    inv = np.float32(10000.0) ** (-np.arange(half, dtype=np.float32) / np.float32(half))
    ang = np.arange(T, dtype=np.float32)[None, :] * inv[i % half][:, None].astype(np.float32)
    c[:, C_COS:C_COS + T] = np.cos(ang)
    c[:, C_SIN:C_SIN + T] = np.sin(ang) * np.where(i % 64 < half, -1, 1)[:, None]
    c[:, C_MHALF:C_MHALF + 2] = -0.5
    return c


def build(nc, a, out):
    ctx = ExitStack()
    with ctx:
        def sb(name, shape, dt=F32):
            return ctx.enter_context(nc.sbuf_tensor(name, shape, dt))

        def sem(name):
            return ctx.enter_context(nc.semaphore(name))

        raw = sb("raw", [P, R, PW])
        wh = sb("wh", [P, R, PW], F32R)
        wl = sb("wl", [P, R, PW], F32R)
        acth = sb("acth", [P, KT, T], F32R)
        actl = sb("actl", [P, KT, T], F32R)
        midh = sb("midh", [P, 6, T], F32R)
        midl = sb("midl", [P, 6, T], F32R)
        mrgh = sb("mrgh", [P, KT, T], F32R)
        mrgl = sb("mrgl", [P, KT, T], F32R)
        cst = sb("cst", [P, C_ALL])
        xt = sb("xt", [P, TT, D])
        xs = sb("xs", [P, TT, D])
        vec = sb("vec", [P, V_ALL])
        vrow = sb("vrow", [V_PK, P])
        prow = sb("prow", [V_ALL - V_PK, P])
        gwr = sb("gwr", [P, KT, 24])
        gwh = sb("gwh", [P, KT, 24], F32R)
        gwl = sb("gwl", [P, KT, 24], F32R)
        cw2 = sb("cw2", [P, 2, 2, DH])
        hid = sb("hid", [P, 2, 2, 2 * NC])
        hidt = sb("hidt", [2 * NC, 2 * CH])
        gatT = sb("gatT", [24, T])
        ssq = sb("ssq", [P, 2 * TT])
        wsq = sb("wsq", [P, 2 * TT])
        part = sb("part", [P, TT])
        var = sb("var", [P, TT])
        rstd = sb("rstd", [P, TT])
        wpart = sb("wpart", [P, TT])
        wvar = sb("wvar", [P, TT])
        wrstd = sb("wrstd", [P, TT])
        small = sb("small", [P, 64])
        lru = sb("lru", [P, 12, KT])
        nmax = sb("nmax", [P, 3, 4])
        sums = sb("sums", [P, 3, 4])
        coef = sb("coef", [P, 3, 4])
        esink = sb("esink", [P, 3, 2])
        nsink = sb("nsink", [P, NH])
        arena = sb("arena", [P, 15600])

        def carve(at, *shape):
            n = int(np.prod(shape))
            v = arena[:, at:at + n]
            names = "abcd"[:len(shape)]
            if len(shape) == 1:
                return v
            return v.rearrange("p (%s) -> p %s" % (" ".join(names), " ".join(names)),
                               **{k: s for k, s in zip(names, shape)})

        xrp = carve(0, KT, T + CW - 1)
        xc = carve(2080, KT, T)
        igx = carve(4128, KT, T)
        gru = carve(6176, KT, T)
        qT = carve(8224, 4, T)
        ksd = carve(9248, GR, T)
        kwd = carve(9760, GR, T)
        vsw = carve(10272, TT, 2, P)
        prob = carve(10784, 768)
        probT = carve(11552, 768)
        vT = carve(10784, 2, T)
        sga = carve(10272, KT, T)
        bd = carve(12320, KT, 2, P)
        sgb = carve(12320, KT, T)
        atok = carve(14368, TT, NH * DH)
        flat = carve(4128, 2, NPOS * 2 * NC)
        abuf = xs[:, :, :].rearrange("p t (k f) -> p (t k) f", f=T)
        gates = sb("gates", [P, TT, NH, 3])
        xsf = xs[:, :, :].rearrange("p t d -> p (t d)")
        vblk = xsf[:, 1024:1536].rearrange("p (g r d) -> p g r d", g=GR, r=4)
        pc = xsf[:, 512:1024].rearrange("p (t h n) -> p t h n", t=TT, h=NH)
        pcT = xsf[:, 1536:2048].rearrange("p (a q) -> p a q", q=P)
        kcd = sb("kcd", [P, GR, NC])
        thr = carve(9760, T)
        nth = carve(9760 + T, T)
        nab = carve(0, TT, NH, T)
        sga2 = carve(4096, KT, T)
        sgb2 = carve(6144, KT, T)
        nabr = carve(4096, TT, NH, T)
        qaT = carve(8192, 4, T)
        kaT = carve(9216, 4, T)
        va = carve(10240, TT, NH * DH)
        qbT = carve(11264, 4, T)
        kbT = carve(12288, T)
        kbd = carve(12544, GR, T)
        vb = carve(13056, TT, P)
        prob2 = carve(13312, TT, T)
        probT2 = carve(13824, 512)
        atok2 = carve(14336, TT, NH * DH)
        btok = xs[:, 0, :].rearrange("p (t n) -> p t n", t=TT)
        vbT = xs[:, 0, 0:T]
        rope1 = xs[:, 1, 0:512]
        rope2 = xs[:, 1, 512:1024]
        fnb = carve(0, D)
        sqx = carve(1024, TT, D)
        sqy = carve(3072, TT, D)
        ffa = xs[:, 0, 0:512]
        ffs = xs[:, 0, 512:1024]

        ps = [ctx.enter_context(nc.psum_tensor(f"ps{i}", [P, 512], F32)) for i in range(2)]
        acc4 = ctx.enter_context(nc.psum_tensor("acc4", [P, 4, 512], F32))
        ps += [acc4[:, i, :] for i in range(4)]
        ps += [ctx.enter_context(nc.psum_tensor(f"ps{i}", [P, 512], F32)) for i in (6, 7)]

        ident = cst[:, C_ID:C_ID + P]

        def vcol(v, k=0):
            return vec[:, v + k:v + k + 1]

        x_loaded = [sem(f"x_loaded{tt}") for tt in range(TT)]
        id_loaded = sem("id_loaded")
        cst_loaded = sem("cst_loaded")
        vec_loaded = sem("vec_loaded")
        small_loaded = sem("small_loaded")
        bd_zeroed = sem("bd_zeroed")
        bd_loaded = sem("bd_loaded")
        fnb_loaded = sem("fnb_loaded")
        nab_loaded = sem("nab_loaded")
        nab_ready = sem("nab_ready")
        sink_ready = sem("sink_ready")
        padded = sem("padded")
        panel_loaded = [sem(f"panel_loaded{s}") for s in range(R)]
        hi_ready = sem("hi_ready")
        lo_ready = sem("lo_ready")
        panel_done = sem("panel_done")
        dve_chain = sem("dve_chain")
        act_chain = sem("act_chain")
        pool_chain = sem("pool_chain")
        vec_turned = sem("vec_turned")
        vec_ready = sem("vec_ready")
        exp_lam = sem("exp_lam")
        abs_lam = sem("abs_lam")
        lru_consts = sem("lru_consts")
        x_summed = sem("x_summed")
        ssq_ready = sem("ssq_ready")
        y_ready = sem("y_ready")
        wsq_ready = sem("wsq_ready")
        rstd_ready = sem("rstd_ready")
        wrstd_ready = sem("wrstd_ready")
        bank_done = sem("bank_done")
        stream_ready = sem("stream_ready")
        xs_ready = sem("xs_ready")
        xs_turned = sem("xs_turned")
        acth_ready = sem("acth_ready")
        actl_ready = sem("actl_ready")
        q_evac = sem("q_evac")
        flat_ready = sem("flat_ready")
        flath_ready = sem("flath_ready")
        flatl_ready = sem("flatl_ready")
        ks_evac = sem("ks_evac")
        kw_evac = sem("kw_evac")
        gw_hi = sem("gw_hi")
        gw_lo = sem("gw_lo")
        gates_done = sem("gates_done")
        gates_tanh = sem("gates_tanh")
        gates_ready = sem("gates_ready")
        hidt_ready = sem("hidt_ready")
        hid_turned = sem("hid_turned")
        hid_ready = sem("hid_ready")
        gates_turned = sem("gates_turned")
        v_turned = sem("v_turned")
        v_ready = sem("v_ready")
        ckv_done = sem("ckv_done")
        ckv_ready = sem("ckv_ready")
        sc_done = sem("sc_done")
        sc_read = sem("sc_read")
        sc_shifted = sem("sc_shifted")
        sc_exped = sem("sc_exped")
        pc_ready = sem("pc_ready")
        pc_turned = sem("pc_turned")
        pcT_ready = sem("pcT_ready")
        oc_done = sem("oc_done")
        oc_read = sem("oc_read")
        scored = sem("scored")
        masked = sem("masked")
        exped = sem("exped")
        turned = sem("turned")
        probT_ready = sem("probT_ready")
        mixed = sem("mixed")
        normed = sem("normed")
        atok_turned = sem("atok_turned")
        midh_ready = sem("midh_ready")
        midl_ready = sem("midl_ready")
        xr_evac = sem("xr_evac")
        gr_evac = sem("gr_evac")
        gr_gelu = sem("gr_gelu")
        ga_evac = sem("ga_evac")
        gb_evac = sem("gb_evac")
        conv_done = sem("conv_done")
        lru_done = sem("lru_done")
        lru_act = sem("lru_act")
        lru_q = sem("lru_q")
        root_ready = sem("root_ready")
        rnn_ready = sem("rnn_ready")
        rnnh_ready = sem("rnnh_ready")
        rnnl_ready = sem("rnnl_ready")
        upa_evac = sem("upa_evac")
        upr_evac = sem("upr_evac")
        mrg_sum = sem("mrg_sum")
        mrgh_ready = sem("mrgh_ready")
        mrgl_ready = sem("mrgl_ready")
        seeded = sem("seeded")
        ff_act = sem("ff_act")
        ff_prod = sem("ff_prod")
        ff_hi = sem("ff_hi")
        ff_lo = sem("ff_lo")
        qa_evac = sem("qa_evac")
        ka_evac = sem("ka_evac")
        va_evac = sem("va_evac")
        qb_evac = sem("qb_evac")
        kv_evac = sem("kv_evac")
        rope_done = sem("rope_done")
        rope_read = sem("rope_read")
        qb_ready = sem("qb_ready")
        kb_ready = sem("kb_ready")
        out_ready = sem("out_ready")
        stored = sem("stored")

        def pv(n, kt, dst):
            return dst[:, n % R, :].rearrange("p (k c) -> p k c", k=kt)

        TURNED = (0, 1, 6, 7)

        def half_row(b):
            return b // 2, slice(512 * (b % 2), 512 * (b % 2) + 512)

        w_in, w_in2 = a["w_in"][0], a["w_in_2"][0]

        def up_src(w, col, width=256):
            return w[:, bass.ds(col, width)].rearrange("(k p) c -> p k c", p=P)

        def down_src(w, row):
            return w[bass.ds(row, 256), :].rearrange("(k p) c -> p k c", p=P)

        col1 = {Q: 0, Q + 1: 256, KCVC: 512, KSVS: 768, KWVW: 1024}
        for u in range(4):
            col1[XR + u] = 1304 + 256 * u
            col1[GRP + u] = 2328 + 256 * u
            col1[GA + u] = 3352 + 256 * u
            col1[GB + u] = 4376 + 256 * u
        col2 = {}
        for u in range(2):
            for s in range(3):
                col2[QKV2 + 3 * u + s] = 512 * s + 256 * u
            col2[QB + u] = 1536 + 256 * u
        col2[KBVB] = 2048
        for u in range(4):
            col2[GA2 + u] = 2304 + 256 * u
            col2[GB2 + u] = 3328 + 256 * u

        block = ctx.enter_context(nc.Block())

        @block.sync
        def _(sp):
            for tt in range(TT):
                sp.dma_start(xt[:, tt, :], a["x"][0, tt * P:(tt + 1) * P, :]).then_inc(x_loaded[tt], 16)
            sp.dma_start(cst[:, 0:C_FIRST], a["consts"][:, 0:C_FIRST]).then_inc(id_loaded, 16)

            def load(n, kt, src):
                if n >= R:
                    sp.wait_ge(lo_ready, n - R + 1)
                sp.dma_start(pv(n, kt, raw), src).then_inc(panel_loaded[n % R], 16)

            def load_in_loop(i, n, kt, src):
                sp.wait_ge(lo_ready, i * 6 + (n - R + 1))
                sp.dma_start(pv(n, kt, raw), src).then_inc(panel_loaded[n % R], 16)

            def load_ffn(n0, wg, wu, wd):
                load(n0, KT, up_src(wg, 0))
                load(n0 + 1, KT, up_src(wu, 0))
                with sp.Fori(0, (FF_STEPS - 1) // 2) as i:
                    for m in range(2):
                        n = n0 + 2 + 3 * m
                        load_in_loop(i, n, KT, up_src(wg, i * 512 + 256 * (m + 1)))
                        load_in_loop(i, n + 1, KT, up_src(wu, i * 512 + 256 * (m + 1)))
                        load_in_loop(i, n + 2, 2, down_src(wd, i * 512 + 256 * m))
                load(n0 + 3 * FF_STEPS - 1, 2, down_src(wd, 256 * (FF_STEPS - 1)))

            load(0, KT, up_src(w_in, col1[0]))
            load(1, KT, up_src(w_in, col1[1]))
            sp.dma_start(cst[:, C_FIRST:], a["consts"][:, C_FIRST:]).then_inc(cst_loaded, 16)
            for n in range(2, CK):
                load(n, KT, up_src(w_in, col1[n]))
            for n, name in ((CK, "cmp_k_w1"), (CV, "cmp_v_w1")):
                for u in range(2):
                    load(n + u, KT, a[name][0, 1024 * u:1024 * (u + 1), :].rearrange("(k p) c -> p k c", p=P))
            for n in range(XR, UPA):
                load(n, KT, up_src(w_in, col1[n]))
            for u in range(2):
                load(UPA + u, 4, up_src(a["w_up_attn"][0], 512 * u, 512))
            for u in range(4):
                load(UPR + u, KT, up_src(a["w_up_rnn"][0], 256 * u))
            for u in range(4):
                load(WO + u, 2, down_src(a["w_out"][0], 256 * u))
            w1, w2 = a["mlp_w1"][0], a["mlp_w2"][0]
            load(ML, KT, up_src(w1, 0))
            with sp.Fori(0, (ML_STEPS - 1) // 3) as i:
                for m in range(3):
                    n = ML + 1 + 2 * m
                    load_in_loop(i, n, KT, up_src(w1, i * 768 + 256 * (m + 1)))
                    load_in_loop(i, n + 1, 2, down_src(w2, i * 768 + 256 * m))
            load(F1 - 1, 2, down_src(w2, 256 * (ML_STEPS - 1)))
            load_ffn(F1, a["ffn1_w_gate_2"][0], a["ffn1_w_up_2"][0], a["ffn1_w_down_2"][0])
            for n in range(QKV2, BRA):
                load(n, KT, up_src(w_in2, col2[n]))
            for n, name in ((BRA, "w_branch_a_2"), (BRB, "w_branch_b_2")):
                for u in range(2):
                    load(n + u, 4, up_src(a[name][0], 512 * u, 512))
            for u in range(4):
                load(WO2 + u, 2, down_src(a["w_out_2"][0], 256 * u))
            load_ffn(F2, a["ffn2_w_gate_2"][0], a["ffn2_w_up_2"][0], a["ffn2_w_down_2"][0])
            for b in range(2 * TT):
                tt, cs = half_row(b)
                sp.wait_ge(out_ready, b + 1)
                sp.dma_start(out[0, tt * P:(tt + 1) * P, cs], xs[:, tt, cs]).then_inc(stored, 16)
            sp.wait_ge(stored, 16 * 2 * TT)

        @block.gpsimd
        def _(pool):
            nc.gpsimd.memset(bd[:, :, :, :], 0.0).then_inc(bd_zeroed, 1)
            nc.gpsimd.memset(xrp[:, :, 0:CW - 1], 0.0)
            nc.gpsimd.memset(atok[:, :, :], 0.0).then_inc(padded, 1)
            pool.dma_start(gwr[:, :, :], w_in[:, 1280:1304].rearrange("(k p) c -> p k c", p=P)).then_inc(small_loaded, 16)
            for s, name in enumerate(("cmp_k_w2", "cmp_v_w2")):
                pool.dma_start(cw2[:, s, :, :], a[name][0].rearrange("(c p) d -> p c d", p=P)).then_inc(small_loaded, 16)
            pool.dma_start(nsink[:, :], a["sink_logit_2"][0:1, :].broadcast_to([P, NH])).then_inc(small_loaded, 16)
            pc_ = [0]

            def link(ins):
                pc_[0] += 1
                ins.then_inc(pool_chain, 1)
                pool.wait_ge(pool_chain, pc_[0])

            def norm_root(r, weighted=False):
                if r == 0:
                    pool.wait_ge(id_loaded, 16)
                for tt in range(TT):
                    t1, first, second = slice(tt, tt + 1), slice(2 * tt, 2 * tt + 1), slice(2 * tt + 1, 2 * tt + 2)
                    mhalf = cst[:, C_MHALF:C_MHALF + 1]
                    pool.wait_ge(ssq_ready, 4 * r + 2 * tt + 1)
                    link(nc.gpsimd.tensor_scalar(part[:, t1], ssq[:, first], 1.0 / D, EPS, ALU.mult, ALU.add))
                    pool.wait_ge(ssq_ready, 4 * r + 2 * tt + 2)
                    link(nc.gpsimd.tensor_scalar(var[:, t1], ssq[:, second], 1.0 / D, part[:, t1], ALU.mult, ALU.add))
                    nc.gpsimd.tensor_tensor(rstd[:, t1], var[:, t1], mhalf, ALU.pow).then_inc(rstd_ready, 1)
                    if weighted:
                        pool.wait_ge(wsq_ready, 2 * tt + 2)
                        link(nc.gpsimd.tensor_tensor(wpart[:, t1], wsq[:, first], wsq[:, second], ALU.add))
                        pool.wait_ge(rstd_ready, TT * r + tt + 1)
                        link(nc.gpsimd.tensor_scalar(wpart[:, t1], wpart[:, t1], rstd[:, t1], rstd[:, t1], ALU.mult, ALU.mult))
                        link(nc.gpsimd.tensor_scalar(wvar[:, t1], wpart[:, t1], 1.0 / D, EPS, ALU.mult, ALU.add))
                        nc.gpsimd.tensor_tensor(wrstd[:, t1], wvar[:, t1], mhalf, ALU.pow).then_inc(wrstd_ready, 1)

            norm_root(0)
            pool.wait_ge(bd_zeroed, 1)
            for s, name in enumerate(("lru_w_a", "lru_w_i")):
                pairs = a[name][0].rearrange("(t e) i j -> e i t j", e=2)
                for e in range(2):
                    pool.dma_start(bd[DH * e:DH * (e + 1), :, s, DH * e:DH * (e + 1)], pairs[e]).then_inc(bd_loaded, 16)
            pool.wait_ge(small_loaded, 64)
            nc.gpsimd.tensor_scalar(small[:, 0:NH], nsink[:, :], -1.0, None, ALU.mult).then_inc(sink_ready, 1)

            pool.wait_ge(panel_done, ML)
            norm_root(1)
            pool.dma_start(fnb[:, :], a["final_norm_w"].rearrange("(o d) -> o d", o=1).broadcast_to([P, D])).then_inc(fnb_loaded, 16)
            norm_root(2, weighted=True)
            pool.wait_ge(stream_ready, TT)
            rpb = a["rpb_rev"]
            for tt in range(TT):
                for rr in range(2):
                    for i in range(4):
                        src = bass.AP(rpb.tensor, (7 + i - 2 * tt - rr) * 31 + 15 - 63, [[1, 64], [15 * 31, NH], [1, 64]])
                        pool.dma_start(nabr[64 * rr:64 * rr + 64, tt, :, 64 * i:64 * i + 64], src).then_inc(nab_loaded, 16)
            pool.wait_ge(nab_loaded, 16 * 16)
            pool.wait_ge(cst_loaded, 16)
            for tt in range(TT):
                bias = nabr[:, tt, :, :].rearrange("p h (i c) -> p (h i) c", c=64)[:, :, ::-1]
                mask = cst[:, C_NA:C_NA + 64].unsqueeze(1).broadcast_to([P, 4 * NH, 64])
                nc.gpsimd.tensor_tensor(nab[:, tt, :, :].rearrange("p h (i c) -> p (h i) c", c=64),
                                        mask, bias, ALU.subtract).then_inc(nab_ready, 1)
            norm_root(3)
            norm_root(4)
            pool.wait_ge(panel_done, F2)
            pool.dma_start(fnb[:, :], a["final_norm_2"].rearrange("(o d) -> o d", o=1).broadcast_to([P, D])).then_inc(fnb_loaded, 16)
            norm_root(5)


        flath = mrgh[:, :, :].rearrange("p k t -> p (k t)")[:, 0:2 * NPOS * 2 * NC]
        flatl = mrgl[:, :, :].rearrange("p k t -> p (k t)")[:, 0:2 * NPOS * 2 * NC]
        ML_F, F1_F, F2_F = 0, ML_STEPS, ML_STEPS + FF_STEPS

        def head2(k):
            h = k % NH
            b = DH * (h % 2)
            if k < NH:
                return (qaT[b:b + DH, h // 2, :], kaT[b:b + DH, h // 2, :],
                        [va[:, kt, DH * h:DH * (h + 1)] for kt in range(TT)])
            g = h // 4
            return (qbT[b:b + DH, h // 2, :], kbd[b:b + DH, g, :],
                    [vb[:, kt, DH * g:DH * (g + 1)] for kt in range(TT)])

        def up_bank(u, c):
            return ps[(6, 7, 0, 1)[2 * u + c]]

        TURN_OUT = ((5, 6), (4, 5))

        turn2 = {(QKV2 + 2 + k, 1): k for k in range(7)}
        turn2[QKV2 + 9, 1] = 7
        turn2[QKV2 + 10, 1] = 8
        for k in range(9, 17):
            turn2[QKV2 + 11 + (k - 9) // 2, (k - 9) % 2] = k
        turn2[QKV2 + 15, 1] = 17

        @block.tensor
        def _(pe):
            def split(n):
                pe.wait_ge(lo_ready, n + 1)

            def three(out_, lh, ll, rh, rl, start, stop, **kw):
                nc.tensor.matmul(out_, lh, rh, start=start, stop=False, **kw)
                nc.tensor.matmul(out_, lh, rl, start=False, stop=False, **kw)
                return nc.tensor.matmul(out_, ll, rh, start=False, stop=stop, **kw)

            def feature_tile(n, kt, c, out_, ah, al, norm=None):
                h, l = pv(n, kt, wh), pv(n, kt, wl)
                for k in range(kt):
                    if norm is not None and c == 0:
                        pe.wait_ge(actl_ready, KT * norm + max(k + 1, 2))
                    last = three(out_, h[:, k, c * P:(c + 1) * P], l[:, k, c * P:(c + 1) * P],
                                 ah[:, k, :], al[:, k, :], k == 0, k == kt - 1)
                return last

            def token_tile(n, c0, c1, tt, out_):
                h, l = pv(n, KT, wh), pv(n, KT, wl)
                s = slice(tt * P, (tt + 1) * P)
                for k in range(KT):
                    last = three(out_, acth[:, k, s], actl[:, k, s], h[:, k, c0:c1], l[:, k, c0:c1],
                                 k == 0, k == KT - 1)
                return last

            def down(n, kt, lhs_h, lhs_l, first, final):
                h, l = pv(n, 2, wh), pv(n, 2, wl)
                steps = [(k, tt, hf) for k in range(2) for tt in range(TT) for hf in range(2)]
                if final:
                    steps = sorted(steps, key=lambda v: (v[1], v[2], v[0]))
                for k, tt, hf in steps:
                    s = slice(tt * P, (tt + 1) * P)
                    cs = slice(512 * hf, 512 * hf + 512)
                    last = three(acc4[:, 2 * tt + hf, :], lhs_h[:, kt + k, s], lhs_l[:, kt + k, s],
                                 h[:, k, cs], l[:, k, cs], first and k == 0, final and k == 1)
                    if final and k == 1 and 2 * tt + hf < 3:
                        last.then_inc(bank_done, 1)
                return last

            def seed(banks, r):
                for b in banks:
                    pe.wait_ge(x_summed, 4 * (r - 1) + b + 1)
                    nc.tensor.matmul(acc4[:, b, :], cst[:, C_ZERO:C_ZERO + P], cst[:, 0:512], start=True, stop=False)

            def turn_tokens(j):
                for b in range(2 * TT):
                    tt, hf = b // 2, b % 2
                    pe.wait_ge(xs_ready, 4 * j + b + 1)
                    for k in range(4 * hf, 4 * hf + 4):
                        m = nc.tensor.transpose(ps[TURNED[k // 2]][:, (k % 2) * T + tt * P:(k % 2) * T + (tt + 1) * P],
                                                xs[:, tt, k * P:(k + 1) * P], ident)
                        if tt == TT - 1 and k % 2:
                            m.then_inc(xs_turned, 1)

            pe.wait_ge(id_loaded, 16)
            turn_tokens(0)
            pe.wait_ge(vec_loaded, 16 * 12)
            nc.tensor.transpose(ps[2][:, 0:V_PK], vrow[:, :], cst[0:V_PK, C_ID:C_ID + V_PK])
            nc.tensor.transpose(ps[2][:, V_PK:V_ALL], prow[:, :],
                                cst[0:V_ALL - V_PK, C_ID:C_ID + V_ALL - V_PK]).then_inc(vec_turned, 1)

            def head_score(k):
                if k:
                    pe.wait_ge(masked, k)
                b, t, g = DH * (k % 2), k // 2, k // 4
                q = qT[b:b + DH, t, :]
                for e, kd in enumerate((ksd, kwd)):
                    nc.tensor.matmul(ps[2][:, e * P:(e + 1) * P], q[:, 0:P], kd[b:b + DH, g, 0:P], start=True, stop=True)
                for e, kd in enumerate((ksd, kwd)):
                    m = nc.tensor.matmul(ps[3][:, e * T:(e + 1) * T], q[:, P:T], kd[b:b + DH, g, :], start=True, stop=True)
                m.then_inc(scored, 1)

            def head_turn(k):
                pe.wait_ge(exped, k + 1)
                if k:
                    pe.wait_ge(probT_ready, k)
                else:
                    pe.wait_ge(gates_ready, 1)
                for i in range(6):
                    m = nc.tensor.transpose(ps[4 + i // 4][:, (i % 4) * P:(i % 4 + 1) * P], prob[:, i * P:(i + 1) * P], ident)
                m.then_inc(turned, 1)

            def head_mix(k):
                pe.wait_ge(probT_ready, k + 1)
                if k:
                    pe.wait_ge(normed, k)
                else:
                    pe.wait_ge(v_ready, 1)
                vs = slice(DH * (k // 4), DH * (k // 4) + DH)
                for e in range(2):
                    nc.tensor.matmul(ps[6][:, e * DH:(e + 1) * DH], probT[:, e * P:(e + 1) * P], vsw[:, 0, e, vs],
                                     start=True, stop=True)
                    for kt in range(TT):
                        c = (2 + 2 * e + kt) * P
                        m = nc.tensor.matmul(ps[6][:, (2 + e) * DH:(3 + e) * DH], probT[:, c:c + P], vsw[:, kt, e, vs],
                                             start=kt == 0, stop=kt == 1)
                m.then_inc(mixed, 1)

            def heads(k):
                if 0 <= k - 2 < NH:
                    head_mix(k - 2)
                if 0 <= k - 1 < NH:
                    head_turn(k - 1)
                if k < NH:
                    head_score(k)

            def free_bank(n):
                if n in (KCVC, KSVS):
                    pe.wait_ge(q_evac, n - 1)
                elif n == KWVW:
                    pe.wait_ge(flat_ready, 2)
                elif n == XR:
                    pe.wait_ge(ks_evac, 1)
                elif n == XR + 1:
                    pe.wait_ge(kw_evac, 1)
                elif XR + 2 <= n < UPA:
                    group = (n - 2 - XR) // 4
                    pe.wait_ge((xr_evac, gr_evac, ga_evac, gb_evac)[group], (n - 2 - XR) % 4 + 1)

            for n in range(UPA):
                split(n)
                free_bank(n)
                if CK <= n < XR:
                    s, u = (n - CK) // 2, (n - CK) % 2
                    if n == CK:
                        pe.wait_ge(flatl_ready, 1)
                    h, l = pv(n, KT, wh), pv(n, KT, wl)
                    for k in range(KT):
                        at = (s * NPOS + u * KT + k) * 2 * NC
                        m = three(ps[7][0:2 * NC, s * CH:(s + 1) * CH], flath[:, at:at + 2 * NC], flatl[:, at:at + 2 * NC],
                                  h[:, k, :], l[:, k, :], u == 0 and k == 0, u == 1 and k == KT - 1)
                else:
                    for c in range(2):
                        m = feature_tile(n, KT, c, ps[n % 2][:, c * T:(c + 1) * T], acth, actl, 0 if n == 0 else None)
                m.then_inc(panel_done, 1)

                if n == KWVW:
                    pe.wait_ge(gw_lo, 1)
                    for k in range(KT):
                        m = three(ps[5][0:24, 0:T], gwh[:, k, :], gwl[:, k, :], acth[:, k, :], actl[:, k, :],
                                  k == 0, k == KT - 1)
                    m.then_inc(gates_done, 1)
                if n == CK:
                    pe.wait_ge(q_evac, 2)
                    pe.wait_ge(ks_evac, 1)
                    pe.wait_ge(kw_evac, 1)
                    for e in range(2):
                        for tt in range(TT):
                            m = nc.tensor.transpose(ps[6][:, (2 * tt + e) * P:(2 * tt + e + 1) * P],
                                                    vT[:, e, tt * P:(tt + 1) * P], ident)
                    m.then_inc(v_turned, 1)
                    pe.wait_ge(gates_tanh, 1)
                    for tt in range(TT):
                        m = nc.tensor.transpose(ps[5][:, tt * 24:(tt + 1) * 24], gatT[:, tt * P:(tt + 1) * P],
                                                cst[0:24, C_ID:C_ID + 24])
                    m.then_inc(gates_turned, 1)
                if CK <= n < CK + NH + 2:
                    heads(n - CK)
                if n == XR:
                    pe.wait_ge(hidt_ready, 1)
                    for i in range(4):
                        m = nc.tensor.transpose(ps[7][:, i * 2 * NC:(i + 1) * 2 * NC], hidt[:, i * P:(i + 1) * P],
                                                cst[0:2 * NC, C_ID:C_ID + 2 * NC])
                    m.then_inc(hid_turned, 1)
                if n == XR + 1:
                    pe.wait_ge(hid_ready, 1)
                    for c in range(2):
                        nc.tensor.matmul(ps[7][0:DH, 128:128 + 2 * NC], cw2[:, 0, c, :], hid[:, 0, c, :],
                                         start=c == 0, stop=c == 1)
                    for g in range(GR):
                        for c in range(2):
                            m = nc.tensor.matmul(ps[7][0:NC, 192 + DH * g:192 + DH * (g + 1)],
                                                 hid[:, 1, c, NC * g:NC * (g + 1)], cw2[:, 1, c, :],
                                                 start=c == 0, stop=c == 1)
                    m.then_inc(ckv_done, 1)
                if n in (XR + 2, XR + 3):
                    e = n - XR - 2
                    pe.wait_ge(ckv_ready, 1)
                    if e:
                        pe.wait_ge(sc_read, 1)
                    b = DH * e
                    for tt in range(TT):
                        for t in range(4):
                            m = nc.tensor.matmul(ps[7][:, (tt * 4 + t) * NC:(tt * 4 + t + 1) * NC],
                                                 qT[b:b + DH, t, tt * P:(tt + 1) * P], kcd[b:b + DH, t // 2, :],
                                                 start=True, stop=True)
                    m.then_inc(sc_done, 1)
                if n == XR + 5:
                    pe.wait_ge(pc_ready, 1)
                    for i in range(2 * TT):
                        tt, g = i // 2, i % 2
                        m = nc.tensor.transpose(ps[7][:, i * P:(i + 1) * P],
                                                pc[:, tt, 4 * g:4 * g + 4, :].rearrange("p h n -> p (h n)"), ident)
                    m.then_inc(pc_turned, 1)
                if n in (XR + 6, XR + 7):
                    tt = n - XR - 6
                    pe.wait_ge(pcT_ready, 1)
                    if tt:
                        pe.wait_ge(oc_read, 1)
                    for g in range(GR):
                        m = nc.tensor.matmul(ps[7][:, g * T:(g + 1) * T], pcT[:, tt * 2 + g, :],
                                             vblk[:, g, :, :].rearrange("p r d -> p (r d)"), start=True, stop=True)
                    m.then_inc(oc_done, 1)
                if XR + 4 <= n < XR + 4 + KT:
                    t = n - XR - 4
                    pe.wait_ge(conv_done, t + 1)
                    if t == 0:
                        pe.wait_ge(bd_loaded, 64)
                        pe.wait_ge(masked, NH)
                    if t >= 2:
                        pe.wait_ge(lru_act, t - 1)
                    for s in range(2):
                        m = nc.tensor.matmul(ps[2 + t % 2][:, s * T:(s + 1) * T], bd[:, t, s, :], xc[:, t, :],
                                             start=True, stop=True)
                    m.then_inc(lru_done, 1)
                if n == GA + 1:
                    pe.wait_ge(normed, NH)
                    pe.wait_ge(oc_read, 2)
                    for k in range(4):
                        for tt in range(TT):
                            m = nc.tensor.transpose(ps[4 + k // 2][:, (k % 2) * T + tt * P:(k % 2) * T + (tt + 1) * P],
                                                    atok[:, tt, k * P:(k + 1) * P], ident)
                    m.then_inc(atok_turned, 1)

            pe.wait_ge(midl_ready, 1)
            for u in range(2):
                split(UPA + u)
                if u:
                    pe.wait_ge(gb_evac, 4)
                for c in range(4):
                    m = feature_tile(UPA + u, 4, c, up_bank(u, c // 2)[:, (c % 2) * T:(c % 2 + 1) * T], midh, midl)
                m.then_inc(panel_done, 1)
            pe.wait_ge(rnnl_ready, 2)
            for u in range(4):
                n = UPR + u
                split(n)
                pe.wait_ge(upa_evac, u + 1)
                for c in range(2):
                    m = feature_tile(n, KT, c, up_bank(u // 2, u % 2)[:, c * T:(c + 1) * T], acth, actl)
                m.then_inc(panel_done, 1)

            def project(n0, e):
                for u in range(4):
                    split(n0 + u)
                    pe.wait_ge(mrgl_ready, 4 * e + u + 1)
                    down(n0 + u, 2 * u, mrgh, mrgl, u == 0, u == 3).then_inc(panel_done, 1)

            project(WO, 0)
            pe.wait_ge(cst_loaded, 16)
            seed(range(3), 1)
            turn_tokens(1)
            seed([3], 1)

            def ffn_up(n, b, norm=None):
                h = [feature_tile(n, KT, c, ps[b][:, c * T:(c + 1) * T], acth, actl, norm) for c in range(2)]
                h[1].then_inc(panel_done, 1)

            split(ML)
            ffn_up(ML, 0, 1)
            with pe.Fori(0, (ML_STEPS - 1) // 3) as i:
                for m in range(3):
                    n = ML + 1 + 2 * m
                    pe.wait_ge(lo_ready, i * 6 + (n + 1))
                    pe.wait_ge(ff_act, i * 3 + (ML_F + m + 1))
                    ffn_up(n, 0)
                    pe.wait_ge(lo_ready, i * 6 + (n + 2))
                    pe.wait_ge(ff_lo, i * 3 + (ML_F + m + 1))
                    down(n + 1, 2 * m, midh, midl, False, False).then_inc(panel_done, 1)
            split(F1 - 1)
            pe.wait_ge(ff_lo, ML_F + ML_STEPS)
            down(F1 - 1, 2 * ((ML_STEPS - 1) % 3), midh, midl, False, True).then_inc(panel_done, 1)

            def swiglu(n0, f0, j):
                seed(range(3), j)
                turn_tokens(j)
                seed([3], j)
                for b in range(2):
                    split(n0 + b)
                    ffn_up(n0 + b, b, None if b else j)
                with pe.Fori(0, (FF_STEPS - 1) // 2) as i:
                    for m in range(2):
                        n = n0 + 2 + 3 * m
                        for b, read in enumerate((ff_act, ff_prod)):
                            pe.wait_ge(lo_ready, i * 6 + (n + b + 1))
                            pe.wait_ge(read, i * 2 + (f0 + m + 1))
                            ffn_up(n + b, b)
                        pe.wait_ge(lo_ready, i * 6 + (n + 3))
                        pe.wait_ge(ff_lo, i * 2 + (f0 + m + 1))
                        down(n + 2, 2 * m, midh, midl, False, False).then_inc(panel_done, 1)
                n = n0 + 3 * FF_STEPS - 1
                split(n)
                pe.wait_ge(ff_lo, f0 + FF_STEPS)
                down(n, 2 * ((FF_STEPS - 1) % 2), midh, midl, False, True).then_inc(panel_done, 1)

            swiglu(F1, F1_F, 2)
            turn_tokens(3)

            def score2(k):
                if k == 0:
                    pe.wait_ge(qa_evac, 1)
                    pe.wait_ge(ka_evac, 1)
                else:
                    pe.wait_ge(masked, NH + k)
                if k == 4:
                    pe.wait_ge(qa_evac, 2)
                    pe.wait_ge(ka_evac, 2)
                if k == NH:
                    pe.wait_ge(qb_ready, 2)
                    pe.wait_ge(kb_ready, 1)
                q, kk, _ = head2(k)
                for tt in range(TT):
                    m = nc.tensor.matmul(ps[2][:, tt * T:(tt + 1) * T], q[:, tt * P:(tt + 1) * P], kk, start=True, stop=True)
                m.then_inc(scored, 1)

            def turn2_(k):
                pe.wait_ge(exped, NH + k + 1)
                pe.wait_ge(probT_ready, NH + k)
                for i in range(4):
                    tt, kt = i // 2, i % 2
                    m = nc.tensor.transpose(ps[3][:, i * P:(i + 1) * P], prob2[:, tt, kt * P:(kt + 1) * P], ident)
                m.then_inc(turned, 1)

            def mix2(k):
                pe.wait_ge(probT_ready, NH + k + 1)
                pe.wait_ge(normed, NH + k)
                if k == 0:
                    pe.wait_ge(va_evac, 1)
                if k == 4:
                    pe.wait_ge(va_evac, 2)
                vt = head2(k)[2]
                for tt in range(TT):
                    for kt in range(TT):
                        c = (2 * tt + kt) * P
                        m = nc.tensor.matmul(ps[4][:, tt * DH:(tt + 1) * DH], probT2[:, c:c + P], vt[kt],
                                             start=kt == 0, stop=kt == 1)
                m.then_inc(mixed, 1)

            def heads2(n, part):
                k = turn2.get((n, part))
                if k is None:
                    return
                if 0 <= k - 2:
                    mix2(k - 2)
                if 0 <= k - 1 < 2 * NH:
                    turn2_(k - 1)
                if k < 2 * NH:
                    score2(k)

            def free_bank2(n):
                last = {QKV2 + 2: (qa_evac, 1), QKV2 + 3: (ka_evac, 1), QKV2 + 4: (va_evac, 1),
                        QKV2 + 5: (qa_evac, 2), QB: (ka_evac, 2), QB + 1: (va_evac, 2),
                        KBVB: (qb_evac, 1), GA2: (qb_evac, 2), GA2 + 1: (kv_evac, 1)}
                if n in last:
                    pe.wait_ge(*last[n])
                elif n >= GA2 + 2:
                    u = n - GA2 - 2
                    pe.wait_ge((ga_evac, gb_evac)[u // 4], 4 + u % 4 + 1)

            def turn_out(tok, br):
                for k in range(4):
                    for tt in range(TT):
                        m = nc.tensor.transpose(ps[TURN_OUT[br][k // 2]][:, (k % 2) * T + tt * P:(k % 2) * T + (tt + 1) * P],
                                                tok[:, tt, k * P:(k + 1) * P], ident)
                m.then_inc(atok_turned, 1)

            for n in range(QKV2, BRA):
                split(n)
                free_bank2(n)
                o = ps[n % 2]
                for c in range(2):
                    if n in (QKV2 + 2, QKV2 + 5):
                        m = token_tile(n, 0, 256, c, o[:, c * T:(c + 1) * T])
                    else:
                        m = feature_tile(n, KT, c, o[:, c * T:(c + 1) * T], acth, actl, 3 if n == QKV2 else None)
                    if c == 1:
                        m.then_inc(panel_done, 1)
                    heads2(n, c)
                if n in (QB + 1, KBVB):
                    u = n - QB - 1
                    pe.wait_ge(qb_evac, u + 1)
                    if u:
                        pe.wait_ge(rope_read, 1)
                    nc.tensor.matmul(ps[7][:, :], cst[:, C_PERM:C_PERM + P],
                                     qbT[:, 2 * u:2 * u + 2, :].rearrange("p a t -> p (a t)"),
                                     start=True, stop=True).then_inc(rope_done, 1)
                if n == GA2:
                    pe.wait_ge(kv_evac, 1)
                    pe.wait_ge(rope_read, 2)
                    for tt in range(TT):
                        nc.tensor.transpose(ps[7][:, T + tt * P:T + (tt + 1) * P], vbT[:, tt * P:(tt + 1) * P], ident)
                    nc.tensor.matmul(ps[7][:, 0:T], cst[:, C_PERM:C_PERM + P], kbT[:, :],
                                     start=True, stop=True).then_inc(rope_done, 1)
                if n == GA2 + 3:
                    pe.wait_ge(normed, 2 * NH)
                    turn_out(atok2, 0)
                if n == GB2 + 3:
                    pe.wait_ge(normed, 3 * NH)
                    pe.wait_ge(midl_ready, 2)
                    turn_out(btok, 1)

            for br, (n0, ah, al) in enumerate(((BRA, midh, midl), (BRB, acth, actl))):
                pe.wait_ge(midl_ready, 2 + br)
                for u in range(2):
                    split(n0 + u)
                    for c in range(4):
                        if br == 0 and u == 1 and c == 0:
                            pe.wait_ge(gb_evac, 8)
                        if br and c % 2 == 0:
                            pe.wait_ge(upa_evac, 4 + 2 * u + c // 2 + 1)
                        m = feature_tile(n0 + u, 4, c, up_bank(u, c // 2)[:, (c % 2) * T:(c % 2 + 1) * T], ah, al)
                    m.then_inc(panel_done, 1)
            project(WO2, 1)
            swiglu(F2, F2_F, 4)

        @block.scalar
        def _(act):
            ac = [0]

            def link(ins):
                ac[0] += 1
                ins.then_inc(act_chain, 1)
                act.wait_ge(act_chain, ac[0])

            def hi(n):
                act.wait_ge(panel_loaded[n % R], 16 * (n // R + 1))
                if n >= R:
                    act.wait_ge(panel_done, n - R + 1)
                nc.scalar.activation(wh[:, n % R, :], raw[:, n % R, :], ACT.Copy).then_inc(hi_ready, 1)

            def hi_in_loop(i, n):
                if n < END:
                    act.wait_ge(panel_loaded[n % R], i * 32 + 16 * (n // R + 1))
                    act.wait_ge(panel_done, i * 6 + (n - R + 1))
                    nc.scalar.activation(wh[:, n % R, :], raw[:, n % R, :], ACT.Copy).then_inc(hi_ready, 1)

            rows = [("norm1_w", V_N1), ("norm2_w", V_N2), ("ffn1_norm_2", V_F1), ("mix_norm_2", V_MX),
                    ("ffn2_norm_2", V_F2), ("conv_b", V_CB), ("lru_b_a", V_BA), ("lru_b_i", V_BI),
                    ("lru_lambda", V_LAM)]
            for name, v in rows:
                act.dma_start(vrow[v:v + KT, :], a[name][0].rearrange("(k p) -> k p", p=P)).then_inc(vec_loaded, 16)
            act.dma_start(vrow[V_CW:V_CW + CW * KT, :],
                          a["conv_w"][0].rearrange("i (k p) -> (i k) p", p=P)).then_inc(vec_loaded, 16)
            for s, name in enumerate(("cmp_pos_k", "cmp_pos_v")):
                act.dma_start(prow[NPOS * s:NPOS * (s + 1), :],
                              a[name][0].rearrange("(j l) d -> j (l d)", l=2)).then_inc(vec_loaded, 16)

            def square_sum(r, weighted=False, apart=False):
                for b in range(2 * TT):
                    tt, cs = half_row(b)
                    if r:
                        act.wait_ge(x_summed, 4 * (r - 1) + b + 1)
                    else:
                        act.wait_ge(x_loaded[tt], 16)
                    junk = sqx if apart else xs
                    nc.scalar.activation(junk[:, tt, cs], xt[:, tt, cs], ACT.Square, accum_out=ssq[:, b:b + 1]).then_inc(ssq_ready, 1)
                    if weighted:
                        act.wait_ge(y_ready, b + 1)
                        nc.scalar.activation(sqy[:, tt, cs], xs[:, tt, cs], ACT.Square,
                                             accum_out=wsq[:, b:b + 1]).then_inc(wsq_ready, 1)

            def norm_hi(j, v):
                if j == 0:
                    act.wait_ge(vec_ready, 1)
                for k in range(KT):
                    act.wait_ge(xs_turned, 4 * j + k // 2 + 1)
                    nc.scalar.activation(acth[:, k, :], ps[TURNED[k // 2]][:, (k % 2) * T:(k % 2 + 1) * T],
                                         ACT.Copy, scale=vcol(v, k)).then_inc(acth_ready, 1)

            square_sum(0)
            hi(0)
            norm_hi(0, V_N1)
            hi(1)
            act.wait_ge(abs_lam, 1)
            nc.scalar.activation(lru[:, 1, :], lru[:, 0, :], ACT.Exp, scale=-1.0).then_inc(exp_lam, 1)
            act.wait_ge(small_loaded, 64)
            nc.scalar.activation(gwh[:, :, :], gwr[:, :, :], ACT.Copy).then_inc(gw_hi, 1)

            def done(n):
                act.wait_ge(panel_done, n + 1)

            def keys_values(b, kd, e, ev):
                for g in range(GR):
                    for half in range(2):
                        nc.scalar.activation(kd[DH * half:DH * (half + 1), g, :], b[DH * g:DH * (g + 1), 0:T], ACT.Copy)
                nc.scalar.activation(vT[:, e, :], b[:, T:2 * T], ACT.Copy).then_inc(ev, 1)

            def head_exp(k):
                act.wait_ge(masked, k + 1)
                o = k % 3
                for i, (c0, c1) in enumerate(((0, P), (P, 2 * P), (2 * P, 4 * P), (4 * P, 6 * P))):
                    m = nc.scalar.activation(prob[:, c0:c1], prob[:, c0:c1], ACT.Exp, scale=-1.0,
                                             bias=nmax[:, o, i:i + 1], accum_out=sums[:, o, i:i + 1])
                m.then_inc(exped, 1)

            def head_copy(k):
                act.wait_ge(turned, k + 1)
                if k:
                    act.wait_ge(mixed, k)
                nc.scalar.activation(probT[:, :], acc4[:, 2:4, :].rearrange("p b c -> p (b c)")[:, 0:768],
                                     ACT.Copy).then_inc(probT_ready, 1)

            for n in range(ML):
                if UPR < n <= UPR + 4:
                    u = n - UPR - 1
                    act.wait_ge(mrg_sum, u + 1)
                    nc.scalar.activation(mrgh[:, 2 * u:2 * u + 2, :], sga[:, 2 * u:2 * u + 2, :], ACT.Copy,
                                         scale=0.5).then_inc(mrgh_ready, 1)
                hi(n + 2)
                if n in (Q + 1, Q + 2):
                    u = n - Q - 1
                    done(n - 1)
                    nc.scalar.activation(qT[:, 2 * u:2 * u + 2, :].rearrange("p a t -> p (a t)"), ps[u][:, :], ACT.Copy,
                                         scale=QSCALE).then_inc(q_evac, 1)
                if n == KCVC + 1:
                    act.wait_ge(flat_ready, 2)
                    nc.scalar.activation(flath, flat[:, :, :].rearrange("p s c -> p (s c)"), ACT.Copy).then_inc(flath_ready, 1)
                if n == KSVS + 1:
                    done(KSVS)
                    keys_values(ps[KSVS % 2], ksd, 0, ks_evac)
                if n == KWVW + 1:
                    done(KWVW)
                    keys_values(ps[KWVW % 2], kwd, 1, kw_evac)
                    act.wait_ge(gates_done, 1)
                    nc.scalar.activation(gatT[:, :], ps[5][0:24, 0:T], ACT.Tanh, scale=0.5).then_inc(gates_tanh, 1)
                if n == CK + 1:
                    act.wait_ge(v_turned, 1)
                    nc.scalar.activation(vsw[:, :, :, :].rearrange("p t e c -> p (t e c)"), ps[6][:, :],
                                         ACT.Copy).then_inc(v_ready, 1)
                k = n - CK - 1
                if 0 <= k - 1 < NH:
                    head_copy(k - 1)
                if 0 <= k < NH:
                    head_exp(k)
                if n == XR:
                    done(XR - 1)
                    nc.scalar.activation(hidt[:, :], ps[7][0:2 * NC, :], ACT.Gelu_apprx_tanh).then_inc(hidt_ready, 1)
                if XR < n <= XR + 4:
                    u = n - XR - 1
                    done(n - 1)
                    nc.scalar.activation(xrp[:, 2 * u:2 * u + 2, CW - 1:CW - 1 + T],
                                         ps[(n - 1) % 2][:, :].rearrange("p (a t) -> p a t", a=2), ACT.Copy).then_inc(xr_evac, 1)
                if n == XR + 5:
                    act.wait_ge(sc_shifted, 1)
                    nc.scalar.activation(pc[:, :, :, 0:NC], pc[:, :, :, 0:NC], ACT.Exp, scale=-1.0).then_inc(sc_exped, 1)
                if n == XR + 6:
                    act.wait_ge(pc_turned, 1)
                    nc.scalar.activation(pcT[:, :, :].rearrange("p a q -> p (a q)"), ps[7][:, :], ACT.Copy).then_inc(pcT_ready, 1)
                if GRP < n <= GRP + 4:
                    u = n - GRP - 1
                    done(n - 1)
                    nc.scalar.activation(gru[:, 2 * u:2 * u + 2, :].rearrange("p a t -> p (a t)"), ps[(n - 1) % 2][:, :],
                                         ACT.Copy).then_inc(gr_evac, 1)
                for g0, sg, ev in ((GA, sga, ga_evac), (GB, sgb, gb_evac)):
                    if g0 < n <= g0 + 4:
                        u = n - g0 - 1
                        done(n - 1)
                        if g0 == GB and u == 0:
                            act.wait_ge(lru_done, KT)
                        nc.scalar.activation(sg[:, 2 * u:2 * u + 2, :].rearrange("p a t -> p (a t)"), ps[(n - 1) % 2][:, :],
                                             ACT.Tanh, scale=0.5).then_inc(ev, 1)
                if n == GRP + 5:
                    act.wait_ge(gr_evac, 4)
                    nc.scalar.activation(gru[:, :, :], gru[:, :, :], ACT.Gelu_apprx_tanh).then_inc(gr_gelu, 1)
                t = n - XR - 5
                if 0 <= t < KT:
                    if t == 0:
                        act.wait_ge(lru_consts, 1)
                    act.wait_ge(lru_done, t + 1)
                    b = ps[2 + t % 2]
                    nc.scalar.activation(igx[:, t, :], b[:, T:2 * T], ACT.Tanh, scale=0.5, bias=lru[:, 9, t:t + 1])
                    if t:
                        act.wait_ge(lru_act, t)
                    link(nc.scalar.activation(thr[:, :], b[:, 0:T], ACT.Tanh, scale=0.5, bias=lru[:, 8, t:t + 1]))
                    nc.scalar.activation(abuf[:, t, :], thr[:, :], ACT.Exp, scale=lru[:, 6, t:t + 1], bias=lru[:, 6, t:t + 1])
                    if t:
                        act.wait_ge(lru_q, t)
                    nc.scalar.activation(nth[:, :], thr[:, :], ACT.Tanh, scale=lru[:, 7, t:t + 1],
                                         bias=lru[:, 7, t:t + 1]).then_inc(lru_act, 1)
                if n in (GA + 1, GB + 1):
                    hf = (n - GA - 1) // 4
                    act.wait_ge(lru_q, 4 * hf + 4)
                    q2 = xrp[:, 4 * hf:4 * hf + 4, 0:T]
                    nc.scalar.activation(q2, q2, ACT.Sqrt).then_inc(root_ready, 1)
                if n == GA + 2:
                    act.wait_ge(atok_turned, 1)
                    nc.scalar.activation(midh[:, 0:4, :].rearrange("p k t -> p (k t)"),
                                         acc4[:, 2:4, :].rearrange("p b c -> p (b c)"), ACT.Copy).then_inc(midh_ready, 1)
                if n == UPA:
                    done(UPA - 1)
                    for hf in range(2):
                        act.wait_ge(rnn_ready, hf + 1)
                        nc.scalar.activation(acth[:, 4 * hf:4 * hf + 4, :], gru[:, 4 * hf:4 * hf + 4, :],
                                             ACT.Copy).then_inc(rnnh_ready, 1)

            square_sum(1)
            norm_hi(1, V_N2)

            def hidden_hi(s):
                return nc.scalar.activation(midh[:, 2 * s:2 * s + 2, :].rearrange("p a t -> p (a t)"), ffs, ACT.Copy)

            hi(ML + 2)
            done(ML)
            nc.scalar.activation(ffa, ps[0][:, :], ACT.Relu).then_inc(ff_act, 1)
            hi(ML + 3)
            act.wait_ge(ff_prod, ML_F + 1)
            hidden_hi(0).then_inc(ff_hi, 1)
            with act.Fori(0, (ML_STEPS - 1) // 3) as i:
                for m in range(3):
                    n = ML + 1 + 2 * m
                    act.wait_ge(panel_done, i * 6 + (n + 1))
                    nc.scalar.activation(ffa, ps[0][:, :], ACT.Relu).then_inc(ff_act, 1)
                    hi_in_loop(i, n + 3)
                    act.wait_ge(ff_prod, i * 3 + (ML_F + m + 2))
                    hidden_hi((m + 1) % 3).then_inc(ff_hi, 1)
                    hi_in_loop(i, n + 4)

            def swiglu(n0, f0):
                hi(n0 + 2)
                done(n0)
                nc.scalar.activation(ffa, ps[0][:, :], ACT.Silu).then_inc(ff_act, 1)
                hi(n0 + 3)
                hi(n0 + 4)
                act.wait_ge(ff_prod, f0 + 1)
                hidden_hi(0).then_inc(ff_hi, 1)

                def two_steps(i, last):
                    for m in range(2):
                        n = n0 + 2 + 3 * m
                        act.wait_ge(panel_done, i * 6 + (n + 1))
                        nc.scalar.activation(ffa, ps[0][:, :], ACT.Silu).then_inc(ff_act, 1)
                        hi_in_loop(i, n + 3)
                        act.wait_ge(ff_prod, i * 2 + (f0 + m + 2))
                        hidden_hi((m + 1) % 2).then_inc(ff_hi, 1)
                        if not (last and m and n0 == F2):
                            hi_in_loop(i, n + 4)
                            hi_in_loop(i, n + 5)

                with act.Fori(0, (FF_STEPS - 1) // 2 - 1) as i:
                    two_steps(i, False)
                two_steps((FF_STEPS - 1) // 2 - 1, True)

            square_sum(2, weighted=True, apart=True)
            norm_hi(2, V_F1)
            swiglu(F1, F1_F)
            square_sum(3)
            norm_hi(3, V_MX)

            def copy2(k):
                act.wait_ge(turned, NH + k + 1)
                act.wait_ge(mixed, NH + k)
                nc.scalar.activation(probT2[:, :], ps[3][:, :], ACT.Copy).then_inc(probT_ready, 1)

            def exp2(k):
                act.wait_ge(masked, NH + k + 1)
                o = k % 3
                if k >= NH:
                    h = k - NH
                    for tt in range(TT):
                        nc.scalar.activation(esink[:, o, tt:tt + 1], small[:, h:h + 1], ACT.Exp, scale=-1.0,
                                             bias=nmax[:, o, tt:tt + 1])
                for tt in range(TT):
                    m = nc.scalar.activation(prob2[:, tt, :], prob2[:, tt, :], ACT.Exp, scale=-1.0,
                                             bias=nmax[:, o, tt:tt + 1], accum_out=sums[:, o, tt:tt + 1])
                m.then_inc(exped, 1)

            def heads2(n, part):
                k = turn2.get((n, part))
                if k is None:
                    return
                if 0 <= k - 1 < 2 * NH:
                    copy2(k - 1)
                if k < 2 * NH:
                    exp2(k)

            for n in range(QKV2, F2):
                hi(n + 2)
                b = ps[(n - 1) % 2][:, :]
                if n - 1 in (QKV2, QKV2 + 3, QB, QB + 1):
                    done(n - 1)
                    dst, ev, u = ((qaT, qa_evac, (n - 1 - QKV2) // 3) if n - 1 < QB else (qbT, qb_evac, n - 1 - QB))
                    nc.scalar.activation(dst[:, 2 * u:2 * u + 2, :].rearrange("p a t -> p (a t)"), b, ACT.Copy,
                                         scale=QSCALE).then_inc(ev, 1)
                if n - 1 in (QKV2 + 2, QKV2 + 5):
                    u = (n - 1 - QKV2) // 3
                    done(n - 1)
                    nc.scalar.activation(va[:, :, 256 * u:256 * (u + 1)], b.rearrange("p (t c) -> p t c", t=TT),
                                         ACT.Copy).then_inc(va_evac, 1)
                if n - 1 == KBVB:
                    done(n - 1)
                    nc.scalar.activation(kbT[:, :], b[:, 0:T], ACT.Copy)
                    nc.scalar.activation(vbT[:, :], b[:, T:2 * T], ACT.Copy).then_inc(kv_evac, 1)
                heads2(n - 1, 1)
                heads2(n, 0)
                for g0, sg, ev in ((GA2, sga2, ga_evac), (GB2, sgb2, gb_evac)):
                    if g0 < n <= g0 + 4:
                        u = n - g0 - 1
                        done(n - 1)
                        if g0 == GA2 and u == 0:
                            act.wait_ge(nab_ready, 2)
                        nc.scalar.activation(sg[:, 2 * u:2 * u + 2, :].rearrange("p a t -> p (a t)"), b,
                                             ACT.Tanh, scale=0.5).then_inc(ev, 1)
                if n in (GA2 + 4, GB2 + 4):
                    br = n == GB2 + 4
                    act.wait_ge(atok_turned, 2 + br)
                    if br:
                        done(BRA - 1)
                    dst = acth if br else midh
                    for i in range(2):
                        m = nc.scalar.activation(dst[:, 2 * i:2 * i + 2, :].rearrange("p k t -> p (k t)"),
                                                 ps[TURN_OUT[br][i]][:, :], ACT.Copy)
                    m.then_inc(midh_ready, 1)
                if n in (BRB + 1, BRB + 2):
                    for u in range(2 * (n - BRB - 1), 2 * (n - BRB)):
                        act.wait_ge(mrg_sum, 4 + u + 1)
                        nc.scalar.activation(mrgh[:, 2 * u:2 * u + 2, :], sga2[:, 2 * u:2 * u + 2, :], ACT.Copy,
                                             scale=0.5).then_inc(mrgh_ready, 1)

            square_sum(4)
            norm_hi(4, V_F2)
            swiglu(F2, F2_F)
            square_sum(5, apart=True)

        @block.vector
        def _(dve):
            dc = [0]

            def link(ins):
                dc[0] += 1
                ins.then_inc(dve_chain, 1)
                dve.wait_ge(dve_chain, dc[0])

            def lo(n):
                dve.wait_ge(hi_ready, n + 1)
                nc.vector.tensor_tensor(wl[:, n % R, :], raw[:, n % R, :], wh[:, n % R, :].bitcast(F32),
                                        ALU.subtract).then_inc(lo_ready, 1)

            def lo_in_loop(i, n):
                dve.wait_ge(hi_ready, i * 6 + (n + 1))
                nc.vector.tensor_tensor(wl[:, n % R, :], raw[:, n % R, :], wh[:, n % R, :].bitcast(F32),
                                        ALU.subtract).then_inc(lo_ready, 1)

            def normalise(r, weighted=False):
                for b in range(2 * TT):
                    tt, cs = half_row(b)
                    root = rstd[:, tt:tt + 1]
                    if b % 2 == 0:
                        dve.wait_ge(rstd_ready, TT * r + tt + 1)
                        if weighted:
                            dve.wait_ge(wrstd_ready, tt + 1)
                    if weighted:
                        m = nc.vector.tensor_scalar(xs[:, tt, cs], xs[:, tt, cs], root, wrstd[:, tt:tt + 1], ALU.mult, ALU.mult)
                    else:
                        m = nc.vector.tensor_scalar(xs[:, tt, cs], xt[:, tt, cs], root, None, ALU.mult)
                    m.then_inc(xs_ready, 1)

            def norm_lo(j, v):
                for k in range(KT):
                    dve.wait_ge(acth_ready, KT * j + k // 2 * 2 + 2)
                    nc.vector.scalar_tensor_tensor(actl[:, k, :], ps[TURNED[k // 2]][:, (k % 2) * T:(k % 2 + 1) * T],
                                                   vcol(v, k), acth[:, k, :].bitcast(F32), ALU.mult,
                                                   ALU.subtract).then_inc(actl_ready, 1)

            def done(n):
                dve.wait_ge(panel_done, n + 1)

            normalise(0)
            dve.wait_ge(vec_turned, 1)
            nc.vector.tensor_copy(vec[:, :], ps[2][:, 0:V_ALL]).then_inc(vec_ready, 1)
            dve.wait_ge(vec_ready, 1)
            lam = vec[:, V_LAM:V_LAM + KT]
            nc.vector.scalar_tensor_tensor(lru[:, 0, :], lam, -1.0, lam, ALU.mult, ALU.max).then_inc(abs_lam, 1)
            lo(0)
            norm_lo(0, V_N1)
            lo(1)
            dve.wait_ge(gw_hi, 1)
            nc.vector.tensor_tensor(gwl[:, :, :], gwr[:, :, :], gwh[:, :, :].bitcast(F32), ALU.subtract).then_inc(gw_lo, 1)

            def lru_constants():
                dve.wait_ge(exp_lam, 1)
                e, den, s, s2, p = (lru[:, i, :] for i in (1, 2, 3, 4, 5))
                link(nc.vector.tensor_scalar(den, e, 2.0, None, ALU.add))
                link(nc.vector.reciprocal(den, den))
                link(nc.vector.tensor_tensor(s, e, den, ALU.mult))
                link(nc.vector.tensor_tensor(s2, s, s, ALU.mult))
                link(nc.vector.tensor_scalar(p, s2, 1.0 / 15, None, ALU.mult))
                for q in (13, 11, 9, 7, 5, 3):
                    link(nc.vector.scalar_tensor_tensor(p, p, 1.0 / q, s2, ALU.add, ALU.mult))
                link(nc.vector.scalar_tensor_tensor(p, p, 1.0, s, ALU.add, ALU.mult))
                link(nc.vector.tensor_scalar(lru[:, 10, :], lam, -1.0, 0.0, ALU.mult, ALU.max))
                link(nc.vector.scalar_tensor_tensor(lru[:, 11, :], p, 2.0, lru[:, 10, :], ALU.mult, ALU.add))
                nc.vector.tensor_scalar(lru[:, 6, :], lru[:, 11, :], -0.5 * 8.0, None, ALU.mult)
                nc.vector.tensor_scalar(lru[:, 7, :], lru[:, 11, :], 0.5 * 8.0, None, ALU.mult)
                nc.vector.tensor_scalar(lru[:, 8, :], vec[:, V_BA:V_BA + KT], 0.5, None, ALU.mult)
                nc.vector.tensor_scalar(lru[:, 9, :], vec[:, V_BI:V_BI + KT], 0.5, None, ALU.mult).then_inc(lru_consts, 1)

            def masked_min(out_, scores, mask, o, i, start=3e38):
                return nc.vector.tensor_tensor_reduce(out=out_, in0=scores, in1=mask, scale=1.0, scalar=start,
                                                      op0=ALU.add, op1=ALU.min, accum_out=nmax[:, o, i:i + 1])

            def head_mask(k):
                dve.wait_ge(scored, k + 1)
                if k:
                    dve.wait_ge(turned, k)
                o = k % 3
                for e in range(2):
                    masked_min(prob[:, e * P:(e + 1) * P], ps[2][:, e * P:(e + 1) * P], cst[:, C_CAUS:C_CAUS + P], o, e)
                for e in range(2):
                    m = masked_min(prob[:, (1 + e) * T:(2 + e) * T], ps[3][:, e * T:(e + 1) * T],
                                   cst[:, C_ZERO:C_ZERO + T], o, 2 + e)
                m.then_inc(masked, 1)

            def head_norm(k):
                dve.wait_ge(mixed, k + 1)
                o = k % 3
                link(nc.vector.reciprocal(coef[:, o, :], sums[:, o, :]))
                c4 = coef[:, o, :].rearrange("p (t e) -> p t e", e=2)
                link(nc.vector.tensor_tensor(c4, c4, gates[:, :, k, 1:3], ALU.mult))
                for e in range(2):
                    for tt in range(TT):
                        i = 2 * tt + e
                        at = atok[:, tt, DH * k:DH * (k + 1)]
                        m = nc.vector.scalar_tensor_tensor(at, ps[6][:, i * DH:(i + 1) * DH], coef[:, o, i:i + 1], at,
                                                           ALU.mult, ALU.add)
                        if e == 0:
                            link(m)
                m.then_inc(normed, 1)
                dve.wait_ge(normed, k + 1)

            def conv(t):
                dve.wait_ge(xr_evac, t // 2 + 1)
                link(nc.vector.tensor_scalar(xc[:, t, :], xrp[:, t, 0:T], vcol(V_CW, t), vcol(V_CB, t), ALU.mult, ALU.add))
                for i in range(1, CW):
                    m = nc.vector.scalar_tensor_tensor(xc[:, t, :], xrp[:, t, i:i + T], vcol(V_CW + KT * i, t), xc[:, t, :],
                                                       ALU.mult, ALU.add)
                    if i < CW - 1:
                        link(m)
                m.then_inc(conv_done, 1)

            def recur(hf):
                t0 = 4 * hf
                ts = slice(t0, t0 + 4)
                dve.wait_ge(root_ready, hf + 1)
                dve.wait_ge(gr_gelu, 1)
                link(nc.vector.scalar_tensor_tensor(igx[:, ts, :], igx[:, ts, :], 1.0, xc[:, ts, :], ALU.add, ALU.mult))
                link(nc.vector.tensor_tensor(igx[:, ts, :], xrp[:, ts, 0:T], igx[:, ts, :], ALU.mult))
                for t in range(t0, t0 + 4):
                    m = nc.vector.tensor_tensor_scan(xc[:, t, :], abuf[:, t, :], igx[:, t, :], 0.0, ALU.mult, ALU.add)
                link(m)
                nc.vector.scalar_tensor_tensor(gru[:, ts, :], xc[:, ts, :], 0.5, gru[:, ts, :], ALU.mult,
                                               ALU.mult).then_inc(rnn_ready, 1)

            def gate_a(sg, u, bank):
                s = sg[:, 2 * u:2 * u + 2, :].rearrange("p a t -> p (a t)")
                nc.vector.scalar_tensor_tensor(s, s, 1.0, bank, ALU.add, ALU.mult).then_inc(upa_evac, 1)

            def gate_b(sa, sg, u, bank, e):
                dst = sa[:, 2 * u:2 * u + 2, :].rearrange("p a t -> p (a t)")
                s = sg[:, 2 * u:2 * u + 2, :].rearrange("p a t -> p (a t)")
                nc.vector.scalar_tensor_tensor(s, s, 1.0, bank, ALU.add, ALU.mult).then_inc(upr_evac, 1)
                dve.wait_ge(upr_evac, 4 * e + u + 1)
                nc.vector.tensor_tensor(dst, dst, s, ALU.add).then_inc(mrg_sum, 1)

            def merge_lo(sa, u, e):
                dst = sa[:, 2 * u:2 * u + 2, :]
                dve.wait_ge(mrgh_ready, 4 * e + u + 1)
                nc.vector.scalar_tensor_tensor(mrgl[:, 2 * u:2 * u + 2, :], dst, 0.5, mrgh[:, 2 * u:2 * u + 2, :].bitcast(F32),
                                               ALU.mult, ALU.subtract).then_inc(mrgl_ready, 1)

            dve.wait_ge(cst_loaded, 16)
            for n in range(ML):
                if n == KCVC + 1:
                    done(KCVC)
                    for s in range(2):
                        for l in range(2):
                            for g in range(GR):
                                first = ps[KCVC % 2][DH * g:DH * (g + 1), s * T + l:s * T + l + 1]
                                win = bass.AP(first.tensor, first.offset, [first.ap[0], [2, NPOS], [16, NC]])
                                dst = flat[DH * l:DH * (l + 1), s, :].rearrange("p (j g n) -> p j g n", g=GR, n=NC)[:, :, g, :]
                                pos = vec[DH * l:DH * (l + 1), V_PK + NPOS * s:V_PK + NPOS * (s + 1)]
                                m = nc.vector.tensor_tensor(dst, win, pos.unsqueeze(2).broadcast_to([DH, NPOS, NC]), ALU.add)
                        m.then_inc(flat_ready, 1)
                k = n - CK - 1
                if 0 <= k < NH:
                    head_mask(k)
                if n in (UPA + 1, UPA + 2):
                    done(n - 1)
                    for c in range(2):
                        gate_a(sga, 2 * (n - UPA - 1) + c, up_bank(n - UPA - 1, c)[:, :])
                if UPR < n <= UPR + 4:
                    u = n - UPR - 1
                    done(n - 1)
                    if u == 0:
                        dve.wait_ge(upa_evac, 4)
                    gate_b(sga, sgb, u, up_bank(u // 2, u % 2)[:, :], 0)
                    merge_lo(sga, u, 0)
                lo(n + 2)
                if n == 1:
                    lru_constants()
                if n == KCVC + 1:
                    dve.wait_ge(flath_ready, 1)
                    nc.vector.tensor_tensor(flatl, flat[:, :, :].rearrange("p s c -> p (s c)"), flath.bitcast(F32),
                                            ALU.subtract).then_inc(flatl_ready, 1)
                if n == KWVW:
                    link(nc.vector.memset(pc[:, :, :, :], 0.0))
                    link(nc.vector.memset(vblk[:, :, :, :], 0.0))
                if n == CK + 1:
                    dve.wait_ge(gates_turned, 1)
                    nc.vector.tensor_scalar(gates[:, :, :, :].rearrange("p t h b -> p (t h b)"), ps[5][:, 0:48], 0.5, 0.5,
                                            ALU.mult, ALU.add).then_inc(gates_ready, 1)
                    dve.wait_ge(gates_ready, 1)
                    dve.wait_ge(padded, 1)
                if 0 <= k - 2 < NH:
                    head_norm(k - 2)
                if n == XR + 1:
                    dve.wait_ge(hid_turned, 1)
                    nc.vector.tensor_copy(hid[:, :, :, :].rearrange("p s c n -> p (s c n)"),
                                          ps[7][:, 0:8 * NC]).then_inc(hid_ready, 1)
                if n == XR + 2:
                    dve.wait_ge(ckv_done, 1)
                    for half in range(2):
                        nc.vector.tensor_copy(kcd[DH * half:DH * (half + 1), :, :].rearrange("p g n -> p (g n)"),
                                              ps[7][0:DH, 128:128 + 2 * NC])
                    for r in range(4):
                        m = nc.vector.tensor_copy(vblk[GS * r:GS * r + NC, :, r, :],
                                                  ps[7][0:NC, 192:192 + 2 * DH].rearrange("p (g d) -> p g d", g=GR))
                    m.then_inc(ckv_ready, 1)
                if n in (XR + 3, XR + 4):
                    e = n - XR - 3
                    dve.wait_ge(sc_done, e + 1)
                    cm = cst[:, C_CMP:C_CMP + TT * NC].rearrange("p (t n) -> p t n", n=NC)
                    nc.vector.tensor_tensor(pc[:, :, e::2, 0:NC], ps[7][:, 0:8 * NC].rearrange("p (t h n) -> p t h n", t=TT, h=4),
                                            cm.unsqueeze(2).broadcast_to([P, TT, 4, NC]), ALU.add).then_inc(sc_read, 1)
                pcv = pc[:, :, :, :].rearrange("p t h n -> p (t h) n")[:, :, 0:NC]

                def over_n(v):
                    return v.unsqueeze(2).broadcast_to([P, TT * NH, NC])

                if n == XR + 4:
                    dve.wait_ge(sc_read, 2)
                    link(nc.vector.tensor_reduce(small[:, 8:24], pcv, AX_X, ALU.min))
                    nc.vector.tensor_tensor(pcv, pcv, over_n(small[:, 8:24]), ALU.subtract).then_inc(sc_shifted, 1)
                if n == XR + 5:
                    dve.wait_ge(sc_exped, 1)
                    c16 = small[:, 40:56]
                    cth = c16.rearrange("p (t h) -> p t h", t=TT)
                    link(nc.vector.tensor_reduce(small[:, 24:40], pcv, AX_X, ALU.add))
                    link(nc.vector.reciprocal(c16, small[:, 24:40]))
                    link(nc.vector.tensor_tensor(cth, cth, gates[:, :, :, 0], ALU.mult))
                    link(nc.vector.tensor_tensor(cth, cth, cst[:, C_VALID:C_VALID + TT].unsqueeze(2).broadcast_to([P, TT, NH]),
                                                 ALU.mult))
                    nc.vector.tensor_tensor(pcv, pcv, over_n(c16), ALU.mult).then_inc(pc_ready, 1)
                if n in (XR + 7, XR + 8):
                    tt = n - XR - 7
                    dve.wait_ge(oc_done, tt + 1)
                    nc.vector.tensor_tensor(atok[:, tt, :], atok[:, tt, :], ps[7][:, :], ALU.add).then_inc(oc_read, 1)
                    dve.wait_ge(oc_read, tt + 1)
                t = n - XR - 3
                if 0 <= t < KT:
                    conv(t)
                t = n - XR - 5
                if 0 <= t < KT:
                    dve.wait_ge(lru_act, t + 1)
                    q2 = xrp[:, t, 0:T]
                    link(nc.vector.tensor_tensor(q2, abuf[:, t, :], abuf[:, t, :], ALU.mult))
                    nc.vector.scalar_tensor_tensor(q2, q2, 1.0, nth[:, :], ALU.add, ALU.mult).then_inc(lru_q, 1)
                if n == GA + 2:
                    dve.wait_ge(midh_ready, 1)
                    nc.vector.tensor_tensor(midl[:, 0:4, :].rearrange("p k t -> p (k t)"),
                                            acc4[:, 2:4, :].rearrange("p b c -> p (b c)"),
                                            midh[:, 0:4, :].rearrange("p k t -> p (k t)").bitcast(F32),
                                            ALU.subtract).then_inc(midl_ready, 1)
                if n in (GA + 2, GB + 2):
                    recur((n - GA - 2) // 4)
                if n == UPA:
                    for hf in range(2):
                        ts = slice(4 * hf, 4 * hf + 4)
                        dve.wait_ge(rnnh_ready, hf + 1)
                        nc.vector.tensor_tensor(actl[:, ts, :], gru[:, ts, :], acth[:, ts, :].bitcast(F32),
                                                ALU.subtract).then_inc(rnnl_ready, 1)

            yc = [0]

            def residual(r, last, weighted=False):
                for b in range(2 * TT):
                    tt, cs = half_row(b)
                    if b < 3:
                        dve.wait_ge(bank_done, 3 * (r - 1) + b + 1)
                    else:
                        done(last)
                    nc.vector.tensor_tensor(xt[:, tt, cs], xt[:, tt, cs], acc4[:, b, :], ALU.add).then_inc(x_summed, 1)
                    if weighted:
                        if b == 0:
                            yc[0] += 1
                            dve.wait_ge(fnb_loaded, 16 * yc[0])
                        dve.wait_ge(x_summed, 4 * (r - 1) + b + 1)
                        nc.vector.tensor_tensor(xs[:, tt, cs], xt[:, tt, cs], fnb[:, cs], ALU.mult).then_inc(y_ready, 1)

            def hidden_lo(s):
                return nc.vector.tensor_tensor(midl[:, 2 * s:2 * s + 2, :].rearrange("p a t -> p (a t)"), ffs,
                                               midh[:, 2 * s:2 * s + 2, :].rearrange("p a t -> p (a t)").bitcast(F32), ALU.subtract)

            residual(1, ML - 1)
            normalise(1)
            norm_lo(1, V_N2)
            lo(ML + 2)
            dve.wait_ge(ff_act, ML_F + 1)
            nc.vector.tensor_tensor(ffs, ffa, ffa, ALU.mult).then_inc(ff_prod, 1)
            lo(ML + 3)
            dve.wait_ge(ff_hi, ML_F + 1)
            hidden_lo(0).then_inc(ff_lo, 1)
            with dve.Fori(0, (ML_STEPS - 1) // 3) as i:
                for m in range(3):
                    n = ML + 1 + 2 * m
                    dve.wait_ge(ff_act, i * 3 + (ML_F + m + 2))
                    dve.wait_ge(ff_lo, i * 3 + (ML_F + m + 1))
                    nc.vector.tensor_tensor(ffs, ffa, ffa, ALU.mult).then_inc(ff_prod, 1)
                    lo_in_loop(i, n + 3)
                    dve.wait_ge(ff_hi, i * 3 + (ML_F + m + 2))
                    hidden_lo((m + 1) % 3).then_inc(ff_lo, 1)
                    lo_in_loop(i, n + 4)

            def swiglu(n0, f0):
                def product(at_panel, at_act, at_lo):
                    dve.wait_ge(panel_done, at_panel)
                    dve.wait_ge(ff_act, at_act)
                    dve.wait_ge(ff_lo, at_lo)
                    nc.vector.scalar_tensor_tensor(ffs, ps[1][:, :], 0.5, ffa, ALU.mult, ALU.mult).then_inc(ff_prod, 1)

                lo(n0 + 2)
                lo(n0 + 3)
                product(n0 + 2, f0 + 1, f0)
                lo(n0 + 4)
                dve.wait_ge(ff_hi, f0 + 1)
                hidden_lo(0).then_inc(ff_lo, 1)

                def two_steps(i, last):
                    for m in range(2):
                        n = n0 + 2 + 3 * m
                        lo_in_loop(i, n + 3)
                        product(i * 6 + (n + 2), i * 2 + (f0 + m + 2), i * 2 + (f0 + m + 1))
                        dve.wait_ge(ff_hi, i * 2 + (f0 + m + 2))
                        hidden_lo((m + 1) % 2).then_inc(ff_lo, 1)
                        if not (last and m and n0 == F2):
                            lo_in_loop(i, n + 4)
                            lo_in_loop(i, n + 5)

                with dve.Fori(0, (FF_STEPS - 1) // 2 - 1) as i:
                    two_steps(i, False)
                two_steps((FF_STEPS - 1) // 2 - 1, True)

            residual(2, F1 - 1, weighted=True)
            normalise(2, weighted=True)
            norm_lo(2, V_F1)
            for tt in range(TT):
                nc.vector.scalar_tensor_tensor(xt[:, tt, :], xt[:, tt, :], rstd[:, tt:tt + 1], fnb[:, :], ALU.mult,
                                               ALU.mult).then_inc(stream_ready, 1)
            swiglu(F1, F1_F)
            residual(3, QKV2 - 1)
            normalise(3)
            norm_lo(3, V_MX)

            def mask2(k):
                dve.wait_ge(scored, NH + k + 1)
                dve.wait_ge(turned, NH + k)
                o = k % 3
                if k == 0:
                    dve.wait_ge(nab_ready, 2)
                if k == NH:
                    dve.wait_ge(sink_ready, 1)
                for tt in range(TT):
                    if k < NH:
                        m = masked_min(prob2[:, tt, :], ps[2][:, tt * T:(tt + 1) * T], nab[:, tt, k, :], o, tt)
                    else:
                        c = (C_ZERO, C_TRIU)[tt]
                        m = masked_min(prob2[:, tt, :], ps[2][:, tt * T:(tt + 1) * T], cst[:, c:c + T], o, tt,
                                       small[:, k - NH:k - NH + 1])
                m.then_inc(masked, 1)

            def norm2(k):
                dve.wait_ge(mixed, NH + k + 1)
                o = k % 3
                h = k % NH
                c = coef[:, o, 0:TT]
                if k < NH:
                    link(nc.vector.reciprocal(c, sums[:, o, 0:TT]))
                else:
                    link(nc.vector.tensor_tensor(c, sums[:, o, 0:TT], esink[:, o, :], ALU.add))
                    link(nc.vector.reciprocal(c, c))
                tok = atok2 if k < NH else btok
                for tt in range(TT):
                    m = nc.vector.tensor_scalar(tok[:, tt, DH * h:DH * (h + 1)], ps[4][:, tt * DH:(tt + 1) * DH],
                                                coef[:, o, tt:tt + 1], None, ALU.mult)
                m.then_inc(normed, 1)

            def heads2(n, part):
                k = turn2.get((n, part))
                if k is None:
                    return
                if k < 2 * NH:
                    mask2(k)
                if 0 <= k - 2:
                    norm2(k - 2)

            def rope(x, swapped, r1, r2, width, done_count):
                dve.wait_ge(rope_done, done_count)
                reps = width // T

                def table(c):
                    return cst[:, c:c + T].unsqueeze(1).broadcast_to([P, reps, T])

                r1, r2, x, swapped = (v.rearrange("p (a t) -> p a t", t=T) for v in (r1, r2, x, swapped))
                nc.vector.tensor_tensor(r1, x, table(C_COS), ALU.mult)
                nc.vector.tensor_tensor(r2, swapped, table(C_SIN), ALU.mult).then_inc(rope_read, 1)
                dve.wait_ge(rope_read, done_count)
                return nc.vector.tensor_tensor(x, r1, r2, ALU.add)

            for n in range(QKV2, F2):
                if n - 1 in (QKV2 + 1, QKV2 + 4):
                    u = (n - 1 - QKV2) // 3
                    done(n - 1)
                    nc.vector.tensor_copy(kaT[:, 2 * u:2 * u + 2, :].rearrange("p a t -> p (a t)"),
                                          ps[(n - 1) % 2][:, :]).then_inc(ka_evac, 1)
                heads2(n - 1, 1)
                if n in (BRA + 1, BRA + 2):
                    done(n - 1)
                    for c in range(2):
                        gate_a(sga2, 2 * (n - BRA - 1) + c, up_bank(n - BRA - 1, c)[:, :])
                if n in (BRB + 1, BRB + 2):
                    done(n - 1)
                    dve.wait_ge(upa_evac, 8)
                    for c in range(2):
                        gate_b(sga2, sgb2, 2 * (n - BRB - 1) + c, up_bank(n - BRB - 1, c)[:, :], 1)
                lo(n + 2)
                if n in (BRB + 1, BRB + 2):
                    for c in range(2):
                        merge_lo(sga2, 2 * (n - BRB - 1) + c, 1)
                if n in (QB + 2, QB + 3):
                    u = n - QB - 2
                    rope(qbT[:, 2 * u:2 * u + 2, :].rearrange("p a t -> p (a t)"), ps[7][:, :], rope1, rope2, 2 * T,
                         u + 1).then_inc(qb_ready, 1)
                if n == GA2 + 1:
                    link(rope(kbT[:, :], ps[7][:, 0:T], rope1[:, 0:T], rope2[:, 0:T], T, 3))
                    nc.vector.tensor_copy(vb[:, :, :].rearrange("p t c -> p (t c)"), ps[7][:, T:2 * T])
                    for g in range(GR):
                        for half in range(2):
                            m = nc.vector.tensor_copy(kbd[DH * half:DH * (half + 1), g, :], kbT[DH * g:DH * (g + 1), :])
                    m.then_inc(kb_ready, 1)
                heads2(n, 0)
                if n in (GA2 + 4, GB2 + 4):
                    br = n == GB2 + 4
                    dve.wait_ge(midh_ready, 2 + br)
                    dl, dh = (actl, acth) if br else (midl, midh)
                    for i in range(2):
                        m = nc.vector.tensor_tensor(dl[:, 2 * i:2 * i + 2, :].rearrange("p k t -> p (k t)"), ps[TURN_OUT[br][i]][:, :],
                                                    dh[:, 2 * i:2 * i + 2, :].rearrange("p k t -> p (k t)").bitcast(F32),
                                                    ALU.subtract)
                    m.then_inc(midl_ready, 1)

            residual(4, F2 - 1)
            normalise(4)
            norm_lo(4, V_F2)
            swiglu(F2, F2_F)
            residual(5, END - 1, weighted=True)
            dve.wait_ge(y_ready, 8)
            for b in range(2 * TT):
                tt, cs = half_row(b)
                dve.wait_ge(rstd_ready, TT * 5 + tt + 1)
                nc.vector.tensor_scalar(xs[:, tt, cs], xs[:, tt, cs], rstd[:, tt:tt + 1], None, ALU.mult).then_inc(out_ready, 1)


_INS = ["x", "norm1_w", "w_in", "cmp_pos_k", "cmp_pos_v", "cmp_k_w1", "cmp_k_w2", "cmp_v_w1", "cmp_v_w2", "conv_w",
        "conv_b", "lru_w_a", "lru_b_a", "lru_w_i", "lru_b_i", "lru_lambda", "w_up_attn", "w_up_rnn", "w_out", "norm2_w",
        "mlp_w1", "mlp_w2", "final_norm_w", "ffn1_norm_2", "ffn1_w_gate_2", "ffn1_w_up_2", "ffn1_w_down_2",
        "mix_norm_2", "w_in_2", "sink_logit_2", "w_branch_a_2", "w_branch_b_2", "w_out_2",
        "ffn2_norm_2", "ffn2_w_gate_2", "ffn2_w_up_2", "ffn2_w_down_2", "final_norm_2"]


def kernel(**inputs):
    import concourse.bacc as bacc
    from concourse.bass_utils import run_bass_kernel_spmd

    nc = bacc.Bacc("TRN2", target_bir_lowering=False, num_devices=1)
    arrays = {name: np.ascontiguousarray(inputs[name]) for name in _INS}
    arrays["rpb_rev"] = np.ascontiguousarray(np.asarray(inputs["na_rpb_2"])[..., ::-1])
    arrays["consts"] = constants()
    aps = {name: nc.dram_tensor(f"in_{name}", v.shape, mybir.dt.from_np(v.dtype), kind="ExternalInput").ap()
           for name, v in arrays.items()}
    out = nc.dram_tensor("out", (1, T, D), F32, kind="ExternalOutput").ap()
    build(nc, aps, out)
    r = run_bass_kernel_spmd(nc, [{f"in_{name}": v for name, v in arrays.items()}], core_ids=[0])
    return r.results[0]["out"]
```

```python
from contextlib import ExitStack

import numpy as np
import concourse.bass as bass
from concourse import mybir

F32 = mybir.dt.float32
F32R = mybir.dt.float32r
ALU = mybir.AluOpType
ACT = mybir.ActivationFunctionType
AX_X = mybir.AxisListType.X

P = 128
T = 256
TT = T // P
D = 1024
KT = D // P
DH = 64
NH = 8
GR = 2
NC = 15
CH = 256
NPOS = 16
CW = 4
PW = 2048
R = 3
QSCALE = -(DH ** -0.5)
EPS = 1e-6
ROOT = D ** -0.5
BIG = 1e30
GS = 32

Q, KCVC, KSVS, KWVW, CK, CV, XR, GRP, GA, GB = 0, 2, 3, 4, 5, 7, 9, 13, 17, 21
UPA, UPR, WO, ML = 25, 27, 31, 35
ML_STEPS = 16
F1 = ML + 2 * ML_STEPS
FF_STEPS = 11
QKV2 = F1 + 3 * FF_STEPS
QB, KBVB, GA2, GB2 = QKV2 + 6, QKV2 + 8, QKV2 + 9, QKV2 + 13
BRA, BRB, WO2, F2 = QKV2 + 17, QKV2 + 19, QKV2 + 21, QKV2 + 25
END = F2 + 3 * FF_STEPS

V_N1, V_N2, V_F1, V_MX, V_F2, V_CW, V_CB, V_BA, V_BI, V_LAM, V_PK, V_PV = (
    0, 8, 16, 24, 32, 40, 72, 80, 88, 96, 104, 120)
V_ALL = 136

C_ID, C_MHALF, C_TRIU, C_ZERO, C_CAUS, C_PERM, C_CMP, C_VALID, C_NA, C_COS, C_SIN = (
    0, 128, 130, 258, 386, 514, 642, 674, 676, 740, 996)
C_FIRST = C_TRIU
C_ONES = 1252
C_ALL = C_ONES + P


def constants():
    c = np.zeros((P, C_ALL), np.float32)
    i = np.arange(P)
    c[:, C_ID:C_ID + P] = np.eye(P)
    c[:, C_TRIU:C_TRIU + P] = np.where(i[None, :] >= i[:, None], 0, BIG)
    c[:, C_CAUS:C_CAUS + P] = np.where(i[None, :] <= i[:, None], 0, BIG)
    swap = np.zeros((P, P), np.float32)
    swap[(i // 64) * 64 + (i % 64 + 32) % 64, i] = 1
    c[:, C_PERM:C_PERM + P] = swap
    n = np.arange(NC)
    for tt in range(TT):
        c[:, C_CMP + tt * NC:C_CMP + tt * NC + NC] = np.where(
            n[None, :] * 16 + 31 <= (tt * P + i)[:, None], 0, BIG)
        c[:, C_VALID + tt] = tt * P + i >= 31
    col = i % 64
    start = np.clip(col - 8, 0, 48)
    cc = np.arange(64)
    inside = (cc[None, :] >= start[:, None]) & (cc[None, :] < start[:, None] + 16)
    c[:, C_NA:C_NA + 64] = np.where(inside, 0, BIG)
    c[:, C_MHALF:C_MHALF + 2] = -0.5
    c[:, C_ONES:C_ONES + P] = 1
    half = DH // 2
    inv = np.float32(10000.0) ** (-np.arange(half, dtype=np.float32) / np.float32(half))
    ang = np.arange(T, dtype=np.float32)[None, :] * inv[i % half][:, None].astype(np.float32)
    c[:, C_COS:C_COS + T] = np.cos(ang)
    c[:, C_SIN:C_SIN + T] = np.sin(ang) * np.where(i % 64 < half, -1, 1)[:, None]
    return c


def build(nc, a, out):
    ctx = ExitStack()
    with ctx:
        def sb(name, shape, dt=F32):
            return ctx.enter_context(nc.sbuf_tensor(name, shape, dt))

        def sem(name):
            return ctx.enter_context(nc.semaphore(name))

        raw = sb("raw", [P, R, PW])
        wh = sb("wh", [P, R, PW], F32R)
        wl = sb("wl", [P, R, PW], F32R)
        acth = sb("acth", [P, KT, T], F32R)
        actl = sb("actl", [P, KT, T], F32R)
        midh = sb("midh", [P, 6, T], F32R)
        midl = sb("midl", [P, 6, T], F32R)
        mrgh = sb("mrgh", [P, KT, T], F32R)
        mrgl = sb("mrgl", [P, KT, T], F32R)
        cst = sb("cst", [P, C_ALL])
        xt = sb("xt", [P, TT, D])
        xs = sb("xs", [P, TT, D])
        vec = sb("vec", [P, V_ALL])
        gwr = sb("gwr", [P, KT, 24])
        gwh = sb("gwh", [P, KT, 24], F32R)
        gwl = sb("gwl", [P, KT, 24], F32R)
        cw2 = sb("cw2", [P, 2, 2, DH])
        hid = sb("hid", [P, 2, 2, 2 * NC])
        hidt = sb("hidt", [2 * NC, 2 * CH])
        ssq = sb("ssq", [P, 2 * TT])
        wsq = sb("wsq", [P, 2 * TT])
        part = sb("part", [P, TT])
        var = sb("var", [P, TT])
        rstd = sb("rstd", [P, TT])
        wpart = sb("wpart", [P, TT])
        wvar = sb("wvar", [P, TT])
        wrstd = sb("wrstd", [P, TT])
        late = sb("late", [P, TT])
        small = sb("small", [P, 64])
        lru = sb("lru", [P, 12, KT])
        nmax = sb("nmax", [P, 3, 4])
        sums = sb("sums", [P, 3, 4])
        coef = sb("coef", [P, 3, 4])
        esink = sb("esink", [P, 3, 2])
        nsink = sb("nsink", [P, NH])
        arena = sb("arena", [P, 15616])

        def carve(at, *shape):
            n = int(np.prod(shape))
            v = arena[:, at:at + n]
            names = "abcd"[:len(shape)]
            if len(shape) == 1:
                return v
            return v.rearrange("p (%s) -> p %s" % (" ".join(names), " ".join(names)),
                               **{k: s for k, s in zip(names, shape)})

        xrp = carve(0, KT, T + CW - 1)
        xc = carve(2080, KT, T)
        igx = carve(4128, KT, T)
        gru = carve(6176, KT, T)
        qT = carve(8224, 4, T)
        ksd = carve(9248, GR, T)
        kwd = carve(9760, GR, T)
        vsw = carve(10272, TT, 2, P)
        prob = carve(10784, 768)
        probT = carve(11552, 768)
        vT = carve(10784, 2, T)
        sga = carve(10272, KT, T)
        bd = carve(12320, KT, 2, P)
        sgb = carve(12320, KT, T)
        atok = carve(14368, TT, NH * DH)
        flat = carve(4128, 2, NPOS * 2 * NC)
        abuf = xs[:, :, :].rearrange("p t (k f) -> p (t k) f", f=T)
        gates = sb("gates", [P, TT, NH, 3])
        xsf = xs[:, :, :].rearrange("p t d -> p (t d)")
        vblk = xsf[:, 1024:1536].rearrange("p (g r d) -> p g r d", g=GR, r=4)
        pc = xsf[:, 512:1024].rearrange("p (t h n) -> p t h n", t=TT, h=NH)
        pcT = xsf[:, 1536:2048].rearrange("p (a q) -> p a q", q=P)
        gatT = xs[0:24, 0, 0:T]
        kcd = sb("kcd", [P, GR, NC])
        thr = carve(9760, T)
        nth = carve(9760 + T, T)
        nab = carve(0, TT, NH, T)
        sga2 = carve(4096, KT, T)
        sgb2 = carve(6144, KT, T)
        nabr = carve(4096, TT, NH, T)
        qaT = carve(8192, 4, T)
        kaT = carve(9216, 4, T)
        va = carve(10240, TT, NH * DH)
        qbT = carve(11264, 4, T)
        kbT = carve(12288, T)
        kbd = carve(12544, GR, T)
        vb = carve(13056, TT, P)
        prob2 = carve(13312, TT, T)
        probT2 = carve(13824, 512)
        atok2 = carve(14336, TT, NH * DH)
        btok = xs[:, 0, :].rearrange("p (t n) -> p t n", t=TT)
        vbT = xs[:, 0, 0:T]
        rope1 = xs[:, 1, 0:512]
        rope2 = xs[:, 1, 512:1024]
        fnb = carve(0, D)
        sqx = carve(1024, TT, D)
        sqy = carve(3072, TT, D)
        ffa = xs[:, 0, 0:512]
        ffs = xs[:, 0, 512:1024]
        ffg = xs[:, 1, 0:512]
        diag = carve(8192, TT, P)
        scale_bc = carve(15360, T)

        ps = [ctx.enter_context(nc.psum_tensor(f"ps{i}", [P, 512], F32)) for i in range(2)]
        acc4 = ctx.enter_context(nc.psum_tensor("acc4", [P, 4, 512], F32))
        ps += [acc4[:, i, :] for i in range(4)]
        ps += [ctx.enter_context(nc.psum_tensor(f"ps{i}", [P, 512], F32)) for i in (6, 7)]

        zero = sb("zero", [P, P], F32R)
        ident = cst[:, C_ID:C_ID + P]

        def vcol(v, k=0):
            return vec[:, v + k:v + k + 1]

        x_loaded = [sem(f"x_loaded{tt}") for tt in range(TT)]
        id_loaded = sem("id_loaded")
        cst_loaded = sem("cst_loaded")
        vec_loaded = sem("vec_loaded")
        small_loaded = sem("small_loaded")
        bd_zeroed = sem("bd_zeroed")
        bd_loaded = sem("bd_loaded")
        fnb_loaded = sem("fnb_loaded")
        nab_loaded = sem("nab_loaded")
        nab_ready = sem("nab_ready")
        sink_ready = sem("sink_ready")
        padded = sem("padded")
        zeroed = sem("zeroed")
        panel_loaded = [sem(f"panel_loaded{s}") for s in range(R)]
        half_loaded = sem("half_loaded")
        half_hi = sem("half_hi")
        half_lo = sem("half_lo")
        hi_ready = sem("hi_ready")
        lo_ready = sem("lo_ready")
        panel_done = sem("panel_done")
        dve_chain = sem("dve_chain")
        act_chain = sem("act_chain")
        pool_chain = sem("pool_chain")
        exp_lam = sem("exp_lam")
        abs_lam = sem("abs_lam")
        lru_consts = sem("lru_consts")
        x_summed = sem("x_summed")
        ssq_ready = sem("ssq_ready")
        y_ready = sem("y_ready")
        wsq_ready = sem("wsq_ready")
        rstd_ready = sem("rstd_ready")
        wrstd_ready = sem("wrstd_ready")
        late_ready = sem("late_ready")
        diag_ready = sem("diag_ready")
        bc_done = sem("bc_done")
        bank_done = sem("bank_done")
        stream_ready = sem("stream_ready")
        xs_ready = sem("xs_ready")
        xs_turned = sem("xs_turned")
        acth_ready = sem("acth_ready")
        actl_ready = sem("actl_ready")
        q_evac = sem("q_evac")
        flat_ready = sem("flat_ready")
        flath_ready = sem("flath_ready")
        flatl_ready = sem("flatl_ready")
        ks_evac = sem("ks_evac")
        kw_evac = sem("kw_evac")
        gw_hi = sem("gw_hi")
        gw_lo = sem("gw_lo")
        gates_done = sem("gates_done")
        gates_tanh = sem("gates_tanh")
        gates_ready = sem("gates_ready")
        hidt_ready = sem("hidt_ready")
        hid_turned = sem("hid_turned")
        hid_ready = sem("hid_ready")
        gates_turned = sem("gates_turned")
        v_turned = sem("v_turned")
        v_ready = sem("v_ready")
        ckv_done = sem("ckv_done")
        ckv_ready = sem("ckv_ready")
        sc_done = sem("sc_done")
        sc_read = sem("sc_read")
        sc_shifted = sem("sc_shifted")
        sc_exped = sem("sc_exped")
        pc_ready = sem("pc_ready")
        pc_turned = sem("pc_turned")
        pcT_ready = sem("pcT_ready")
        oc_done = sem("oc_done")
        oc_read = sem("oc_read")
        scored = sem("scored")
        masked = sem("masked")
        exped = sem("exped")
        turned = sem("turned")
        probT_ready = sem("probT_ready")
        mixed = sem("mixed")
        normed = sem("normed")
        atok_turned = sem("atok_turned")
        midh_ready = sem("midh_ready")
        midl_ready = sem("midl_ready")
        xr_evac = sem("xr_evac")
        gr_evac = sem("gr_evac")
        gr_gelu = sem("gr_gelu")
        ga_scaled = sem("ga_scaled")
        gb_scaled = sem("gb_scaled")
        ga_evac = sem("ga_evac")
        gb_evac = sem("gb_evac")
        conv_done = sem("conv_done")
        lru_done = sem("lru_done")
        lru_act = sem("lru_act")
        lru_q = sem("lru_q")
        root_ready = sem("root_ready")
        rnn_ready = sem("rnn_ready")
        rnnh_ready = sem("rnnh_ready")
        rnnl_ready = sem("rnnl_ready")
        upa_evac = sem("upa_evac")
        upr_evac = sem("upr_evac")
        mrg_sum = sem("mrg_sum")
        mrgh_ready = sem("mrgh_ready")
        mrgl_ready = sem("mrgl_ready")
        seeded = sem("seeded")
        ff_gate = sem("ff_gate")
        ff_act = sem("ff_act")
        ff_prod = sem("ff_prod")
        ff_hi = sem("ff_hi")
        ff_lo = sem("ff_lo")
        qa_evac = sem("qa_evac")
        ka_evac = sem("ka_evac")
        va_evac = sem("va_evac")
        qb_evac = sem("qb_evac")
        kv_evac = sem("kv_evac")
        rope_done = sem("rope_done")
        rope_read = sem("rope_read")
        qb_ready = sem("qb_ready")
        kb_ready = sem("kb_ready")
        out_ready = [sem(f"out_ready{tt}") for tt in range(TT)]
        stored = sem("stored")

        def pv(n, kt, dst):
            return dst[:, n % R, :].rearrange("p (k c) -> p k c", k=kt)

        TURNED = (6, 7, 1, 5)

        def half_row(b):
            return b // 2, slice(512 * (b % 2), 512 * (b % 2) + 512)

        w_in, w_in2 = a["w_in"][0], a["w_in_2"][0]

        def up_src(w, col, width=256):
            return w[:, bass.ds(col, width)].rearrange("(k p) c -> p k c", p=P)

        def down_src(w, row):
            return w[bass.ds(row, 256), :].rearrange("(k p) c -> p k c", p=P)

        col1 = {Q: 0, Q + 1: 256, KCVC: 512, KSVS: 768, KWVW: 1024}
        for u in range(4):
            col1[XR + u] = 1304 + 256 * u
            col1[GRP + u] = 2328 + 256 * u
            col1[GA + u] = 3352 + 256 * u
            col1[GB + u] = 4376 + 256 * u
        col2 = {}
        for u in range(2):
            for s in range(3):
                col2[QKV2 + 3 * u + s] = 512 * s + 256 * u
            col2[QB + u] = 1536 + 256 * u
        col2[KBVB] = 2048
        for u in range(4):
            col2[GA2 + u] = 2304 + 256 * u
            col2[GB2 + u] = 3328 + 256 * u

        block = ctx.enter_context(nc.Block())

        @block.sync
        def _(sp):
            for tt in range(TT):
                sp.dma_start(xt[:, tt, :], a["x"][0, tt * P:(tt + 1) * P, :]).then_inc(x_loaded[tt], 16)
            sp.dma_start(cst[:, 0:C_FIRST], a["consts"][:, 0:C_FIRST]).then_inc(id_loaded, 16)
            sp.dma_start(vec[:, :], a["vectors"]).then_inc(vec_loaded, 16)

            def load(n, kt, src):
                if n >= R:
                    sp.wait_ge(lo_ready, n - R + 1)
                sp.dma_start(pv(n, kt, raw), src).then_inc(panel_loaded[n % R], 16)

            def load_in_loop(i, n, kt, src):
                sp.wait_ge(lo_ready, i * 6 + (n - R + 1))
                sp.dma_start(pv(n, kt, raw), src).then_inc(panel_loaded[n % R], 16)

            def load_ffn(n0, wg, wu, wd):
                load(n0, KT, up_src(wg, 0))
                load(n0 + 1, KT, up_src(wu, 0))
                with sp.Fori(0, (FF_STEPS - 1) // 2) as i:
                    for m in range(2):
                        n = n0 + 2 + 3 * m
                        load_in_loop(i, n, KT, up_src(wg, i * 512 + 256 * (m + 1)))
                        load_in_loop(i, n + 1, KT, up_src(wu, i * 512 + 256 * (m + 1)))
                        load_in_loop(i, n + 2, 2, down_src(wd, i * 512 + 256 * m))
                load(n0 + 3 * FF_STEPS - 1, 2, down_src(wd, 256 * (FF_STEPS - 1)))

            for hf, loaded in enumerate((half_loaded, panel_loaded[0])):
                ks = slice(KT // 2 * hf, KT // 2 * (hf + 1))
                sp.dma_start(pv(0, KT, raw)[:, ks, :], up_src(w_in, col1[0])[:, ks, :]).then_inc(loaded, 16)
            for n in range(1, CK):
                load(n, KT, up_src(w_in, col1[n]))
                if n == R - 1:
                    sp.dma_start(cst[:, C_FIRST:], a["consts"][:, C_FIRST:]).then_inc(cst_loaded, 16)
            for n, name in ((CK, "cmp_k_w1"), (CV, "cmp_v_w1")):
                for u in range(2):
                    load(n + u, KT, a[name][0, 1024 * u:1024 * (u + 1), :].rearrange("(k p) c -> p k c", p=P))
            for n in range(XR, UPA):
                load(n, KT, up_src(w_in, col1[n]))
            for u in range(2):
                load(UPA + u, 4, up_src(a["w_up_attn"][0], 512 * u, 512))
            for u in range(4):
                load(UPR + u, KT, up_src(a["w_up_rnn"][0], 256 * u))
            for u in range(4):
                load(WO + u, 2, down_src(a["w_out"][0], 256 * u))
            w1, w2 = a["mlp_w1"][0], a["mlp_w2"][0]
            load(ML, KT, up_src(w1, 0))
            with sp.Fori(0, (ML_STEPS - 1) // 3) as i:
                for m in range(3):
                    n = ML + 1 + 2 * m
                    load_in_loop(i, n, KT, up_src(w1, i * 768 + 256 * (m + 1)))
                    load_in_loop(i, n + 1, 2, down_src(w2, i * 768 + 256 * m))
            load(F1 - 1, 2, down_src(w2, 256 * (ML_STEPS - 1)))
            load_ffn(F1, a["ffn1_w_gate_2"][0], a["ffn1_w_up_2"][0], a["ffn1_w_down_2"][0])
            for n in range(QKV2, BRA):
                load(n, KT, up_src(w_in2, col2[n]))
            for n, name in ((BRA, "w_branch_a_2"), (BRB, "w_branch_b_2")):
                for u in range(2):
                    load(n + u, 4, up_src(a[name][0], 512 * u, 512))
            for u in range(4):
                load(WO2 + u, 2, down_src(a["w_out_2"][0], 256 * u))
            load_ffn(F2, a["ffn2_w_gate_2"][0], a["ffn2_w_up_2"][0], a["ffn2_w_down_2"][0])
            for b in range(2 * TT):
                tt, cs = half_row(b)
                sp.wait_ge(out_ready[tt], b % 2 + 1)
                sp.dma_start(out[0, tt * P:(tt + 1) * P, cs], xs[:, tt, cs]).then_inc(stored, 16)
            sp.wait_ge(stored, 16 * 2 * TT)

        @block.gpsimd
        def _(pool):
            nc.gpsimd.memset(bd[:, :, :, :], 0.0).then_inc(bd_zeroed, 1)
            nc.gpsimd.memset(zero[:, :].bitcast(F32), 0.0).then_inc(zeroed, 1)
            nc.gpsimd.memset(xrp[:, :, 0:CW - 1], 0.0)
            nc.gpsimd.memset(atok[:, :, :], 0.0).then_inc(padded, 1)
            pc_ = [0]

            def link(ins):
                pc_[0] += 1
                ins.then_inc(pool_chain, 1)
                pool.wait_ge(pool_chain, pc_[0])

            def norm_root(r, weighted=False):
                if r == 0:
                    pool.wait_ge(id_loaded, 16)
                for tt in range(TT):
                    t1, first, second = slice(tt, tt + 1), slice(2 * tt, 2 * tt + 1), slice(2 * tt + 1, 2 * tt + 2)
                    mhalf = cst[:, C_MHALF:C_MHALF + 1]
                    pool.wait_ge(ssq_ready, 4 * r + 2 * tt + 1)
                    link(nc.gpsimd.tensor_scalar(part[:, t1], ssq[:, first], EPS, None, ALU.add))
                    pool.wait_ge(ssq_ready, 4 * r + 2 * tt + 2)
                    link(nc.gpsimd.tensor_tensor(var[:, t1], ssq[:, second], part[:, t1], ALU.add))
                    nc.gpsimd.tensor_tensor(rstd[:, t1], var[:, t1], mhalf, ALU.pow).then_inc(rstd_ready, 1)
                    if weighted:
                        pool.wait_ge(wsq_ready, 2 * tt + 2)
                        pool.wait_ge(rstd_ready, TT * r + tt + 1)
                        link(nc.gpsimd.tensor_scalar(wpart[:, t1], wsq[:, second], wsq[:, first], rstd[:, t1], ALU.add, ALU.mult))
                        link(nc.gpsimd.tensor_scalar(wvar[:, t1], wpart[:, t1], rstd[:, t1], EPS, ALU.mult, ALU.add))
                        nc.gpsimd.tensor_tensor(wrstd[:, t1], wvar[:, t1], mhalf, ALU.pow).then_inc(wrstd_ready, 1)
                    if r in (1, 2, 3, 4):
                        pool.wait_ge(rstd_ready, TT * r + tt + 1)
                        if r > 2:
                            m = nc.gpsimd.tensor_scalar(late[:, t1], rstd[:, t1], 1.0, None, ALU.mult)
                        else:
                            if weighted:
                                pool.wait_ge(wrstd_ready, tt + 1)
                            m = nc.gpsimd.tensor_tensor(late[:, t1], rstd[:, t1], (wrstd if weighted else rstd)[:, t1], ALU.mult)
                        m.then_inc(late_ready, 1)

            norm_root(0)
            pool.dma_start(gwr[:, :, :], w_in[:, 1280:1304].rearrange("(k p) c -> p k c", p=P)).then_inc(small_loaded, 16)
            for s, name in enumerate(("cmp_k_w2", "cmp_v_w2")):
                pool.dma_start(cw2[:, s, :, :], a[name][0].rearrange("(c p) d -> p c d", p=P)).then_inc(small_loaded, 16)
            pool.dma_start(nsink[:, :], a["sink_logit_2"][0:1, :].broadcast_to([P, NH])).then_inc(small_loaded, 16)
            pool.wait_ge(bd_zeroed, 1)
            for s, name in enumerate(("lru_w_a", "lru_w_i")):
                pairs = a[name][0].rearrange("(t e) i j -> e i t j", e=2)
                for e in range(2):
                    pool.dma_start(bd[DH * e:DH * (e + 1), :, s, DH * e:DH * (e + 1)], pairs[e]).then_inc(bd_loaded, 16)
            pool.wait_ge(small_loaded, 64)
            nc.gpsimd.tensor_scalar(small[:, 0:NH], nsink[:, :], -1.0, None, ALU.mult).then_inc(sink_ready, 1)

            pool.wait_ge(panel_done, ML)
            norm_root(1)
            pool.dma_start(fnb[:, :], a["final_norm_w"].rearrange("(o d) -> o d", o=1).broadcast_to([P, D])).then_inc(fnb_loaded, 16)
            norm_root(2, weighted=True)
            pool.wait_ge(stream_ready, TT)
            rpb = a["rpb_rev"]
            for tt in range(TT):
                for rr in range(2):
                    for i in range(4):
                        src = bass.AP(rpb.tensor, (7 + i - 2 * tt - rr) * 31 + 15 - 63, [[1, 64], [15 * 31, NH], [1, 64]])
                        pool.dma_start(nabr[64 * rr:64 * rr + 64, tt, :, 64 * i:64 * i + 64], src).then_inc(nab_loaded, 16)
            pool.wait_ge(nab_loaded, 16 * 16)
            pool.wait_ge(cst_loaded, 16)
            for tt in range(TT):
                bias = nabr[:, tt, :, :].rearrange("p h (i c) -> p (h i) c", c=64)[:, :, ::-1]
                mask = cst[:, C_NA:C_NA + 64].unsqueeze(1).broadcast_to([P, 4 * NH, 64])
                nc.gpsimd.tensor_tensor(nab[:, tt, :, :].rearrange("p h (i c) -> p (h i) c", c=64),
                                        mask, bias, ALU.subtract).then_inc(nab_ready, 1)
            norm_root(3)
            norm_root(4)
            pool.wait_ge(panel_done, F2)
            pool.dma_start(fnb[:, :], a["final_norm_2"].rearrange("(o d) -> o d", o=1).broadcast_to([P, D])).then_inc(fnb_loaded, 16)
            norm_root(5)

        flath = mrgh[:, :, :].rearrange("p k t -> p (k t)")[:, 0:2 * NPOS * 2 * NC]
        flatl = mrgl[:, :, :].rearrange("p k t -> p (k t)")[:, 0:2 * NPOS * 2 * NC]
        ML_F, F1_F, F2_F = 0, ML_STEPS, ML_STEPS + FF_STEPS

        def head2(k):
            h = k % NH
            b = DH * (h % 2)
            if k < NH:
                return (qaT[b:b + DH, h // 2, :], kaT[b:b + DH, h // 2, :],
                        [va[:, kt, DH * h:DH * (h + 1)] for kt in range(TT)])
            g = h // 4
            return (qbT[b:b + DH, h // 2, :], kbd[b:b + DH, g, :],
                    [vb[:, kt, DH * g:DH * (g + 1)] for kt in range(TT)])

        def up_bank(u, c):
            return ps[(6, 7, 0, 1)[2 * u + c]]

        TURN_OUT = ((5, 6), (4, 5))

        turn2 = {(QKV2 + 2 + k, 1): k for k in range(7)}
        turn2[QKV2 + 9, 1] = 7
        turn2[QKV2 + 10, 1] = 8
        for k in range(9, 17):
            turn2[QKV2 + 11 + (k - 9) // 2, (k - 9) % 2] = k
        turn2[QKV2 + 15, 1] = 17

        @block.tensor
        def _(pe):
            def split(n):
                pe.wait_ge(lo_ready, n + 1)

            def three(out_, lh, ll, rh, rl, start, stop, **kw):
                nc.tensor.matmul(out_, lh, rh, start=start, stop=False, **kw)
                nc.tensor.matmul(out_, lh, rl, start=False, stop=False, **kw)
                return nc.tensor.matmul(out_, ll, rh, start=False, stop=stop, **kw)

            def feature_tile(n, kt, c, out_, ah, al, norm=None):
                h, l = pv(n, kt, wh), pv(n, kt, wl)
                if norm is not None and c == 0:
                    cs = slice(c * P, (c + 1) * P)
                    for k in range(kt):
                        pe.wait_ge(acth_ready, KT * norm + k + 1)
                        nc.tensor.matmul(out_, h[:, k, cs], ah[:, k, :], start=k == 0, stop=False)
                        nc.tensor.matmul(out_, l[:, k, cs], ah[:, k, :], start=False, stop=False)
                    for k in range(kt):
                        pe.wait_ge(actl_ready, KT * norm + k + 1)
                        last = nc.tensor.matmul(out_, h[:, k, cs], al[:, k, :], start=False, stop=k == kt - 1)
                    return last
                for k in range(kt):
                    last = three(out_, h[:, k, c * P:(c + 1) * P], l[:, k, c * P:(c + 1) * P],
                                 ah[:, k, :], al[:, k, :], k == 0, k == kt - 1)
                return last

            def token_tile(n, c0, c1, tt, out_):
                h, l = pv(n, KT, wh), pv(n, KT, wl)
                s = slice(tt * P, (tt + 1) * P)
                for k in range(KT):
                    last = three(out_, acth[:, k, s], actl[:, k, s], h[:, k, c0:c1], l[:, k, c0:c1],
                                 k == 0, k == KT - 1)
                return last

            def turn_part(j, b, ks):
                tt = b // 2
                src = xt if j in (1, 3, 4) else xs
                if j in (1, 3, 4):
                    pe.wait_ge(x_summed, 4 * (j - 1) + b + 1)
                elif j == 2:
                    pe.wait_ge(y_ready, b + 1)
                else:
                    pe.wait_ge(xs_ready, b + 1)
                for k in ks:
                    m = nc.tensor.transpose(ps[TURNED[k // 2]][:, (k % 2) * T + tt * P:(k % 2) * T + (tt + 1) * P],
                                            src[:, tt, k * P:(k + 1) * P], ident)
                    if tt == TT - 1 and k % 2:
                        m.then_inc(xs_turned, 1)

            def turn_tokens(j):
                for b in range(2 * TT):
                    turn_part(j, b, range(4 * (b % 2), 4 * (b % 2) + 4))

            def turn_rest(j):
                turn_part(j, 2, range(4))
                if j != 3:
                    seed(range(3), j)
                turn_part(j, 1, (4, 5))
                pe.wait_ge(x_summed, 4 * (j - 1) + 4)
                turn_part(j, 1, (6, 7))
                turn_part(j, 3, range(4, 8))

            def down(n, kt, lhs_h, lhs_l, first, final, turn=None):
                h, l = pv(n, 2, wh), pv(n, 2, wl)
                steps = [(k, tt, hf) for k in range(2) for tt in range(TT) for hf in range(2)]
                if final:
                    steps = sorted(steps, key=lambda v: (v[1], v[2], v[0]))
                for k, tt, hf in steps:
                    s = slice(tt * P, (tt + 1) * P)
                    cs = slice(512 * hf, 512 * hf + 512)
                    last = three(acc4[:, 2 * tt + hf, :], lhs_h[:, kt + k, s], lhs_l[:, kt + k, s],
                                 h[:, k, cs], l[:, k, cs], first and k == 0, final and k == 1)
                    if final and k == 1 and 2 * tt + hf < 3:
                        last.then_inc(bank_done, 1)
                        if turn is not None and 2 * tt + hf == 2:
                            turn_part(turn, 0, range(4))
                return last

            def seed(banks, r):
                for b in banks:
                    pe.wait_ge(x_summed, 4 * (r - 1) + b + 1)
                    nc.tensor.matmul(acc4[:, b, :], zero[:, :], mrgh[:, 0:2, :].rearrange("p a t -> p (a t)"),
                                     start=True, stop=False)

            pe.wait_ge(id_loaded, 16)
            turn_tokens(0)

            def head_score(k):
                if k:
                    pe.wait_ge(masked, k)
                b, t, g = DH * (k % 2), k // 2, k // 4
                q = qT[b:b + DH, t, :]
                for e, kd in enumerate((ksd, kwd)):
                    nc.tensor.matmul(ps[2][:, e * P:(e + 1) * P], q[:, 0:P], kd[b:b + DH, g, 0:P], start=True, stop=True)
                for e, kd in enumerate((ksd, kwd)):
                    m = nc.tensor.matmul(ps[3][:, e * T:(e + 1) * T], q[:, P:T], kd[b:b + DH, g, :], start=True, stop=True)
                m.then_inc(scored, 1)

            def head_turn(k):
                pe.wait_ge(exped, k + 1)
                if k:
                    pe.wait_ge(probT_ready, k)
                else:
                    pe.wait_ge(gates_ready, 1)
                for i in range(6):
                    m = nc.tensor.transpose(ps[4 + i // 4][:, (i % 4) * P:(i % 4 + 1) * P], prob[:, i * P:(i + 1) * P], ident)
                m.then_inc(turned, 1)

            def head_mix(k):
                pe.wait_ge(probT_ready, k + 1)
                if k:
                    pe.wait_ge(normed, k)
                else:
                    pe.wait_ge(v_ready, 1)
                vs = slice(DH * (k // 4), DH * (k // 4) + DH)
                for e in range(2):
                    nc.tensor.matmul(ps[6][:, e * DH:(e + 1) * DH], probT[:, e * P:(e + 1) * P], vsw[:, 0, e, vs],
                                     start=True, stop=True)
                    for kt in range(TT):
                        c = (2 + 2 * e + kt) * P
                        m = nc.tensor.matmul(ps[6][:, (2 + e) * DH:(3 + e) * DH], probT[:, c:c + P], vsw[:, kt, e, vs],
                                             start=kt == 0, stop=kt == 1)
                m.then_inc(mixed, 1)

            def heads(k):
                if 0 <= k - 2 < NH:
                    head_mix(k - 2)
                if 0 <= k - 1 < NH:
                    head_turn(k - 1)
                if k < NH:
                    head_score(k)

            def free_bank(n):
                if n in (KCVC, KSVS):
                    pe.wait_ge(q_evac, n - 1)
                elif n == KWVW:
                    pe.wait_ge(flat_ready, 2)
                elif n == XR:
                    pe.wait_ge(ks_evac, 1)
                elif n == XR + 1:
                    pe.wait_ge(kw_evac, 1)
                elif XR + 2 <= n < UPA:
                    group = (n - 2 - XR) // 4
                    pe.wait_ge((xr_evac, gr_evac, ga_evac, gb_evac)[group], (n - 2 - XR) % 4 + 1)

            for n in range(UPA):
                split(n)
                free_bank(n)
                if CK <= n < XR:
                    s, u = (n - CK) // 2, (n - CK) % 2
                    if n == CK:
                        pe.wait_ge(flatl_ready, 1)
                    h, l = pv(n, KT, wh), pv(n, KT, wl)
                    for k in range(KT):
                        at = (s * NPOS + u * KT + k) * 2 * NC
                        m = three(ps[7][0:2 * NC, s * CH:(s + 1) * CH], flath[:, at:at + 2 * NC], flatl[:, at:at + 2 * NC],
                                  h[:, k, :], l[:, k, :], u == 0 and k == 0, u == 1 and k == KT - 1)
                else:
                    for c in range(2):
                        m = feature_tile(n, KT, c, ps[n % 2][:, c * T:(c + 1) * T], acth, actl, 0 if n == 0 else None)
                m.then_inc(panel_done, 1)

                if n == KWVW:
                    pe.wait_ge(gw_lo, 1)
                    for k in range(KT):
                        m = three(ps[5][0:24, 0:T], gwh[:, k, :], gwl[:, k, :], acth[:, k, :], actl[:, k, :],
                                  k == 0, k == KT - 1)
                    m.then_inc(gates_done, 1)
                if n == CK:
                    pe.wait_ge(q_evac, 2)
                    pe.wait_ge(ks_evac, 1)
                    pe.wait_ge(kw_evac, 1)
                    for e in range(2):
                        for tt in range(TT):
                            m = nc.tensor.transpose(ps[6][:, (2 * tt + e) * P:(2 * tt + e + 1) * P],
                                                    vT[:, e, tt * P:(tt + 1) * P], ident)
                    m.then_inc(v_turned, 1)
                    pe.wait_ge(gates_tanh, 1)
                    for tt in range(TT):
                        m = nc.tensor.transpose(ps[5][:, tt * 24:(tt + 1) * 24], gatT[:, tt * P:(tt + 1) * P],
                                                cst[0:24, C_ID:C_ID + 24])
                    m.then_inc(gates_turned, 1)
                if CK <= n < CK + NH + 2:
                    heads(n - CK)
                if n == XR:
                    pe.wait_ge(hidt_ready, 1)
                    for i in range(4):
                        m = nc.tensor.transpose(ps[7][:, i * 2 * NC:(i + 1) * 2 * NC], hidt[:, i * P:(i + 1) * P],
                                                cst[0:2 * NC, C_ID:C_ID + 2 * NC])
                    m.then_inc(hid_turned, 1)
                if n == XR + 1:
                    pe.wait_ge(hid_ready, 1)
                    for c in range(2):
                        nc.tensor.matmul(ps[7][0:DH, 128:128 + 2 * NC], cw2[:, 0, c, :], hid[:, 0, c, :],
                                         start=c == 0, stop=c == 1)
                    for g in range(GR):
                        for c in range(2):
                            m = nc.tensor.matmul(ps[7][0:NC, 192 + DH * g:192 + DH * (g + 1)],
                                                 hid[:, 1, c, NC * g:NC * (g + 1)], cw2[:, 1, c, :],
                                                 start=c == 0, stop=c == 1)
                    m.then_inc(ckv_done, 1)
                if n in (XR + 2, XR + 3):
                    e = n - XR - 2
                    pe.wait_ge(ckv_ready, 1)
                    if e:
                        pe.wait_ge(sc_read, 1)
                    b = DH * e
                    for tt in range(TT):
                        for t in range(4):
                            m = nc.tensor.matmul(ps[7][:, (tt * 4 + t) * NC:(tt * 4 + t + 1) * NC],
                                                 qT[b:b + DH, t, tt * P:(tt + 1) * P], kcd[b:b + DH, t // 2, :],
                                                 start=True, stop=True)
                    m.then_inc(sc_done, 1)
                if n == XR + 5:
                    pe.wait_ge(pc_ready, 1)
                    for i in range(2 * TT):
                        tt, g = i // 2, i % 2
                        m = nc.tensor.transpose(ps[7][:, i * P:(i + 1) * P],
                                                pc[:, tt, 4 * g:4 * g + 4, :].rearrange("p h n -> p (h n)"), ident)
                    m.then_inc(pc_turned, 1)
                if n in (XR + 6, XR + 7):
                    tt = n - XR - 6
                    pe.wait_ge(pcT_ready, 1)
                    if tt:
                        pe.wait_ge(oc_read, 1)
                    for g in range(GR):
                        m = nc.tensor.matmul(ps[7][:, g * T:(g + 1) * T], pcT[:, tt * 2 + g, :],
                                             vblk[:, g, :, :].rearrange("p r d -> p (r d)"), start=True, stop=True)
                    m.then_inc(oc_done, 1)
                if XR + 4 <= n < XR + 4 + KT:
                    t = n - XR - 4
                    pe.wait_ge(conv_done, t + 1)
                    if t == 0:
                        pe.wait_ge(bd_loaded, 64)
                        pe.wait_ge(masked, NH)
                    if t >= 2:
                        pe.wait_ge(lru_act, t - 1)
                    for s in range(2):
                        m = nc.tensor.matmul(ps[2 + t % 2][:, s * T:(s + 1) * T], bd[:, t, s, :], xc[:, t, :],
                                             start=True, stop=True)
                    m.then_inc(lru_done, 1)
                if n == GA + 1:
                    pe.wait_ge(normed, NH)
                    pe.wait_ge(oc_read, 2)
                    for k in range(4):
                        for tt in range(TT):
                            m = nc.tensor.transpose(ps[4 + k // 2][:, (k % 2) * T + tt * P:(k % 2) * T + (tt + 1) * P],
                                                    atok[:, tt, k * P:(k + 1) * P], ident)
                    m.then_inc(atok_turned, 1)

            pe.wait_ge(midl_ready, 1)
            for u in range(2):
                split(UPA + u)
                if u:
                    pe.wait_ge(gb_evac, 4)
                for c in range(4):
                    m = feature_tile(UPA + u, 4, c, up_bank(u, c // 2)[:, (c % 2) * T:(c % 2 + 1) * T], midh, midl)
                m.then_inc(panel_done, 1)
            pe.wait_ge(rnnl_ready, 2)
            for u in range(4):
                n = UPR + u
                split(n)
                pe.wait_ge(upa_evac, u + 1)
                for c in range(2):
                    m = feature_tile(n, KT, c, up_bank(u // 2, u % 2)[:, c * T:(c + 1) * T], acth, actl)
                m.then_inc(panel_done, 1)

            def project(n0, e):
                for u in range(4):
                    split(n0 + u)
                    pe.wait_ge(mrgl_ready, 4 * e + u + 1)
                    down(n0 + u, 2 * u, mrgh, mrgl, u == 0, u == 3,
                         (1, 4)[e] if u == 3 else None).then_inc(panel_done, 1)

            project(WO, 0)
            pe.wait_ge(zeroed, 1)
            turn_rest(1)

            def ffn_up(n, b, norm=None):
                h = [feature_tile(n, KT, c, ps[b][:, c * T:(c + 1) * T], acth, actl, norm) for c in range(2)]
                h[1].then_inc(panel_done, 1)

            split(ML)
            ffn_up(ML, 0, 1)
            seed([3], 1)
            with pe.Fori(0, (ML_STEPS - 1) // 3) as i:
                for m in range(3):
                    n = ML + 1 + 2 * m
                    pe.wait_ge(lo_ready, i * 6 + (n + 1))
                    pe.wait_ge(ff_act, i * 3 + (ML_F + m + 1))
                    ffn_up(n, 0)
                    pe.wait_ge(lo_ready, i * 6 + (n + 2))
                    pe.wait_ge(ff_lo, i * 3 + (ML_F + m + 1))
                    down(n + 1, 2 * m, midh, midl, False, False).then_inc(panel_done, 1)
            split(F1 - 1)
            pe.wait_ge(ff_lo, ML_F + ML_STEPS)
            down(F1 - 1, 2 * ((ML_STEPS - 1) % 3), midh, midl, False, True, 2).then_inc(panel_done, 1)

            def spread(j):
                pe.wait_ge(diag_ready, j - 1)
                for tt in range(TT):
                    m = nc.tensor.matmul(ps[TURNED[0]][:, tt * P:(tt + 1) * P], cst[:, C_ONES:C_ONES + P], diag[:, tt, :],
                                         start=True, stop=True)
                m.then_inc(bc_done, 1)

            def swiglu(n0, f0, j):
                turn_rest(j)
                split(n0)
                ffn_up(n0, 0, j)
                seed([3], j)
                spread(j)
                split(n0 + 1)
                ffn_up(n0 + 1, 1)
                with pe.Fori(0, (FF_STEPS - 1) // 2) as i:
                    for m in range(2):
                        n = n0 + 2 + 3 * m
                        for b, (read, r0) in enumerate(((ff_gate, f0 - F1_F), (ff_prod, f0))):
                            pe.wait_ge(lo_ready, i * 6 + (n + b + 1))
                            pe.wait_ge(read, i * 2 + (r0 + m + 1))
                            ffn_up(n + b, b)
                        pe.wait_ge(lo_ready, i * 6 + (n + 3))
                        pe.wait_ge(ff_lo, i * 2 + (f0 + m + 1))
                        down(n + 2, 2 * m, midh, midl, False, False).then_inc(panel_done, 1)
                n = n0 + 3 * FF_STEPS - 1
                split(n)
                pe.wait_ge(ff_lo, f0 + FF_STEPS)
                down(n, 2 * ((FF_STEPS - 1) % 2), midh, midl, False, True,
                     3 if n0 == F1 else None).then_inc(panel_done, 1)

            swiglu(F1, F1_F, 2)
            turn_rest(3)

            def score2(k):
                if k == 0:
                    pe.wait_ge(qa_evac, 1)
                    pe.wait_ge(ka_evac, 1)
                else:
                    pe.wait_ge(masked, NH + k)
                if k == 4:
                    pe.wait_ge(qa_evac, 2)
                    pe.wait_ge(ka_evac, 2)
                if k == NH:
                    pe.wait_ge(qb_ready, 2)
                    pe.wait_ge(kb_ready, 1)
                q, kk, _ = head2(k)
                for tt in range(TT):
                    m = nc.tensor.matmul(ps[2][:, tt * T:(tt + 1) * T], q[:, tt * P:(tt + 1) * P], kk, start=True, stop=True)
                m.then_inc(scored, 1)

            def turn2_(k):
                pe.wait_ge(exped, NH + k + 1)
                pe.wait_ge(probT_ready, NH + k)
                for i in range(4):
                    tt, kt = i // 2, i % 2
                    m = nc.tensor.transpose(ps[3][:, i * P:(i + 1) * P], prob2[:, tt, kt * P:(kt + 1) * P], ident)
                m.then_inc(turned, 1)

            def mix2(k):
                pe.wait_ge(probT_ready, NH + k + 1)
                pe.wait_ge(normed, NH + k)
                if k == 0:
                    pe.wait_ge(va_evac, 1)
                if k == 4:
                    pe.wait_ge(va_evac, 2)
                vt = head2(k)[2]
                for tt in range(TT):
                    for kt in range(TT):
                        c = (2 * tt + kt) * P
                        m = nc.tensor.matmul(ps[4][:, tt * DH:(tt + 1) * DH], probT2[:, c:c + P], vt[kt],
                                             start=kt == 0, stop=kt == 1)
                m.then_inc(mixed, 1)

            def heads2(n, part):
                k = turn2.get((n, part))
                if k is None:
                    return
                if 0 <= k - 2:
                    mix2(k - 2)
                if 0 <= k - 1 < 2 * NH:
                    turn2_(k - 1)
                if k < 2 * NH:
                    score2(k)

            def free_bank2(n):
                last = {QKV2 + 2: (qa_evac, 1), QKV2 + 3: (ka_evac, 1), QKV2 + 4: (va_evac, 1),
                        QKV2 + 5: (qa_evac, 2), QB: (ka_evac, 2), QB + 1: (va_evac, 2),
                        KBVB: (qb_evac, 1), GA2: (qb_evac, 2), GA2 + 1: (kv_evac, 1)}
                if n in last:
                    pe.wait_ge(*last[n])
                elif n >= GA2 + 2:
                    u = n - GA2 - 2
                    pe.wait_ge((ga_scaled, gb_scaled)[u // 4], u % 4 + 1)

            def turn_out(tok, br):
                for k in range(4):
                    for tt in range(TT):
                        m = nc.tensor.transpose(ps[TURN_OUT[br][k // 2]][:, (k % 2) * T + tt * P:(k % 2) * T + (tt + 1) * P],
                                                tok[:, tt, k * P:(k + 1) * P], ident)
                m.then_inc(atok_turned, 1)

            for n in range(QKV2, BRA):
                split(n)
                free_bank2(n)
                o = ps[n % 2]
                for c in range(2):
                    if n in (QKV2 + 2, QKV2 + 5):
                        m = token_tile(n, 0, 256, c, o[:, c * T:(c + 1) * T])
                    else:
                        m = feature_tile(n, KT, c, o[:, c * T:(c + 1) * T], acth, actl, 3 if n == QKV2 else None)
                    if c == 1:
                        m.then_inc(panel_done, 1)
                    heads2(n, c)
                if n == QKV2:
                    spread(3)
                if n in (QB + 1, KBVB):
                    u = n - QB - 1
                    pe.wait_ge(qb_evac, u + 1)
                    if u:
                        pe.wait_ge(rope_read, 1)
                    nc.tensor.matmul(ps[7][:, :], cst[:, C_PERM:C_PERM + P],
                                     qbT[:, 2 * u:2 * u + 2, :].rearrange("p a t -> p (a t)"),
                                     start=True, stop=True).then_inc(rope_done, 1)
                if n == GA2:
                    pe.wait_ge(kv_evac, 1)
                    pe.wait_ge(rope_read, 2)
                    for tt in range(TT):
                        nc.tensor.transpose(ps[7][:, T + tt * P:T + (tt + 1) * P], vbT[:, tt * P:(tt + 1) * P], ident)
                    nc.tensor.matmul(ps[7][:, 0:T], cst[:, C_PERM:C_PERM + P], kbT[:, :],
                                     start=True, stop=True).then_inc(rope_done, 1)
                if n == GA2 + 3:
                    pe.wait_ge(normed, 2 * NH)
                    turn_out(atok2, 0)
                if n == GB2 + 3:
                    pe.wait_ge(normed, 3 * NH)
                    pe.wait_ge(midl_ready, 2)
                    turn_out(btok, 1)

            for br, (n0, ah, al) in enumerate(((BRA, midh, midl), (BRB, acth, actl))):
                pe.wait_ge(midl_ready, 2 + br)
                for u in range(2):
                    split(n0 + u)
                    for c in range(4):
                        if br == 0 and u == 1 and c == 0:
                            pe.wait_ge(gb_scaled, 4)
                        if br and c % 2 == 0:
                            pe.wait_ge(upa_evac, 4 + 2 * u + c // 2 + 1)
                        m = feature_tile(n0 + u, 4, c, up_bank(u, c // 2)[:, (c % 2) * T:(c % 2 + 1) * T], ah, al)
                    m.then_inc(panel_done, 1)
            project(WO2, 1)
            swiglu(F2, F2_F, 4)

        @block.scalar
        def _(act):
            ac = [0]

            def link(ins):
                ac[0] += 1
                ins.then_inc(act_chain, 1)
                act.wait_ge(act_chain, ac[0])

            def hi(n):
                act.wait_ge(panel_loaded[n % R], 16 * (n // R + 1))
                if n >= R:
                    act.wait_ge(panel_done, n - R + 1)
                nc.scalar.activation(wh[:, n % R, :], raw[:, n % R, :], ACT.Copy).then_inc(hi_ready, 1)

            def hi_in_loop(i, n):
                if n < END:
                    act.wait_ge(panel_loaded[n % R], i * 32 + 16 * (n // R + 1))
                    act.wait_ge(panel_done, i * 6 + (n - R + 1))
                    nc.scalar.activation(wh[:, n % R, :], raw[:, n % R, :], ACT.Copy).then_inc(hi_ready, 1)

            def square_sum(r, weighted=False, apart=False, result=False, halves=range(2 * TT)):
                for b in halves:
                    tt, cs = half_row(b)
                    if result and b == 3:
                        act.wait_ge(rstd_ready, TT * r + 1)
                        act.wait_ge(y_ready, 4 + 2)
                        for c in (0, 1):
                            _, c0 = half_row(c)
                            nc.scalar.activation(xs[:, 0, c0], xs[:, 0, c0], ACT.Copy,
                                                 scale=rstd[:, 0:1]).then_inc(out_ready[0], 1)
                    if r:
                        act.wait_ge(x_summed, 4 * (r - 1) + b + 1)
                    else:
                        act.wait_ge(x_loaded[tt], 16)
                    junk = sqx if apart else xs
                    nc.scalar.activation(junk[:, tt, cs], xt[:, tt, cs], ACT.Square, scale=ROOT, accum_out=ssq[:, b:b + 1]).then_inc(ssq_ready, 1)
                    if weighted:
                        act.wait_ge(y_ready, b + 1)
                        nc.scalar.activation(sqy[:, tt, cs], xs[:, tt, cs], ACT.Square, scale=ROOT,
                                             accum_out=wsq[:, b:b + 1]).then_inc(wsq_ready, 1)

            def norm_hi(j, v):
                if j == 0:
                    act.wait_ge(vec_loaded, 16)
                for k in range(KT):
                    act.wait_ge(xs_turned, 4 * j + k // 2 + 1)
                    nc.scalar.activation(acth[:, k, :], ps[TURNED[k // 2]][:, (k % 2) * T:(k % 2 + 1) * T],
                                         ACT.Copy, scale=vcol(v, k)).then_inc(acth_ready, 1)

            def squares_and_hi(j, v, **kw):
                square_sum(j, halves=range(3), **kw)
                norm_hi(j, v)
                square_sum(j, halves=(3,), **kw)

            square_sum(0)
            for hf, (loaded, ready) in enumerate(((half_loaded, half_hi), (panel_loaded[0], hi_ready))):
                act.wait_ge(loaded, 16)
                cs = slice(PW // 2 * hf, PW // 2 * (hf + 1))
                nc.scalar.activation(wh[:, 0, cs], raw[:, 0, cs], ACT.Copy).then_inc(ready, 1)
            norm_hi(0, V_N1)
            hi(1)
            act.wait_ge(abs_lam, 1)
            nc.scalar.activation(lru[:, 1, :], lru[:, 0, :], ACT.Exp, scale=-1.0).then_inc(exp_lam, 1)

            def done(n):
                act.wait_ge(panel_done, n + 1)

            def keys_values(b, kd, e, ev):
                for g in range(GR):
                    for half in range(2):
                        nc.scalar.activation(kd[DH * half:DH * (half + 1), g, :], b[DH * g:DH * (g + 1), 0:T], ACT.Copy)
                nc.scalar.activation(vT[:, e, :], b[:, T:2 * T], ACT.Copy).then_inc(ev, 1)

            def head_exp(k):
                act.wait_ge(masked, k + 1)
                o = k % 3
                for i, (c0, c1) in enumerate(((0, P), (P, 2 * P), (2 * P, 4 * P), (4 * P, 6 * P))):
                    m = nc.scalar.activation(prob[:, c0:c1], prob[:, c0:c1], ACT.Exp, scale=-1.0,
                                             bias=nmax[:, o, i:i + 1], accum_out=sums[:, o, i:i + 1])
                m.then_inc(exped, 1)

            def head_copy(k):
                act.wait_ge(turned, k + 1)
                if k:
                    act.wait_ge(mixed, k)
                nc.scalar.activation(probT[:, :], acc4[:, 2:4, :].rearrange("p b c -> p (b c)")[:, 0:768],
                                     ACT.Copy).then_inc(probT_ready, 1)

            for n in range(ML):
                if UPR < n <= UPR + 4:
                    u = n - UPR - 1
                    act.wait_ge(mrg_sum, u + 1)
                    nc.scalar.activation(mrgh[:, 2 * u:2 * u + 2, :], sga[:, 2 * u:2 * u + 2, :], ACT.Copy,
                                         scale=0.5).then_inc(mrgh_ready, 1)
                if n in (Q + 1, Q + 2):
                    u = n - Q - 1
                    done(n - 1)
                    nc.scalar.activation(qT[:, 2 * u:2 * u + 2, :].rearrange("p a t -> p (a t)"), ps[u][:, :], ACT.Copy,
                                         scale=QSCALE).then_inc(q_evac, 1)
                hi(n + 2)
                k = n - CK - 1
                if 0 <= k - 1 < NH:
                    head_copy(k - 1)
                if 0 <= k < NH:
                    head_exp(k)
                if n == Q + 2:
                    act.wait_ge(small_loaded, 64)
                    nc.scalar.activation(gwh[:, :, :], gwr[:, :, :], ACT.Copy).then_inc(gw_hi, 1)
                if n == KCVC + 1:
                    act.wait_ge(flat_ready, 2)
                    nc.scalar.activation(flath, flat[:, :, :].rearrange("p s c -> p (s c)"), ACT.Copy).then_inc(flath_ready, 1)
                if n == KSVS + 1:
                    done(KSVS)
                    keys_values(ps[KSVS % 2], ksd, 0, ks_evac)
                if n == KWVW + 1:
                    done(KWVW)
                    keys_values(ps[KWVW % 2], kwd, 1, kw_evac)
                    act.wait_ge(gates_done, 1)
                    nc.scalar.activation(gatT[:, :], ps[5][0:24, 0:T], ACT.Tanh, scale=0.5).then_inc(gates_tanh, 1)
                if n == CK + 1:
                    act.wait_ge(v_turned, 1)
                    nc.scalar.activation(vsw[:, :, :, :].rearrange("p t e c -> p (t e c)"), ps[6][:, :],
                                         ACT.Copy).then_inc(v_ready, 1)
                if n == XR:
                    done(XR - 1)
                    nc.scalar.activation(hidt[:, :], ps[7][0:2 * NC, :], ACT.Gelu_apprx_tanh).then_inc(hidt_ready, 1)
                if XR < n <= XR + 4:
                    u = n - XR - 1
                    done(n - 1)
                    nc.scalar.activation(xrp[:, 2 * u:2 * u + 2, CW - 1:CW - 1 + T],
                                         ps[(n - 1) % 2][:, :].rearrange("p (a t) -> p a t", a=2), ACT.Copy).then_inc(xr_evac, 1)
                if n == XR + 5:
                    act.wait_ge(sc_shifted, 1)
                    nc.scalar.activation(pc[:, :, :, 0:NC], pc[:, :, :, 0:NC], ACT.Exp, scale=-1.0).then_inc(sc_exped, 1)
                if n == XR + 6:
                    act.wait_ge(pc_turned, 1)
                    nc.scalar.activation(pcT[:, :, :].rearrange("p a q -> p (a q)"), ps[7][:, :], ACT.Copy).then_inc(pcT_ready, 1)
                if GRP < n <= GRP + 4:
                    u = n - GRP - 1
                    done(n - 1)
                    nc.scalar.activation(gru[:, 2 * u:2 * u + 2, :].rearrange("p a t -> p (a t)"), ps[(n - 1) % 2][:, :],
                                         ACT.Copy).then_inc(gr_evac, 1)
                for g0, sg, ev in ((GA, sga, ga_evac), (GB, sgb, gb_evac)):
                    if g0 < n <= g0 + 4:
                        u = n - g0 - 1
                        done(n - 1)
                        if g0 == GB and u == 0:
                            act.wait_ge(lru_done, KT)
                        nc.scalar.activation(sg[:, 2 * u:2 * u + 2, :].rearrange("p a t -> p (a t)"), ps[(n - 1) % 2][:, :],
                                             ACT.Tanh, scale=0.5).then_inc(ev, 1)
                if n == GRP + 5:
                    act.wait_ge(gr_evac, 4)
                    nc.scalar.activation(gru[:, :, :], gru[:, :, :], ACT.Gelu_apprx_tanh).then_inc(gr_gelu, 1)
                t = n - XR - 5
                if 0 <= t < KT:
                    if t == 0:
                        act.wait_ge(lru_consts, 1)
                    act.wait_ge(lru_done, t + 1)
                    b = ps[2 + t % 2]
                    nc.scalar.activation(igx[:, t, :], b[:, T:2 * T], ACT.Tanh, scale=0.5, bias=lru[:, 9, t:t + 1])
                    if t:
                        act.wait_ge(lru_act, t)
                    link(nc.scalar.activation(thr[:, :], b[:, 0:T], ACT.Tanh, scale=0.5, bias=lru[:, 8, t:t + 1]))
                    nc.scalar.activation(abuf[:, t, :], thr[:, :], ACT.Exp, scale=lru[:, 6, t:t + 1], bias=lru[:, 6, t:t + 1])
                    if t:
                        act.wait_ge(lru_q, t)
                    nc.scalar.activation(nth[:, :], thr[:, :], ACT.Tanh, scale=lru[:, 7, t:t + 1],
                                         bias=lru[:, 7, t:t + 1]).then_inc(lru_act, 1)
                if n in (GA + 1, GB + 1):
                    hf = (n - GA - 1) // 4
                    act.wait_ge(lru_q, 4 * hf + 4)
                    q2 = xrp[:, 4 * hf:4 * hf + 4, 0:T]
                    nc.scalar.activation(q2, q2, ACT.Sqrt).then_inc(root_ready, 1)
                if n == GA + 2:
                    act.wait_ge(atok_turned, 1)
                    nc.scalar.activation(midh[:, 0:4, :].rearrange("p k t -> p (k t)"),
                                         acc4[:, 2:4, :].rearrange("p b c -> p (b c)"), ACT.Copy).then_inc(midh_ready, 1)
                if n == UPA:
                    done(UPA - 1)
                    for hf in range(2):
                        act.wait_ge(rnn_ready, hf + 1)
                        nc.scalar.activation(acth[:, 4 * hf:4 * hf + 4, :], gru[:, 4 * hf:4 * hf + 4, :],
                                             ACT.Copy).then_inc(rnnh_ready, 1)

            squares_and_hi(1, V_N2)

            def hidden_hi(s):
                return nc.scalar.activation(midh[:, 2 * s:2 * s + 2, :].rearrange("p a t -> p (a t)"), ffs, ACT.Copy)

            hi(ML + 2)
            done(ML)
            nc.scalar.activation(ffa, ps[0][:, :], ACT.Relu).then_inc(ff_act, 1)
            hi(ML + 3)
            act.wait_ge(ff_prod, ML_F + 1)
            hidden_hi(0).then_inc(ff_hi, 1)
            with act.Fori(0, (ML_STEPS - 1) // 3) as i:
                for m in range(3):
                    n = ML + 1 + 2 * m
                    act.wait_ge(panel_done, i * 6 + (n + 1))
                    nc.scalar.activation(ffa, ps[0][:, :], ACT.Relu).then_inc(ff_act, 1)
                    hi_in_loop(i, n + 3)
                    act.wait_ge(ff_prod, i * 3 + (ML_F + m + 2))
                    hidden_hi((m + 1) % 3).then_inc(ff_hi, 1)
                    hi_in_loop(i, n + 4)

            def swiglu(n0, f0):
                hi(n0 + 2)
                hi(n0 + 3)
                act.wait_ge(ff_gate, f0 - F1_F + 1)
                nc.scalar.activation(ffa, ffg, ACT.Silu).then_inc(ff_act, 1)
                hi(n0 + 4)
                act.wait_ge(ff_prod, f0 + 1)
                hidden_hi(0).then_inc(ff_hi, 1)

                def two_steps(i, last):
                    for m in range(2):
                        n = n0 + 2 + 3 * m
                        hi_in_loop(i, n + 3)
                        act.wait_ge(ff_gate, i * 2 + (f0 - F1_F + m + 2))
                        nc.scalar.activation(ffa, ffg, ACT.Silu).then_inc(ff_act, 1)
                        act.wait_ge(ff_prod, i * 2 + (f0 + m + 2))
                        hidden_hi((m + 1) % 2).then_inc(ff_hi, 1)
                        if not (last and m and n0 == F2):
                            hi_in_loop(i, n + 4)
                            hi_in_loop(i, n + 5)

                with act.Fori(0, (FF_STEPS - 1) // 2 - 1) as i:
                    two_steps(i, False)
                two_steps((FF_STEPS - 1) // 2 - 1, True)

            squares_and_hi(2, V_F1, weighted=True, apart=True)
            swiglu(F1, F1_F)
            squares_and_hi(3, V_MX)

            def copy2(k):
                act.wait_ge(turned, NH + k + 1)
                act.wait_ge(mixed, NH + k)
                nc.scalar.activation(probT2[:, :], ps[3][:, :], ACT.Copy).then_inc(probT_ready, 1)

            def exp2(k):
                act.wait_ge(masked, NH + k + 1)
                o = k % 3
                if k >= NH:
                    h = k - NH
                    for tt in range(TT):
                        nc.scalar.activation(esink[:, o, tt:tt + 1], small[:, h:h + 1], ACT.Exp, scale=-1.0,
                                             bias=nmax[:, o, tt:tt + 1])
                for tt in range(TT):
                    m = nc.scalar.activation(prob2[:, tt, :], prob2[:, tt, :], ACT.Exp, scale=-1.0,
                                             bias=nmax[:, o, tt:tt + 1], accum_out=sums[:, o, tt:tt + 1])
                m.then_inc(exped, 1)

            def heads2(n, part):
                k = turn2.get((n, part))
                if k is None:
                    return
                if 0 <= k - 1 < 2 * NH:
                    copy2(k - 1)
                if k < 2 * NH:
                    exp2(k)

            for n in range(QKV2, F2):
                hi(n + 2)
                b = ps[(n - 1) % 2][:, :]
                if n - 1 in (QKV2 + 2, QKV2 + 5):
                    u = (n - 1 - QKV2) // 3
                    done(n - 1)
                    act.wait_ge(rstd_ready, TT * 4)
                    for tt in range(TT):
                        m = nc.scalar.activation(va[:, tt, 256 * u:256 * (u + 1)], b[:, tt * 256:(tt + 1) * 256], ACT.Copy,
                                                 scale=rstd[:, tt:tt + 1])
                    m.then_inc(va_evac, 1)
                heads2(n - 1, 1)
                heads2(n, 0)
                for g0, sg, scaled, ev in ((GA2, sga2, ga_scaled, ga_evac), (GB2, sgb2, gb_scaled, gb_evac)):
                    if g0 < n <= g0 + 4:
                        u = n - g0 - 1
                        act.wait_ge(scaled, u + 1)
                        gate = sg[:, 2 * u:2 * u + 2, :]
                        nc.scalar.activation(gate, gate, ACT.Tanh, scale=0.5).then_inc(ev, 1)
                if n in (GA2 + 4, GB2 + 4):
                    br = n == GB2 + 4
                    act.wait_ge(atok_turned, 2 + br)
                    if br:
                        done(BRA - 1)
                    dst = acth if br else midh
                    for i in range(2):
                        m = nc.scalar.activation(dst[:, 2 * i:2 * i + 2, :].rearrange("p k t -> p (k t)"),
                                                 ps[TURN_OUT[br][i]][:, :], ACT.Copy)
                    m.then_inc(midh_ready, 1)
                if n in (BRB + 1, BRB + 2):
                    for u in range(2 * (n - BRB - 1), 2 * (n - BRB)):
                        act.wait_ge(mrg_sum, 4 + u + 1)
                        nc.scalar.activation(mrgh[:, 2 * u:2 * u + 2, :], sga2[:, 2 * u:2 * u + 2, :], ACT.Copy,
                                             scale=0.5).then_inc(mrgh_ready, 1)

            squares_and_hi(4, V_F2)
            swiglu(F2, F2_F)
            square_sum(5, apart=True, result=True)

        @block.vector
        def _(dve):
            dc = [0]

            def link(ins):
                dc[0] += 1
                ins.then_inc(dve_chain, 1)
                dve.wait_ge(dve_chain, dc[0])

            def lo(n):
                dve.wait_ge(hi_ready, n + 1)
                nc.vector.tensor_tensor(wl[:, n % R, :], raw[:, n % R, :], wh[:, n % R, :].bitcast(F32),
                                        ALU.subtract).then_inc(lo_ready, 1)

            def lo_in_loop(i, n):
                dve.wait_ge(hi_ready, i * 6 + (n + 1))
                nc.vector.tensor_tensor(wl[:, n % R, :], raw[:, n % R, :], wh[:, n % R, :].bitcast(F32),
                                        ALU.subtract).then_inc(lo_ready, 1)

            def normalise():
                for b in range(2 * TT):
                    tt, cs = half_row(b)
                    if b % 2 == 0:
                        dve.wait_ge(rstd_ready, tt + 1)
                    nc.vector.tensor_scalar(xs[:, tt, cs], xt[:, tt, cs], rstd[:, tt:tt + 1], None, ALU.mult).then_inc(xs_ready, 1)

            bc2 = scale_bc.unsqueeze(1).broadcast_to([P, 2, T])

            def two(v):
                return v.rearrange("p (a t) -> p a t", t=T)

            def diagonals(j):
                dve.wait_ge(late_ready, TT * j)
                for tt in range(TT):
                    m = nc.vector.tensor_scalar(diag[:, tt, :], ident, late[:, tt:tt + 1], None, ALU.mult)
                m.then_inc(diag_ready, 1)

            def take_scales(j):
                dve.wait_ge(bc_done, j - 1)
                link(nc.vector.tensor_copy(scale_bc, ps[TURNED[0]][:, 0:T]))

            def norm_lo(j, v):
                for k in range(KT):
                    dve.wait_ge(acth_ready, KT * j + k // 2 * 2 + 2)
                    nc.vector.scalar_tensor_tensor(actl[:, k, :], ps[TURNED[k // 2]][:, (k % 2) * T:(k % 2 + 1) * T],
                                                   vcol(v, k), acth[:, k, :].bitcast(F32), ALU.mult,
                                                   ALU.subtract).then_inc(actl_ready, 1)

            def done(n):
                dve.wait_ge(panel_done, n + 1)

            normalise()
            dve.wait_ge(vec_loaded, 16)
            lam = vec[:, V_LAM:V_LAM + KT]
            nc.vector.scalar_tensor_tensor(lru[:, 0, :], lam, -1.0, lam, ALU.mult, ALU.max).then_inc(abs_lam, 1)
            for hf, (ready, split) in enumerate(((half_hi, half_lo), (hi_ready, lo_ready))):
                dve.wait_ge(ready, 1)
                cs = slice(PW // 2 * hf, PW // 2 * (hf + 1))
                nc.vector.tensor_tensor(wl[:, 0, cs], raw[:, 0, cs], wh[:, 0, cs].bitcast(F32), ALU.subtract).then_inc(split, 1)
            norm_lo(0, V_N1)
            lo(1)

            def lru_constants():
                dve.wait_ge(exp_lam, 1)
                e, den, s, s2, p = (lru[:, i, :] for i in (1, 2, 3, 4, 5))
                link(nc.vector.tensor_scalar(den, e, 2.0, None, ALU.add))
                link(nc.vector.reciprocal(den, den))
                link(nc.vector.tensor_tensor(s, e, den, ALU.mult))
                link(nc.vector.tensor_tensor(s2, s, s, ALU.mult))
                link(nc.vector.tensor_scalar(p, s2, 1.0 / 15, None, ALU.mult))
                for q in (13, 11, 9, 7, 5, 3):
                    link(nc.vector.scalar_tensor_tensor(p, p, 1.0 / q, s2, ALU.add, ALU.mult))
                link(nc.vector.scalar_tensor_tensor(p, p, 1.0, s, ALU.add, ALU.mult))
                link(nc.vector.tensor_scalar(lru[:, 10, :], lam, -1.0, 0.0, ALU.mult, ALU.max))
                link(nc.vector.scalar_tensor_tensor(lru[:, 11, :], p, 2.0, lru[:, 10, :], ALU.mult, ALU.add))
                nc.vector.tensor_scalar(lru[:, 6, :], lru[:, 11, :], -0.5 * 8.0, None, ALU.mult)
                nc.vector.tensor_scalar(lru[:, 7, :], lru[:, 11, :], 0.5 * 8.0, None, ALU.mult)
                nc.vector.tensor_scalar(lru[:, 8, :], vec[:, V_BA:V_BA + KT], 0.5, None, ALU.mult)
                nc.vector.tensor_scalar(lru[:, 9, :], vec[:, V_BI:V_BI + KT], 0.5, None, ALU.mult).then_inc(lru_consts, 1)

            def masked_min(out_, scores, mask, o, i, start=3e38):
                return nc.vector.tensor_tensor_reduce(out=out_, in0=scores, in1=mask, scale=1.0, scalar=start,
                                                      op0=ALU.add, op1=ALU.min, accum_out=nmax[:, o, i:i + 1])

            def head_mask(k):
                dve.wait_ge(scored, k + 1)
                if k:
                    dve.wait_ge(turned, k)
                o = k % 3
                for e in range(2):
                    masked_min(prob[:, e * P:(e + 1) * P], ps[2][:, e * P:(e + 1) * P], cst[:, C_CAUS:C_CAUS + P], o, e)
                for e in range(2):
                    m = masked_min(prob[:, (1 + e) * T:(2 + e) * T], ps[3][:, e * T:(e + 1) * T],
                                   cst[:, C_ZERO:C_ZERO + T], o, 2 + e)
                m.then_inc(masked, 1)

            def head_norm(k):
                dve.wait_ge(mixed, k + 1)
                o = k % 3
                link(nc.vector.reciprocal(coef[:, o, :], sums[:, o, :]))
                c4 = coef[:, o, :].rearrange("p (t e) -> p t e", e=2)
                link(nc.vector.tensor_tensor(c4, c4, gates[:, :, k, 1:3], ALU.mult))
                for e in range(2):
                    for tt in range(TT):
                        i = 2 * tt + e
                        at = atok[:, tt, DH * k:DH * (k + 1)]
                        m = nc.vector.scalar_tensor_tensor(at, ps[6][:, i * DH:(i + 1) * DH], coef[:, o, i:i + 1], at,
                                                           ALU.mult, ALU.add)
                        if e == 0:
                            link(m)
                m.then_inc(normed, 1)
                dve.wait_ge(normed, k + 1)

            def conv(t):
                dve.wait_ge(xr_evac, t // 2 + 1)
                link(nc.vector.tensor_scalar(xc[:, t, :], xrp[:, t, 0:T], vcol(V_CW, t), vcol(V_CB, t), ALU.mult, ALU.add))
                for i in range(1, CW):
                    m = nc.vector.scalar_tensor_tensor(xc[:, t, :], xrp[:, t, i:i + T], vcol(V_CW + KT * i, t), xc[:, t, :],
                                                       ALU.mult, ALU.add)
                    if i < CW - 1:
                        link(m)
                m.then_inc(conv_done, 1)

            def recur(hf):
                t0 = 4 * hf
                ts = slice(t0, t0 + 4)
                dve.wait_ge(root_ready, hf + 1)
                dve.wait_ge(gr_gelu, 1)
                link(nc.vector.scalar_tensor_tensor(igx[:, ts, :], igx[:, ts, :], 1.0, xc[:, ts, :], ALU.add, ALU.mult))
                link(nc.vector.tensor_tensor(igx[:, ts, :], xrp[:, ts, 0:T], igx[:, ts, :], ALU.mult))
                for t in range(t0, t0 + 4):
                    m = nc.vector.tensor_tensor_scan(xc[:, t, :], abuf[:, t, :], igx[:, t, :], 0.0, ALU.mult, ALU.add)
                link(m)
                nc.vector.scalar_tensor_tensor(gru[:, ts, :], xc[:, ts, :], 0.5, gru[:, ts, :], ALU.mult,
                                               ALU.mult).then_inc(rnn_ready, 1)

            def gate_a(sg, u, bank):
                s = sg[:, 2 * u:2 * u + 2, :].rearrange("p a t -> p (a t)")
                nc.vector.scalar_tensor_tensor(s, s, 1.0, bank, ALU.add, ALU.mult).then_inc(upa_evac, 1)

            def gate_b(sa, sg, u, bank, e):
                dst = sa[:, 2 * u:2 * u + 2, :].rearrange("p a t -> p (a t)")
                s = sg[:, 2 * u:2 * u + 2, :].rearrange("p a t -> p (a t)")
                nc.vector.scalar_tensor_tensor(s, s, 1.0, bank, ALU.add, ALU.mult).then_inc(upr_evac, 1)
                dve.wait_ge(upr_evac, 4 * e + u + 1)
                nc.vector.tensor_tensor(dst, dst, s, ALU.add).then_inc(mrg_sum, 1)

            def merge_lo(sa, u, e):
                dst = sa[:, 2 * u:2 * u + 2, :]
                dve.wait_ge(mrgh_ready, 4 * e + u + 1)
                nc.vector.scalar_tensor_tensor(mrgl[:, 2 * u:2 * u + 2, :], dst, 0.5, mrgh[:, 2 * u:2 * u + 2, :].bitcast(F32),
                                               ALU.mult, ALU.subtract).then_inc(mrgl_ready, 1)

            dve.wait_ge(cst_loaded, 16)
            for n in range(ML):
                if n == KCVC + 1:
                    done(KCVC)
                    for s in range(2):
                        for l in range(2):
                            for g in range(GR):
                                first = ps[KCVC % 2][DH * g:DH * (g + 1), s * T + l:s * T + l + 1]
                                win = bass.AP(first.tensor, first.offset, [first.ap[0], [2, NPOS], [16, NC]])
                                dst = flat[DH * l:DH * (l + 1), s, :].rearrange("p (j g n) -> p j g n", g=GR, n=NC)[:, :, g, :]
                                pos = vec[DH * l:DH * (l + 1), V_PK + NPOS * s:V_PK + NPOS * (s + 1)]
                                m = nc.vector.tensor_tensor(dst, win, pos.unsqueeze(2).broadcast_to([DH, NPOS, NC]), ALU.add)
                        m.then_inc(flat_ready, 1)
                k = n - CK - 1
                if 0 <= k < NH:
                    head_mask(k)
                if 0 <= k - 2 < NH:
                    head_norm(k - 2)
                if n in (UPA + 1, UPA + 2):
                    done(n - 1)
                    for c in range(2):
                        gate_a(sga, 2 * (n - UPA - 1) + c, up_bank(n - UPA - 1, c)[:, :])
                if UPR < n <= UPR + 4:
                    u = n - UPR - 1
                    done(n - 1)
                    if u == 0:
                        dve.wait_ge(upa_evac, 4)
                    gate_b(sga, sgb, u, up_bank(u // 2, u % 2)[:, :], 0)
                    merge_lo(sga, u, 0)
                if n < ML - 1:
                    lo(n + 2)
                if n == KSVS:
                    lru_constants()
                if n == Q + 2:
                    dve.wait_ge(gw_hi, 1)
                    nc.vector.tensor_tensor(gwl[:, :, :], gwr[:, :, :], gwh[:, :, :].bitcast(F32), ALU.subtract).then_inc(gw_lo, 1)
                if n == KCVC + 1:
                    dve.wait_ge(flath_ready, 1)
                    nc.vector.tensor_tensor(flatl, flat[:, :, :].rearrange("p s c -> p (s c)"), flath.bitcast(F32),
                                            ALU.subtract).then_inc(flatl_ready, 1)
                if n == KWVW:
                    link(nc.vector.memset(pc[:, :, :, :], 0.0))
                    link(nc.vector.memset(vblk[:, :, :, :], 0.0))
                if n == CK + 1:
                    dve.wait_ge(gates_turned, 1)
                    nc.vector.tensor_scalar(gates[:, :, :, :].rearrange("p t h b -> p (t h b)"), ps[5][:, 0:48], 0.5, 0.5,
                                            ALU.mult, ALU.add).then_inc(gates_ready, 1)
                    dve.wait_ge(gates_ready, 1)
                    dve.wait_ge(padded, 1)
                if n == XR + 1:
                    dve.wait_ge(hid_turned, 1)
                    nc.vector.tensor_copy(hid[:, :, :, :].rearrange("p s c n -> p (s c n)"),
                                          ps[7][:, 0:8 * NC]).then_inc(hid_ready, 1)
                if n == XR + 2:
                    dve.wait_ge(ckv_done, 1)
                    for half in range(2):
                        nc.vector.tensor_copy(kcd[DH * half:DH * (half + 1), :, :].rearrange("p g n -> p (g n)"),
                                              ps[7][0:DH, 128:128 + 2 * NC])
                    for r in range(4):
                        m = nc.vector.tensor_copy(vblk[GS * r:GS * r + NC, :, r, :],
                                                  ps[7][0:NC, 192:192 + 2 * DH].rearrange("p (g d) -> p g d", g=GR))
                    m.then_inc(ckv_ready, 1)
                if n in (XR + 3, XR + 4):
                    e = n - XR - 3
                    dve.wait_ge(sc_done, e + 1)
                    cm = cst[:, C_CMP:C_CMP + TT * NC].rearrange("p (t n) -> p t n", n=NC)
                    nc.vector.tensor_tensor(pc[:, :, e::2, 0:NC], ps[7][:, 0:8 * NC].rearrange("p (t h n) -> p t h n", t=TT, h=4),
                                            cm.unsqueeze(2).broadcast_to([P, TT, 4, NC]), ALU.add).then_inc(sc_read, 1)
                pcv = pc[:, :, :, :].rearrange("p t h n -> p (t h) n")[:, :, 0:NC]

                def over_n(v):
                    return v.unsqueeze(2).broadcast_to([P, TT * NH, NC])

                if n == XR + 4:
                    dve.wait_ge(sc_read, 2)
                    link(nc.vector.tensor_reduce(small[:, 8:24], pcv, AX_X, ALU.min))
                    nc.vector.tensor_tensor(pcv, pcv, over_n(small[:, 8:24]), ALU.subtract).then_inc(sc_shifted, 1)
                if n == XR + 5:
                    dve.wait_ge(sc_exped, 1)
                    c16 = small[:, 40:56]
                    cth = c16.rearrange("p (t h) -> p t h", t=TT)
                    link(nc.vector.tensor_reduce(small[:, 24:40], pcv, AX_X, ALU.add))
                    link(nc.vector.reciprocal(c16, small[:, 24:40]))
                    link(nc.vector.tensor_tensor(cth, cth, gates[:, :, :, 0], ALU.mult))
                    link(nc.vector.tensor_tensor(cth, cth, cst[:, C_VALID:C_VALID + TT].unsqueeze(2).broadcast_to([P, TT, NH]),
                                                 ALU.mult))
                    nc.vector.tensor_tensor(pcv, pcv, over_n(c16), ALU.mult).then_inc(pc_ready, 1)
                if n in (XR + 7, XR + 8):
                    tt = n - XR - 7
                    dve.wait_ge(oc_done, tt + 1)
                    nc.vector.tensor_tensor(atok[:, tt, :], atok[:, tt, :], ps[7][:, :], ALU.add).then_inc(oc_read, 1)
                    dve.wait_ge(oc_read, tt + 1)
                t = n - XR - 3
                if 0 <= t < KT:
                    conv(t)
                t = n - XR - 5
                if 0 <= t < KT:
                    dve.wait_ge(lru_act, t + 1)
                    q2 = xrp[:, t, 0:T]
                    link(nc.vector.tensor_tensor(q2, abuf[:, t, :], abuf[:, t, :], ALU.mult))
                    nc.vector.scalar_tensor_tensor(q2, q2, 1.0, nth[:, :], ALU.add, ALU.mult).then_inc(lru_q, 1)
                if n == GA + 2:
                    dve.wait_ge(midh_ready, 1)
                    nc.vector.tensor_tensor(midl[:, 0:4, :].rearrange("p k t -> p (k t)"),
                                            acc4[:, 2:4, :].rearrange("p b c -> p (b c)"),
                                            midh[:, 0:4, :].rearrange("p k t -> p (k t)").bitcast(F32),
                                            ALU.subtract).then_inc(midl_ready, 1)
                if n in (GA + 2, GB + 2):
                    recur((n - GA - 2) // 4)
                if n == UPA:
                    for hf in range(2):
                        ts = slice(4 * hf, 4 * hf + 4)
                        dve.wait_ge(rnnh_ready, hf + 1)
                        nc.vector.tensor_tensor(actl[:, ts, :], gru[:, ts, :], acth[:, ts, :].bitcast(F32),
                                                ALU.subtract).then_inc(rnnl_ready, 1)

            yc = [0]

            def residual(r, last, weighted=False, scaled=None):
                if scaled:
                    dve.wait_ge(late_ready, TT * scaled)
                for b in range(2 * TT):
                    tt, cs = half_row(b)
                    if b < 3:
                        dve.wait_ge(bank_done, 3 * (r - 1) + b + 1)
                    else:
                        done(last)
                    if scaled:
                        m = nc.vector.scalar_tensor_tensor(xt[:, tt, cs], acc4[:, b, :], late[:, tt:tt + 1], xt[:, tt, cs],
                                                           ALU.mult, ALU.add)
                    else:
                        m = nc.vector.tensor_tensor(xt[:, tt, cs], xt[:, tt, cs], acc4[:, b, :], ALU.add)
                    m.then_inc(x_summed, 1)
                    if weighted:
                        if b == 0:
                            yc[0] += 1
                            dve.wait_ge(fnb_loaded, 16 * yc[0])
                        dve.wait_ge(x_summed, 4 * (r - 1) + b + 1)
                        nc.vector.tensor_tensor(xs[:, tt, cs], xt[:, tt, cs], fnb[:, cs], ALU.mult).then_inc(y_ready, 1)

            def hidden_lo(s):
                return nc.vector.tensor_tensor(midl[:, 2 * s:2 * s + 2, :].rearrange("p a t -> p (a t)"), ffs,
                                               midh[:, 2 * s:2 * s + 2, :].rearrange("p a t -> p (a t)").bitcast(F32), ALU.subtract)

            residual(1, ML - 1)
            norm_lo(1, V_N2)
            lo(ML + 1)
            lo(ML + 2)
            dve.wait_ge(ff_act, ML_F + 1)
            nc.vector.tensor_tensor(ffs, ffa, ffa, ALU.mult).then_inc(ff_prod, 1)
            dve.wait_ge(ff_hi, ML_F + 1)
            hidden_lo(0).then_inc(ff_lo, 1)
            with dve.Fori(0, (ML_STEPS - 1) // 3) as i:
                for m in range(3):
                    n = ML + 1 + 2 * m
                    lo_in_loop(i, n + 2)
                    dve.wait_ge(ff_act, i * 3 + (ML_F + m + 2))
                    dve.wait_ge(ff_lo, i * 3 + (ML_F + m + 1))
                    nc.vector.tensor_tensor(ffs, ffa, ffa, ALU.mult).then_inc(ff_prod, 1)
                    lo_in_loop(i, n + 3)
                    dve.wait_ge(ff_hi, i * 3 + (ML_F + m + 2))
                    hidden_lo((m + 1) % 3).then_inc(ff_lo, 1)

            def swiglu(n0, f0, meanwhile=None):
                def product(at_panel, at_act, at_lo):
                    dve.wait_ge(panel_done, at_panel)
                    dve.wait_ge(ff_act, at_act)
                    dve.wait_ge(ff_lo, at_lo)
                    nc.vector.scalar_tensor_tensor(ffs, ps[1][:, :], 0.5, ffa, ALU.mult, ALU.mult).then_inc(ff_prod, 1)

                def gate(at_panel):
                    dve.wait_ge(panel_done, at_panel)
                    nc.vector.tensor_tensor(two(ffg), two(ps[0][:, :]), bc2, ALU.mult).then_inc(ff_gate, 1)

                j = 2 if n0 == F1 else 4
                lo(n0 + 1)
                diagonals(j)
                lo(n0 + 2)
                take_scales(j)
                gate(n0 + 1)
                if meanwhile:
                    meanwhile()
                lo(n0 + 3)
                product(n0 + 2, f0 + 1, f0)
                dve.wait_ge(ff_hi, f0 + 1)
                hidden_lo(0).then_inc(ff_lo, 1)

                def two_steps(i, last):
                    for m in range(2):
                        n = n0 + 2 + 3 * m
                        lo_in_loop(i, n + 2)
                        gate(i * 6 + (n + 1))
                        lo_in_loop(i, n + 3)
                        product(i * 6 + (n + 2), i * 2 + (f0 + m + 2), i * 2 + (f0 + m + 1))
                        dve.wait_ge(ff_hi, i * 2 + (f0 + m + 2))
                        hidden_lo((m + 1) % 2).then_inc(ff_lo, 1)
                        if not (last and m and n0 == F2):
                            lo_in_loop(i, n + 4)

                with dve.Fori(0, (FF_STEPS - 1) // 2 - 1) as i:
                    two_steps(i, False)
                two_steps((FF_STEPS - 1) // 2 - 1, True)

            residual(2, F1 - 1, weighted=True, scaled=1)
            norm_lo(2, V_F1)

            def next_stream():
                for tt in range(TT):
                    nc.vector.scalar_tensor_tensor(xt[:, tt, :], xt[:, tt, :], rstd[:, tt:tt + 1], fnb[:, :], ALU.mult,
                                                   ALU.mult).then_inc(stream_ready, 1)

            swiglu(F1, F1_F, next_stream)
            residual(3, QKV2 - 1, scaled=2)
            norm_lo(3, V_MX)
            lo(QKV2 + 1)
            diagonals(3)

            def mask2(k):
                dve.wait_ge(scored, NH + k + 1)
                dve.wait_ge(turned, NH + k)
                o = k % 3
                if k == 0:
                    dve.wait_ge(nab_ready, 2)
                if k == NH:
                    dve.wait_ge(sink_ready, 1)
                for tt in range(TT):
                    if k < NH:
                        m = masked_min(prob2[:, tt, :], ps[2][:, tt * T:(tt + 1) * T], nab[:, tt, k, :], o, tt)
                    else:
                        c = (C_ZERO, C_TRIU)[tt]
                        m = masked_min(prob2[:, tt, :], ps[2][:, tt * T:(tt + 1) * T], cst[:, c:c + T], o, tt,
                                       small[:, k - NH:k - NH + 1])
                m.then_inc(masked, 1)

            def norm2(k):
                dve.wait_ge(mixed, NH + k + 1)
                o = k % 3
                h = k % NH
                c = coef[:, o, 0:TT]
                if k < NH:
                    link(nc.vector.reciprocal(c, sums[:, o, 0:TT]))
                else:
                    link(nc.vector.tensor_tensor(c, sums[:, o, 0:TT], esink[:, o, :], ALU.add))
                    link(nc.vector.reciprocal(c, c))
                tok = atok2 if k < NH else btok
                for tt in range(TT):
                    m = nc.vector.tensor_scalar(tok[:, tt, DH * h:DH * (h + 1)], ps[4][:, tt * DH:(tt + 1) * DH],
                                                coef[:, o, tt:tt + 1], None, ALU.mult)
                m.then_inc(normed, 1)

            def heads2(n, part):
                k = turn2.get((n, part))
                if k is None:
                    return
                if k < 2 * NH:
                    mask2(k)
                if 0 <= k - 2:
                    norm2(k - 2)

            def rope(x, swapped, r1, r2, width, done_count):
                dve.wait_ge(rope_done, done_count)
                reps = width // T

                def table(c):
                    return cst[:, c:c + T].unsqueeze(1).broadcast_to([P, reps, T])

                r1, r2, x, swapped = (v.rearrange("p (a t) -> p a t", t=T) for v in (r1, r2, x, swapped))
                nc.vector.tensor_tensor(r1, x, table(C_COS), ALU.mult)
                nc.vector.tensor_tensor(r2, swapped, table(C_SIN), ALU.mult).then_inc(rope_read, 1)
                dve.wait_ge(rope_read, done_count)
                return nc.vector.tensor_tensor(x, r1, r2, ALU.add)

            for n in range(QKV2, F2):
                bank = two(ps[(n - 1) % 2][:, :])
                if n == QKV2 + 1:
                    take_scales(3)
                if n - 1 in (QKV2, QKV2 + 3, QB, QB + 1):
                    done(n - 1)
                    dst, ev, u = ((qaT, qa_evac, (n - 1 - QKV2) // 3) if n - 1 < QB else (qbT, qb_evac, n - 1 - QB))
                    nc.vector.scalar_tensor_tensor(dst[:, 2 * u:2 * u + 2, :], bank, QSCALE, bc2, ALU.mult,
                                                   ALU.mult).then_inc(ev, 1)
                if n - 1 in (QKV2 + 1, QKV2 + 4):
                    u = (n - 1 - QKV2) // 3
                    done(n - 1)
                    nc.vector.tensor_tensor(kaT[:, 2 * u:2 * u + 2, :], bank, bc2, ALU.mult).then_inc(ka_evac, 1)
                if n - 1 == KBVB:
                    done(n - 1)
                    nc.vector.tensor_tensor(kbT[:, :], bank[:, 0, :], scale_bc, ALU.mult)
                    nc.vector.tensor_tensor(vbT[:, :], bank[:, 1, :], scale_bc, ALU.mult).then_inc(kv_evac, 1)
                for g0, sg, scaled in ((GA2, sga2, ga_scaled), (GB2, sgb2, gb_scaled)):
                    if g0 < n <= g0 + 4:
                        u = n - g0 - 1
                        done(n - 1)
                        if g0 == GA2 and u == 0:
                            dve.wait_ge(nab_ready, 2)
                        nc.vector.tensor_tensor(sg[:, 2 * u:2 * u + 2, :], bank, bc2, ALU.mult).then_inc(scaled, 1)
                heads2(n - 1, 1)
                if n in (BRA + 1, BRA + 2):
                    done(n - 1)
                    dve.wait_ge(ga_evac, 8)
                    dve.wait_ge(gb_evac, 8)
                    for c in range(2):
                        gate_a(sga2, 2 * (n - BRA - 1) + c, up_bank(n - BRA - 1, c)[:, :])
                if n in (BRB + 1, BRB + 2):
                    done(n - 1)
                    dve.wait_ge(upa_evac, 8)
                    for c in range(2):
                        gate_b(sga2, sgb2, 2 * (n - BRB - 1) + c, up_bank(n - BRB - 1, c)[:, :], 1)
                if n < F2 - 1:
                    lo(n + 2)
                if n in (BRB + 1, BRB + 2):
                    for c in range(2):
                        merge_lo(sga2, 2 * (n - BRB - 1) + c, 1)
                if n in (QB + 2, QB + 3):
                    u = n - QB - 2
                    rope(qbT[:, 2 * u:2 * u + 2, :].rearrange("p a t -> p (a t)"), ps[7][:, :], rope1, rope2, 2 * T,
                         u + 1).then_inc(qb_ready, 1)
                if n == GA2 + 1:
                    link(rope(kbT[:, :], ps[7][:, 0:T], rope1[:, 0:T], rope2[:, 0:T], T, 3))
                    nc.vector.tensor_copy(vb[:, :, :].rearrange("p t c -> p (t c)"), ps[7][:, T:2 * T])
                    for g in range(GR):
                        for half in range(2):
                            m = nc.vector.tensor_copy(kbd[DH * half:DH * (half + 1), g, :], kbT[DH * g:DH * (g + 1), :])
                    m.then_inc(kb_ready, 1)
                heads2(n, 0)
                if n in (GA2 + 4, GB2 + 4):
                    br = n == GB2 + 4
                    dve.wait_ge(midh_ready, 2 + br)
                    dl, dh = (actl, acth) if br else (midl, midh)
                    for i in range(2):
                        m = nc.vector.tensor_tensor(dl[:, 2 * i:2 * i + 2, :].rearrange("p k t -> p (k t)"), ps[TURN_OUT[br][i]][:, :],
                                                    dh[:, 2 * i:2 * i + 2, :].rearrange("p k t -> p (k t)").bitcast(F32),
                                                    ALU.subtract)
                    m.then_inc(midl_ready, 1)

            residual(4, F2 - 1)
            norm_lo(4, V_F2)
            swiglu(F2, F2_F)
            residual(5, END - 1, weighted=True, scaled=4)
            dve.wait_ge(y_ready, 8)
            dve.wait_ge(rstd_ready, TT * 5 + 2)
            for b in (2, 3):
                tt, cs = half_row(b)
                nc.vector.tensor_scalar(xs[:, tt, cs], xs[:, tt, cs], rstd[:, tt:tt + 1], None, ALU.mult).then_inc(out_ready[tt], 1)


_INS = ["x", "w_in", "cmp_k_w1", "cmp_k_w2", "cmp_v_w1", "cmp_v_w2", "lru_w_a", "lru_w_i", "w_up_attn", "w_up_rnn",
        "w_out", "mlp_w1", "mlp_w2", "final_norm_w", "ffn1_w_gate_2", "ffn1_w_up_2", "ffn1_w_down_2", "w_in_2",
        "sink_logit_2", "w_branch_a_2", "w_branch_b_2", "w_out_2", "ffn2_w_gate_2", "ffn2_w_up_2", "ffn2_w_down_2",
        "final_norm_2"]
_VECTORS = ["norm1_w", "norm2_w", "ffn1_norm_2", "mix_norm_2", "ffn2_norm_2", "conv_w", "conv_b", "lru_b_a", "lru_b_i",
            "lru_lambda", "cmp_pos_k", "cmp_pos_v"]


def kernel(**inputs):
    import concourse.bacc as bacc
    from concourse.bass_utils import run_bass_kernel_spmd

    nc = bacc.Bacc("TRN2", target_bir_lowering=False, num_devices=1)
    arrays = {name: np.ascontiguousarray(inputs[name]) for name in _INS}
    arrays["vectors"] = np.ascontiguousarray(np.concatenate(
        [np.asarray(inputs[name]).reshape(-1, P) for name in _VECTORS], axis=0).T)
    arrays["rpb_rev"] = np.ascontiguousarray(np.asarray(inputs["na_rpb_2"])[..., ::-1])
    arrays["consts"] = constants()
    aps = {name: nc.dram_tensor(f"in_{name}", v.shape, mybir.dt.from_np(v.dtype), kind="ExternalInput").ap()
           for name, v in arrays.items()}
    out = nc.dram_tensor("out", (1, T, D), F32, kind="ExternalOutput").ap()
    build(nc, aps, out)
    r = run_bass_kernel_spmd(nc, [{f"in_{name}": v for name, v in arrays.items()}], core_ids=[0])
    return r.results[0]["out"]
```
